# Optimizing a Trainium2 kernel written in Bass

```python
import jax, jax.numpy as jnp
from jax import lax
import numpy as np

D_MODEL = 1024
BATCH = 1
SEQ = 256
DEPTH = 1
DEC_BATCH = 8
DEC_SEQ = 1
PAST_LEN = 1024
PAGE_SIZE = 128

HEAD_DIM = 64
D_ATTN = D_MODEL // 2
N_HEADS = D_ATTN // HEAD_DIM
N_KV_HEADS = N_HEADS // 4
GROUP = N_HEADS // N_KV_HEADS
WINDOW = 128
ATTN_BLOCK = 128
ROT_DIM = HEAD_DIM // 4
ROPE_THETA = 500000.0
D_RNN = D_MODEL - D_ATTN
N_RNN_BLOCKS = 8
RNN_BLOCK_W = D_RNN // N_RNN_BLOCKS
CONV_WIDTH = 4
LRU_C = 8.0
D_MIX = D_ATTN + D_RNN
KV_W = N_KV_HEADS * HEAD_DIM
D_IN = D_ATTN + 2 * KV_W + 2 * D_RNN
N_EXPERTS = 32
TOP_K = 4
D_FF_EXPERT = D_MODEL
SWIGLU_LIMIT = 7.0
SWIGLU_ALPHA = 1.702
MOE_BLOCK = 128
EPS = 1e-6

kernel_name = "hymba_swa_sink_rglru_moe_step"

def rmsnorm(x, g):
    xf = x.astype(jnp.float32)
    y = xf * lax.rsqrt(jnp.mean(xf * xf, axis=-1, keepdims=True) + EPS)
    return (y * g.astype(jnp.float32)).astype(x.dtype)

def partial_rope(x, pos):
    inv = ROPE_THETA ** (-jnp.arange(0, ROT_DIM, 2, dtype=jnp.float32) / ROT_DIM)
    ang = pos.astype(jnp.float32)[:, None] * inv[None, :]
    cos = jnp.cos(ang)[None, :, None, :]
    sin = jnp.sin(ang)[None, :, None, :]
    xr = x[..., :ROT_DIM].astype(jnp.float32)
    x1, x2 = xr[..., :ROT_DIM // 2], xr[..., ROT_DIM // 2:]
    rot = jnp.concatenate([x1 * cos - x2 * sin, x2 * cos + x1 * sin], axis=-1)
    return jnp.concatenate([rot.astype(x.dtype), x[..., ROT_DIM:]], axis=-1)

def window_attention(q, k_ext, v_ext, sinks, pos0):
    B, S = q.shape[0], q.shape[1]
    qb = ATTN_BLOCK if S % ATTN_BLOCK == 0 else S
    nb = S // qb
    kspan = qb + WINDOW
    qr = q.reshape(B, nb, qb, N_KV_HEADS, GROUP, HEAD_DIM)
    kidx = jnp.arange(nb)[:, None] * qb + jnp.arange(kspan)[None, :]
    kb = k_ext[:, kidx]
    vb = v_ext[:, kidx]
    s = jnp.einsum('bnqkgd,bnskd->bnkgqs', qr, kb).astype(jnp.float32) * (HEAD_DIM ** -0.5)
    rel = jnp.arange(qb)[:, None] + WINDOW - jnp.arange(kspan)[None, :]
    band = (rel >= 0) & (rel <= WINDOW)
    valid = (pos0 - WINDOW + kidx) >= 0
    mask = band[None, :, :] & valid[:, None, :]
    s = jnp.where(mask[None, :, None, None, :, :], s, -jnp.inf)
    sink = jnp.broadcast_to(sinks.astype(jnp.float32).reshape(N_KV_HEADS, GROUP)[None, None, :, :, None, None],
                            s.shape[:-1] + (1,))
    p = jax.nn.softmax(jnp.concatenate([s, sink], axis=-1), axis=-1)[..., :-1]
    o = jnp.einsum('bnkgqs,bnskd->bnqkgd', p.astype(vb.dtype), vb)
    return o.reshape(B, S, N_HEADS * HEAD_DIM)

def causal_conv(ext, w, b):
    out = lax.conv_general_dilated(ext, w[:, None, :], window_strides=(1,), padding='VALID',
                                   dimension_numbers=('NWC', 'WIO', 'NWC'),
                                   feature_group_count=ext.shape[-1])
    return out + b

def _lin_combine(e1, e2):
    a1, b1 = e1
    a2, b2 = e2
    return a1 * a2, a2 * b1 + b2

def rglru(xc, h0, w_a, b_a, w_x, b_x, lam):
    B, S, C = xc.shape
    xb = xc.reshape(B, S, N_RNN_BLOCKS, RNN_BLOCK_W)
    r = jax.nn.sigmoid(jnp.einsum('bsni,nio->bsno', xb, w_a).reshape(B, S, C).astype(jnp.float32)
                       + b_a.reshape(C).astype(jnp.float32))
    i = jax.nn.sigmoid(jnp.einsum('bsni,nio->bsno', xb, w_x).reshape(B, S, C).astype(jnp.float32)
                       + b_x.reshape(C).astype(jnp.float32))
    log_a = -LRU_C * r * jax.nn.softplus(-lam.astype(jnp.float32))
    a = jnp.exp(log_a)
    u = jnp.sqrt(-jnp.expm1(2.0 * log_a)) * (i * xc.astype(jnp.float32))
    u = u.at[:, 0].add(a[:, 0] * h0.astype(jnp.float32))
    _, h = lax.associative_scan(_lin_combine, (a, u), axis=1)
    return h.astype(xc.dtype), h[:, -1].astype(xc.dtype)

def moe(x2d, w_router, b_router, w_gu, b_gu, w_dn, b_dn):
    T, D = x2d.shape
    logits = jnp.einsum('td,de->te', x2d, w_router).astype(jnp.float32) + b_router.astype(jnp.float32)
    top_vals, top_idx = lax.top_k(logits, TOP_K)
    gates = jax.nn.softmax(top_vals, axis=-1).astype(x2d.dtype)
    n_slots = T * TOP_K
    flat_e = top_idx.reshape(-1).astype(jnp.int32)
    flat_t = (jnp.arange(n_slots, dtype=jnp.int32) // TOP_K)
    flat_g = gates.reshape(-1)
    order = jnp.argsort(flat_e)
    sorted_e = flat_e[order]
    counts = jnp.bincount(flat_e, length=N_EXPERTS).astype(jnp.int32)
    padded = (counts + MOE_BLOCK - 1) // MOE_BLOCK * MOE_BLOCK
    pad_end = jnp.cumsum(padded)
    pad_start = pad_end - padded
    start = jnp.cumsum(counts) - counts
    dest = pad_start[sorted_e] + (jnp.arange(n_slots, dtype=jnp.int32) - start[sorted_e])
    n_blocks = -(-n_slots // MOE_BLOCK) + N_EXPERTS
    n_rows = n_blocks * MOE_BLOCK
    slot_tok = jnp.full((n_rows,), T, jnp.int32).at[dest].set(flat_t[order])
    slot_gate = jnp.zeros((n_rows,), x2d.dtype).at[dest].set(flat_g[order])
    block_e = jnp.minimum(jnp.searchsorted(pad_end, jnp.arange(n_blocks) * MOE_BLOCK, side='right'),
                          N_EXPERTS - 1).astype(jnp.int32)
    x_pad = jnp.concatenate([x2d, jnp.zeros((1, D), x2d.dtype)], axis=0)
    xs = x_pad[slot_tok].reshape(n_blocks, MOE_BLOCK, D)

    def expert_block(args):
        xb, e = args
        h = xb @ w_gu[e] + b_gu[e]
        g = jnp.minimum(h[:, 0::2], SWIGLU_LIMIT)
        up = jnp.clip(h[:, 1::2], -SWIGLU_LIMIT, SWIGLU_LIMIT)
        act = (up + 1.0) * (g * jax.nn.sigmoid(SWIGLU_ALPHA * g))
        return act @ w_dn[e] + b_dn[e]

    ys = lax.map(expert_block, (xs, block_e)).reshape(n_rows, D)
    out = jnp.zeros((T + 1, D), x2d.dtype).at[slot_tok].add(ys * slot_gate[:, None])
    return out[:T]

def block(x, k_buf, v_buf, conv_buf, h0, pos0,
          g_mix_norm, w_in, g_q_norm, g_k_norm, attn_sinks, conv_w, conv_b,
          w_lru_a, b_lru_a, w_lru_x, b_lru_x, lru_lambda, g_attn_out, g_rnn_out, w_out,
          g_ffn_norm, w_router, b_router, w_gate_up, b_gate_up, w_down, b_down):
    B, S, D = x.shape
    h = rmsnorm(x, g_mix_norm)
    proj = jnp.einsum('bsd,de->bse', h, w_in)
    q, k, v, xr, yr = jnp.split(proj, [D_ATTN, D_ATTN + KV_W, D_ATTN + 2 * KV_W,
                                       D_ATTN + 2 * KV_W + D_RNN], axis=-1)
    pos = pos0 + jnp.arange(S)
    q = partial_rope(rmsnorm(q.reshape(B, S, N_HEADS, HEAD_DIM), g_q_norm), pos)
    k = partial_rope(rmsnorm(k.reshape(B, S, N_KV_HEADS, HEAD_DIM), g_k_norm), pos)
    v = v.reshape(B, S, N_KV_HEADS, HEAD_DIM)
    k_ext = jnp.concatenate([k_buf, k], axis=1)
    v_ext = jnp.concatenate([v_buf, v], axis=1)
    attn = window_attention(q, k_ext, v_ext, attn_sinks, pos0)
    conv_ext = jnp.concatenate([conv_buf, xr], axis=1)
    xc = causal_conv(conv_ext, conv_w, conv_b)
    hseq, h_last = rglru(xc, h0, w_lru_a, b_lru_a, w_lru_x, b_lru_x, lru_lambda)
    rnn = jax.nn.gelu(yr) * hseq
    mixed = jnp.concatenate([rmsnorm(attn, g_attn_out), rmsnorm(rnn, g_rnn_out)], axis=-1)
    x = x + jnp.einsum('bse,ed->bsd', mixed, w_out)
    f = moe(rmsnorm(x, g_ffn_norm).reshape(B * S, D), w_router, b_router,
            w_gate_up, b_gate_up, w_down, b_down).reshape(B, S, D)
    x = x + f
    return (x, k_ext[:, -WINDOW:], v_ext[:, -WINDOW:],
            conv_ext[:, -(CONV_WIDTH - 1):], h_last)

def setup_inputs(seed: int = 0) -> dict:
    key = jax.random.key(seed)
    ks = jax.random.split(key, 32)
    f32 = jnp.float32
    nrm = lambda k, shape, scale: jax.random.normal(k, shape, f32) * scale
    a8 = jax.random.uniform(ks[17], (DEPTH, D_RNN), f32, minval=0.9, maxval=0.999)
    s = a8 ** (1.0 / LRU_C)
    lru_lambda = jnp.log(s) - jnp.log1p(-s)
    return {
        "x_prompt": nrm(ks[0], (BATCH, SEQ, D_MODEL), 1.0),
        "x_sample": nrm(ks[1], (DEC_BATCH, DEC_SEQ, D_MODEL), 1.0),
        "cache_k": nrm(ks[2], (DEPTH, DEC_BATCH, WINDOW, N_KV_HEADS, HEAD_DIM), 1.0),
        "cache_v": nrm(ks[3], (DEPTH, DEC_BATCH, WINDOW, N_KV_HEADS, HEAD_DIM), 1.0),
        "state_conv": nrm(ks[4], (DEPTH, DEC_BATCH, CONV_WIDTH - 1, D_RNN), 1.0),
        "state_h": nrm(ks[5], (DEPTH, DEC_BATCH, D_RNN), 0.5),
        "g_mix_norm": 1.0 + nrm(ks[6], (DEPTH, D_MODEL), 0.02),
        "w_in": nrm(ks[7], (DEPTH, D_MODEL, D_IN), D_MODEL ** -0.5),
        "g_q_norm": 1.0 + nrm(ks[8], (DEPTH, HEAD_DIM), 0.02),
        "g_k_norm": 1.0 + nrm(ks[9], (DEPTH, HEAD_DIM), 0.02),
        "attn_sinks": nrm(ks[10], (DEPTH, N_HEADS), 0.5),
        "conv_w": nrm(ks[11], (DEPTH, CONV_WIDTH, D_RNN), CONV_WIDTH ** -0.5),
        "conv_b": nrm(ks[12], (DEPTH, D_RNN), 0.01),
        "w_lru_a": nrm(ks[13], (DEPTH, N_RNN_BLOCKS, RNN_BLOCK_W, RNN_BLOCK_W), RNN_BLOCK_W ** -0.5),
        "b_lru_a": nrm(ks[14], (DEPTH, N_RNN_BLOCKS, RNN_BLOCK_W), 0.01),
        "w_lru_x": nrm(ks[15], (DEPTH, N_RNN_BLOCKS, RNN_BLOCK_W, RNN_BLOCK_W), RNN_BLOCK_W ** -0.5),
        "b_lru_x": nrm(ks[16], (DEPTH, N_RNN_BLOCKS, RNN_BLOCK_W), 0.01),
        "lru_lambda": lru_lambda,
        "g_attn_out": 1.0 + nrm(ks[18], (DEPTH, D_ATTN), 0.02),
        "g_rnn_out": 1.0 + nrm(ks[19], (DEPTH, D_RNN), 0.02),
        "w_out": nrm(ks[20], (DEPTH, D_MIX, D_MODEL), D_MIX ** -0.5),
        "g_ffn_norm": 1.0 + nrm(ks[21], (DEPTH, D_MODEL), 0.02),
        "w_router": nrm(ks[22], (DEPTH, D_MODEL, N_EXPERTS), D_MODEL ** -0.5),
        "b_router": nrm(ks[23], (DEPTH, N_EXPERTS), 0.01),
        "w_gate_up": nrm(ks[24], (DEPTH, N_EXPERTS, D_MODEL, 2 * D_FF_EXPERT), D_MODEL ** -0.5),
        "b_gate_up": nrm(ks[25], (DEPTH, N_EXPERTS, 2 * D_FF_EXPERT), 0.01),
        "w_down": nrm(ks[26], (DEPTH, N_EXPERTS, D_FF_EXPERT, D_MODEL), D_FF_EXPERT ** -0.5),
        "b_down": nrm(ks[27], (DEPTH, N_EXPERTS, D_MODEL), 0.01),
    }

def reference(x_prompt, x_sample, cache_k, cache_v, state_conv, state_h,
              g_mix_norm, w_in, g_q_norm, g_k_norm, attn_sinks, conv_w, conv_b,
              w_lru_a, b_lru_a, w_lru_x, b_lru_x, lru_lambda, g_attn_out, g_rnn_out, w_out,
              g_ffn_norm, w_router, b_router, w_gate_up, b_gate_up, w_down, b_down):
    B = x_prompt.shape[0]
    dt = x_prompt.dtype
    k0 = jnp.zeros((B, WINDOW, N_KV_HEADS, HEAD_DIM), dt)
    c0 = jnp.zeros((B, CONV_WIDTH - 1, D_RNN), dt)
    h0 = jnp.zeros((B, D_RNN), dt)
    yp, ys = x_prompt, x_sample
    kp_l, vp_l, cp_l, hp_l, ks_l, vs_l, cs_l, hs_l = [], [], [], [], [], [], [], []
    for l in range(DEPTH):
        lp = (g_mix_norm[l], w_in[l], g_q_norm[l], g_k_norm[l], attn_sinks[l], conv_w[l], conv_b[l],
              w_lru_a[l], b_lru_a[l], w_lru_x[l], b_lru_x[l], lru_lambda[l], g_attn_out[l], g_rnn_out[l],
              w_out[l], g_ffn_norm[l], w_router[l], b_router[l], w_gate_up[l], b_gate_up[l],
              w_down[l], b_down[l])
        yp, kp, vp, cp, hp = block(yp, k0, k0, c0, h0, 0, *lp)
        ys, kn, vn, cn, hn = block(ys, cache_k[l], cache_v[l], state_conv[l], state_h[l], PAST_LEN, *lp)
        kp_l.append(kp); vp_l.append(vp); cp_l.append(cp); hp_l.append(hp)
        ks_l.append(kn); vs_l.append(vn); cs_l.append(cn); hs_l.append(hn)
    return (yp, ys,
            jnp.stack(kp_l), jnp.stack(vp_l), jnp.stack(cp_l), jnp.stack(hp_l),
            jnp.stack(ks_l), jnp.stack(vs_l), jnp.stack(cs_l), jnp.stack(hs_l))


_drawn_inputs = setup_inputs


def setup_inputs(seed=0):
    import zlib

    import numpy as np

    out = dict(_drawn_inputs(seed))
    spreads = {}
    factors = {'attn_sinks': 6.883,
     'b_lru_a': 23.479,
     'b_lru_x': 8.0,
     'b_router': 3.16,
     'b_gate_up': 8.0,
     'b_down': 8.0}
    for name, (base, spread) in spreads.items():
        noise = np.random.default_rng([zlib.crc32(name.encode()), seed]).standard_normal(out[name].shape)
        drawn = base * np.exp(spread * noise) if base else spread * noise
        out[name] = __import__('jax').numpy.asarray(drawn.astype(out[name].dtype))
    for name, factor in factors.items():
        out[name] = (out[name] * factor).astype(out[name].dtype)
    return out
```

```python
from contextlib import ExitStack

import concourse.bass as bass
from concourse import mybir

F32 = mybir.dt.float32
I32 = mybir.dt.int32
U32 = mybir.dt.uint32
ALU = mybir.AluOpType
ACT = mybir.ActivationFunctionType
AX = mybir.AxisListType.X

P = 128
D = 1024
KT = D // P
NP_ = 256
NS = 8
T = NP_ + NS
TT = 88
NT = T // TT
HD = 64
NC = 4
DG = 512
E = 32
TK = 4
FF = 1024
D_IN = 1792
CAP = 64
N_OVER = 16
ITEMS = E + N_OVER + 2
SLOTS = 12
BIG = 1 << 20
EPS = 1e-6
SCALE = HD ** -0.5
LRU_C = 8.0
LIMIT = 7.0
ALPHA = 1.702

CONST_SIZES = [("ident", 128), ("blk64", 128), ("mean512", 128), ("rot", 128), ("cos", T), ("sin", T),
               ("mask", 256), ("iota", E), ("tri", TT), ("ones", TT), ("diag", NS), ("sel", 6 * 64)]
COFF = {}
_at = 0
for _n, _w in CONST_SIZES:
    COFF[_n] = (_at, _at + _w)
    _at += _w
NCONST = _at

R_CONV, R_H0, R_CW, R_CB, R_BA, R_BX, R_LAM, R_GR, R_GA, N_VROWS = 0, 24, 32, 36, 37, 38, 39, 40, 41, 42


def hybrid_layer(nc, a, o, scratch):
    ctx = ExitStack()
    with ctx:
        def sb(name, shape, dt=F32):
            return ctx.enter_context(nc.sbuf_tensor(name, shape, dt))

        def sem(name):
            return ctx.enter_context(nc.semaphore(name))

        ring = sb("ring", [P, SLOTS, 2 * FF])
        regA = sb("regA", [P, KT * D_IN])
        con = sb("con", [P, NCONST])
        x_row = sb("x_row", [P, NT, D])
        hT_t = sb("hT_t", [P, KT * T])
        qk = sb("qk", [P, 5, T])
        vT = sb("vT", [P, T])
        xe = sb("xe", [P, NC, 3 + NP_])
        xs = sb("xs", [P, NC, NS])
        yT = sb("yT", [P, NC, T])
        xc = sb("xc", [P, NC, T])
        bd = sb("bd", [P, 2, NC, P])
        vec = sb("vec", [P, NC, N_VROWS])
        vgq = sb("vgq", [P, 2])
        small = sb("small", [P, 64])
        smx = sb("smx", [P, 4, 16])
        kv_new = sb("kv_new", [P, 3, P])
        meta = sb("meta", [P, ITEMS, 3], I32)
        pay = sb("pay", [TT, NT * TK, 3], I32)
        rowi = sb("rowi", [TT, NT * TK], I32)
        ovi = sb("ovi", [1, 1 + N_OVER], I32)
        brt = sb("brt", [TT, E])
        wr = sb("wr", [P, KT, E])
        sink_p = sb("sink_p", [P, 8])
        sink_s = sb("sink_s", [64, 1])
        qbd = sb("qbd", [P, NS, 8])

        ps = ctx.enter_context(nc.psum_tensor("ps", [P, 8, 512], F32))

        def cc(name, p0=0, p1=P):
            return con[p0:p1, COFF[name][0]:COFF[name][1]]

        ident = cc("ident")
        w_in = regA[:, :].rearrange("p (k n) -> p k n", k=KT)
        w_out = regA[:, 0:KT * D].rearrange("p (k n) -> p k n", k=KT)

        def tail(n0, *shape):
            n = shape[0] * shape[1]
            base = KT * D + n0
            return regA[:, base:base + n].rearrange("p (c t) -> p c t", c=shape[0])

        sq = tail(0, 5, T)
        rT = tail(1320, NC, T)
        uT = tail(1320 + 1056, NC, T)
        hs = tail(1320 + 2 * 1056, NC, T)
        tq = tail(1320 + 3 * 1056, NC, T)
        k_rows = tail(1320 + 4 * 1056, 2, P)
        rs_t = xc[:, 0:2, :]
        xg = regA[0:CAP, 0:1024]
        xT = regA[:, 1024:1536].rearrange("p (k t) -> p k t", k=KT)
        b_gu = regA[:, 1536:2048]
        b_dn = regA[:, 2048:2560]
        g_sb = regA[:, 2560:3072]
        up_sb = regA[:, 3072:3584]
        sig_sb = regA[:, 3584:4096]
        act_sb = regA[:, 4096:4608]
        actT = regA[:, 4608:5120].rearrange("p (j t) -> p j t", j=4)
        y_sb = regA[:, 5120:5632]
        gix = regA[:, 5632:5633].bitcast(I32)
        six = regA[:, 5634:5635].bitcast(I32)
        scr = ring[:, 8:12, :].rearrange("p s n -> p (s n)")
        h_row = scr[0:TT, 0:3072].rearrange("p (i n) -> p i n", i=NT)
        g_bc = scr[0:TT, 3072:4096]
        v1 = scr[0:N_VROWS, 4096:4608]
        v2 = scr[0:2, 4608:4736]
        p1_sb = scr[:, 0:2048].rearrange("p (h k) -> p h k", h=8)
        p0_sb = scr[:, 2048:3072].rearrange("p (h k) -> p h k", h=8)
        pT = scr[:, 3072:6144].rearrange("p (g n) -> p g n", g=6)
        kc = scr[:, 6144:7168].rearrange("p (b n) -> p b n", b=NS)
        vc = scr[:, 7168:8192].rearrange("p (b n) -> p b n", b=NS)
        gf_bc = scr[0:TT, 3072:4096]
        hT = hT_t[:, :].rearrange("p (k t) -> p k t", k=KT)
        kcT = hT_t[:, 0:1024].rearrange("p (b n) -> p b n", b=NS)
        oT = hT_t[:, 1024:2080].rearrange("p (c t) -> p c t", c=NC)
        bdf = bd[:, :, :, :].rearrange("p a c n -> p (a c n)")
        s_sb = bdf[0:64, 0:129]
        s_nT = bdf[:, 136:200]
        s_pT = bdf[:, 200:264]
        s_dT = bdf[0:NS, 264:328]
        s_dg = bdf[0:64, 328:336]
        oh = bdf[0:TT, 0:384]
        oht = bdf[0:TT, 384:768]
        rt = bdf[0:TT, 768:1024]

        sinkT = small[:, 0:8]

        s_x, s_con, s_vrow, s_gm, s_kc, s_vc, s_bd, s_misc, s_wout, s_gf = map(
            sem, ("x_landed", "const_landed", "vrows_landed", "gmix_landed", "kcache_landed", "vcache_landed",
                  "gatew_landed", "misc_landed", "wout_landed", "gffn_landed"))
        s_win = [sem(f"win_landed{j}") for j in range(7)]
        s_slot = [sem(f"slot_landed{j}") for j in range(SLOTS)]
        s_empty = sem("table_emptied")
        s_zero = sem("zeroed")
        s_dve, s_act, s_pool = sem("dve_step"), sem("act_step"), sem("pool_step")
        names = ("ss_x", "ms_x", "rstd_x", "hrow", "ht_tr", "ht_cp", "ht_cp2", "vec_tr", "vec_cp", "proj", "proj_cp",
                 "kc_tr", "kc_cp", "v_tr", "v_cp", "sqqk", "msqk", "ivqk", "rsqk", "qn", "rotd", "roped",
                 "conv", "lamabs", "lamexp", "sp", "gate", "gate_s", "av", "u2", "us", "rnn", "sqg", "msg", "ivg",
                 "rsg", "mixed", "scores", "masked", "neg_m", "exps", "pn", "p_tr", "p_cp", "p_cp2", "pv", "o_cp", "qbd_r",
                 "sc_t", "sc_cp", "sc_tr", "s_neg", "s_exp", "s_pn", "s_ptr", "s_pcp", "s_pv", "s_ocp",
                 "h_last", "krow_tr", "krow_cp", "st_tr", "st_cp", "outp", "xmid", "ss_f", "ms_f", "rstd_f", "xn",
                 "xnt_tr", "xnt_cp", "xnt_cp2", "logit", "topd", "tope", "mask", "posd", "rows", "ovd", "metaok", "pay_g")
        S = {n: sem(n) for n in names}
        s_kout, s_xnd, s_tab, s_meta, s_base, s_stout = map(
            sem, ("kv_stored", "xn_stored", "table_scattered", "meta_landed", "base_stored", "states_stored"))
        m_used, m_gu, m_g, m_sig, m_act, m_atr, m_aT, m_y, m_ysb, m_xtr, m_xT = map(
            sem, ("slot_used", "gateup_done", "g_done", "sigmoid_done", "act_done", "act_transposed", "actT_copied",
                  "down_done", "y_scaled", "x_transposed", "xT_copied"))
        m_bgu, m_bdn, m_gix, m_six, m_xg, m_add, s_out = map(
            sem, ("gu_bias_landed", "dn_bias_landed", "gather_index_set", "scatter_index_set", "x_gathered",
                  "results_added", "outputs_stored"))

        m_passed = [sem("pe_waits_passed"), sem("pool_waits_passed")]

        w_gu = a["w_gate_up"].rearrange("l e k n -> (l e k) n")
        w_dn = a["w_down"].rearrange("l e k n -> (l e k) n")
        bgu_v = a["b_gate_up"].rearrange("l e (j n) -> (l e j) n", n=512)
        bdn_v = a["b_down"].rearrange("l e (j n) -> (l e j) n", n=512)
        xn_d, acc_d, tab_d = scratch["xn"], scratch["acc"], scratch["table"]

        block = ctx.enter_context(nc.Block())

        def counter():
            n = {}

            def up(s, k=1):
                n[s.name] = n.get(s.name, 0) + k
                return n[s.name]
            return up

        @block.sync
        def _(sp):
            xp = a["x_prompt"].rearrange("b t d -> (b t) d")
            xsm = a["x_sample"].rearrange("b t d -> (b t) d")
            sp.dma_start(x_row[0:TT, 0:2, :], xp[0:2 * TT, :].rearrange("(i p) d -> p i d", p=TT)).then_inc(s_x, 16)
            sp.dma_start(x_row[0:NP_ - 2 * TT, 2, :], xp[2 * TT:NP_, :]).then_inc(s_x, 16)
            sp.dma_start(x_row[NP_ - 2 * TT:TT, 2, :], xsm).then_inc(s_x, 16)
            sp.dma_start(con[:, :], a["const"][:, :]).then_inc(s_con, 16)
            for j, c0 in enumerate((768, 1024, 0, 256, 512, 1280, 1536)):
                sp.dma_start(w_in[:, :, c0:c0 + 256],
                             a["w_in"][0, :, c0:c0 + 256].rearrange("(k p) n -> p k n", p=P)).then_inc(s_win[j], 16)

            def load_slot(s, e):
                if s < KT:
                    src = w_gu[bass.ds(e * D + s * P, P), :]
                    dst = ring[:, s, :]
                else:
                    src = w_dn[bass.ds(e * FF + (s - KT) * 2 * P, 2 * P), :].rearrange("(t p) n -> p t n", p=P)
                    dst = ring[:, s, :].rearrange("p (t n) -> p t n", t=2)
                sp.dma_start(dst, src).then_inc(s_slot[s], 16)

            for s in range(KT):
                load_slot(s, 0)
            sp.wait_ge(S["proj"], 14)
            for g in range(2):
                sp.dma_start(w_out[64 * g:64 * g + 64, 0:NC, :],
                             a["w_out"][0, 256 * g:256 * g + 256, :].rearrange("(c d) n -> d c n", d=HD)
                             ).then_inc(s_wout, 16)
            sp.dma_start(w_out[:, NC:KT, :],
                         a["w_out"][0, DG:D, :].rearrange("(c p) n -> p c n", p=P)).then_inc(s_wout, 16)
            sp.wait_ge(S["pv"], 2)
            sp.dma_start(gf_bc, a["g_ffn_norm"].to_broadcast([TT, D])).then_inc(s_gf, 16)
            sp.wait_ge(S["xmid"], 2 * NT)
            sp.dma_start(acc_d[:, :].rearrange("(i p) d -> p i d", p=TT), x_row[0:TT, :, :]).then_inc(s_base, 16)
            sp.wait_ge(S["xn"], NT)
            sp.dma_start(xn_d[:, :].rearrange("(i p) d -> p i d", p=TT), h_row[:, :, :]).then_inc(s_xnd, 16)
            sp.wait_ge(s_xnd, 16)
            sp.wait_ge(s_stout, 16 * 4)
            sp.wait_ge(S["xnt_tr"], KT)
            for s in range(KT, SLOTS):
                load_slot(s, 0)
            sp.wait_ge(s_tab, 16 * NT * TK)
            for g in range(2):
                sp.dma_start(meta[64 * g:64 * g + 64, :, :],
                             tab_d[:, :].rearrange("(p i) f -> p i f", p=CAP)).then_inc(s_meta, 16)

            def load_item(q, e):
                for s in range(SLOTS):
                    sp.wait_ge(m_used, q * SLOTS - (SLOTS - 1 - s))
                    load_slot(s, e)

            with sp.Fori(1, E) as q:
                load_item(q, q)
            sp.wait_ge(S["ovd"], 1)
            n_over = sp.value_load(ovi[0:1, 0:1], min_val=0, max_val=N_OVER)
            with sp.If(n_over > 0):
                with sp.Fori(0, n_over) as m:
                    e = sp.value_load(ovi[0:1, bass.ds(m + 1, 1)], min_val=0, max_val=E - 1)
                    load_item(m + E, e)
            sp.wait_ge(s_kout, 16 * 7)
            sp.wait_ge(s_stout, 16 * 4)

        @block.gpsimd
        def _(pool):
            for t in (xe[:, :, 0:3], bd[:, :, :, :], qbd[:, :, :]):
                pool.memset(t, 0).then_inc(s_zero, 1)
            pool.wait_ge(s_zero, 2)
            for n, w in enumerate((a["w_lru_a"], a["w_lru_x"])):
                for j in range(2):
                    pool.dma_start(bd[64 * j:64 * j + 64, n, :, 64 * j:64 * j + 64],
                                   w[0].rearrange("(c j) i o -> j i c o", j=2)[j]).then_inc(s_bd, 16)
            pool.dma_start(kc[:, :, :], a["cache_k"][0].rearrange("b w k d -> w b (k d)")).then_inc(s_kc, 16)
            pool.dma_start(vc[:, :, :], a["cache_v"][0].rearrange("b w k d -> w b (k d)")).then_inc(s_vc, 16)
            pool.dma_start(wr[:, :, :], a["w_router"][0].rearrange("(k p) n -> p k n", p=P)).then_inc(s_misc, 16)
            pool.dma_start(brt[:, :], a["b_router"].to_broadcast([TT, E])).then_inc(s_misc, 16)
            pool.dma_start(sink_p[:, :], a["attn_sinks"].to_broadcast([P, 8])).then_inc(s_misc, 16)
            for b in range(NS):
                pool.dma_start(sink_s[8 * b:8 * b + 8, :],
                               a["attn_sinks"].rearrange("l h -> h l")).then_inc(s_misc, 16)
            pool.dma_start(pay[:, :, 0:2], a["slots"][:, :].rearrange("p (s f) -> p s f", f=2)).then_inc(s_misc, 16)
            pool.dma_start(tab_d[:, :], a["empty"][:, :]).then_inc(s_empty, 16)
            for name in "kv":
                pool.dma_start(o[f"new_{name}_sample"][0, :, 0:127].rearrange("b w k d -> b (w k d)"),
                               a[f"cache_{name}"][0, :, 1:128].rearrange("b w k d -> b (w k d)")
                               ).then_inc(s_kout, 16)
            pool.dma_start(o["new_conv_sample"][0, :, 0:2, :].rearrange("b j c -> b (j c)"),
                           a["state_conv"][0, :, 1:3, :].rearrange("b j c -> b (j c)")).then_inc(s_kout, 16)
            pool.wait_ge(S["v_cp"], 1)
            pool.dma_start(o["new_v_prompt"][0, 0].rearrange("w k d -> w (k d)"), kv_new[:, 1, :]).then_inc(s_kout, 16)
            pool.dma_start(o["new_v_sample"][0, :, 127].rearrange("b k d -> b (k d)"),
                           kv_new[0:NS, 2, :]).then_inc(s_kout, 16)
            pool.wait_ge(S["krow_cp"], 1)
            pool.dma_start(o["new_k_prompt"][0, 0].rearrange("w k d -> w (k d)"), k_rows[:, 0, :]).then_inc(s_kout, 16)
            pool.dma_start(o["new_k_sample"][0, :, 127].rearrange("b k d -> b (k d)"),
                           k_rows[0:NS, 1, :]).then_inc(s_kout, 16)

            pool.wait_ge(S["outp"], 2 * NT)
            for n, t in enumerate((b_gu, b_dn, xg)):
                pool.memset(t, 0.0).then_inc(s_zero, 1)
            pool.wait_ge(S["rows"], 1)
            pool.wait_ge(S["pay_g"], 1)
            pool.wait_ge(s_empty, 16)
            for s in range(NT * TK):
                pool.indirect_dma_start(tab_d[:, :],
                                        bass.IndirectOffsetOnAxis(ap=rowi[:, s:s + 1].bitcast(U32), axis=0),
                                        pay[:, s, :], None, bounds_check=CAP * ITEMS - 1,
                                        oob_is_err=False).then_inc(s_tab, 16)

            def gather(q):
                pool.tensor_copy(gix[0:CAP, :], meta[0:CAP, bass.ds(q, 1), 0]).then_inc(m_gix, 1)
                pool.wait_ge(m_gix, q + 1)
                pool.sem_inc(m_passed[1], 1)
                pool.indirect_dma_start(xg, None, xn_d[:, :],
                                        bass.IndirectOffsetOnAxis(ap=gix[0:CAP, 0:1].bitcast(U32), axis=0),
                                        bounds_check=T - 1, oob_is_err=False).then_inc(m_xg, 16)

            pool.wait_ge(S["metaok"], 1)
            pool.wait_ge(s_zero, 6)
            pool.wait_ge(s_xnd, 16)
            gather(0)
            pool.wait_ge(m_xg, 16)
            pool.wait_ge(m_xtr, 1)
            gather(1)
            pool.wait_ge(s_base, 16)

            halves = acc_d[:, :].rearrange("t (h d) -> (t h) d", h=2)

            def item(q):
                pool.tensor_copy(six, meta[:, bass.ds(q, 1), 1]).then_inc(m_six, 1)
                pool.wait_ge(m_xg, 16 * q + 32)
                pool.wait_ge(m_xtr, q + 2)
                gather(q + 2)
                pool.wait_ge(m_six, q + 1)
                pool.wait_ge(m_ysb, q + 1)
                pool.sem_inc(m_passed[1], 1)
                pool.indirect_dma_start(halves, bass.IndirectOffsetOnAxis(ap=six.bitcast(U32), axis=0),
                                        y_sb, None, bounds_check=2 * T - 1, oob_is_err=False,
                                        compute_op=ALU.add).then_inc(m_add, 16)
                pool.wait_ge(m_add, 16 * q + 16)

            with pool.Fori(0, E) as q:
                item(q)
            n_over = pool.value_load(ovi[0:1, 0:1], min_val=0, max_val=N_OVER)
            with pool.If(n_over > 0):
                with pool.Fori(0, n_over) as m:
                    item(m + E)
            pool.wait_ge(m_xg, 16 * E + 32 + 16 * n_over)
            pool.sem_inc(m_passed[1], 1)
            pool.dma_start(o["y_prompt"][0], acc_d[0:NP_, :]).then_inc(s_out, 16)
            pool.dma_start(o["y_sample"].rearrange("b t d -> (b t) d"), acc_d[NP_:T, :]).then_inc(s_out, 16)
            pool.wait_ge(s_out, 32)

        @block.scalar
        def _(act):
            up = counter()

            def then(ins, name=None):
                s = S[name] if name else s_act
                n = up(s)
                ins.then_inc(s, 1)
                act.wait_ge(s, n)

            r = v1
            act.dma_start(r[R_CONV:R_CONV + 24, :], a["state_conv"][0].rearrange("b j c -> (b j) c")
                          ).then_inc(s_vrow, 16)
            act.dma_start(r[R_H0:R_H0 + NS, :], a["state_h"][0]).then_inc(s_vrow, 16)
            act.dma_start(r[R_CW:R_CW + 4, :], a["conv_w"][0]).then_inc(s_vrow, 16)
            act.dma_start(r[R_CB:R_CB + 1, :], a["conv_b"]).then_inc(s_vrow, 16)
            act.dma_start(r[R_BA:R_BA + 1, :], a["b_lru_a"].rearrange("l n c -> l (n c)")).then_inc(s_vrow, 16)
            act.dma_start(r[R_BX:R_BX + 1, :], a["b_lru_x"].rearrange("l n c -> l (n c)")).then_inc(s_vrow, 16)
            act.dma_start(r[R_LAM:R_LAM + 1, :], a["lru_lambda"]).then_inc(s_vrow, 16)
            act.dma_start(r[R_GR:R_GR + 1, :], a["g_rnn_out"]).then_inc(s_vrow, 16)
            for g in range(2):
                act.dma_start(r[R_GA:R_GA + 1, :].rearrange("p (c g d) -> p g c d", g=2, d=HD)[:, g],
                              a["g_attn_out"].rearrange("l (g c d) -> l g c d", g=2, d=HD)[:, g]
                              ).then_inc(s_vrow, 16)
                for n, w in enumerate((a["g_q_norm"], a["g_k_norm"])):
                    act.dma_start(v2[n:n + 1, 64 * g:64 * g + 64], w).then_inc(s_vrow, 16)
            act.dma_start(g_bc, a["g_mix_norm"].to_broadcast([TT, D])).then_inc(s_gm, 16)

            act.wait_ge(s_x, 48)
            for i in range(NT):
                then(act.activation(h_row[:, i, :], x_row[0:TT, i, :], ACT.Square,
                                    accum_out=small[0:TT, i:i + 1]), "ss_x")
            act.wait_ge(S["ms_x"], 1)
            then(act.activation(small[0:TT, 8:11], small[0:TT, 4:7], ACT.Sqrt), "rstd_x")
            act.wait_ge(S["vec_tr"], 1)
            then(act.activation(vec[:, :, :], ps[:, 6, 0:NC * N_VROWS].rearrange("p (c r) -> p c r", c=NC), ACT.Copy))
            then(act.activation(vgq[:, :], ps[:, 6, 200:202], ACT.Copy), "vec_cp")
            for kt in range(1, KT, 2):
                act.wait_ge(S["ht_tr"], kt + 1)
                then(act.activation(hT[:, kt, :], ps[:, kt % 4, 0:T], ACT.Copy), "ht_cp")
            act.wait_ge(S["lamabs"], 1)
            then(act.activation(small[:, 20:24], small[:, 16:20], ACT.Exp, scale=-1.0), "lamexp")
            for n in range(14):
                act.wait_ge(S["proj"], n + 1)
                src = ps[:, n % 4, 0:T]
                if n < 4:
                    if n == 0:
                        act.wait_ge(s_zero, 1)
                    then(act.activation(xs[:, n, :], src[:, NP_:T], ACT.Copy))
                    then(act.activation(xe[:, n, 3:3 + NP_], src[:, 0:NP_], ACT.Copy), "proj_cp")
                elif n < 8:
                    for h in (2 * (n - 4), 2 * (n - 4) + 1):
                        g, p0 = h // 4, 64 * (h % 2)
                        then(act.activation(qk[64 * g:64 * g + 64, h % 4, :], src[p0:p0 + 64], ACT.Copy),
                             "proj_cp" if h % 2 else None)
                elif n == 8:
                    then(act.activation(qk[:, 4, :], src, ACT.Copy), "proj_cp")
                elif n == 9:
                    then(act.activation(vT[:, :], src, ACT.Copy), "proj_cp")
                else:
                    then(act.activation(yT[:, n - 10, :], src, ACT.Gelu_apprx_tanh), "proj_cp")
            then(act.activation(sq[:, :, :], qk[:, :, :], ACT.Square), "sqqk")
            act.wait_ge(S["kc_tr"], 1)
            then(act.activation(kcT[:, :, :], ps[:, 0:2, :].rearrange("p g (b n) -> p (g b) n", b=4), ACT.Copy),
                 "kc_cp")
            act.wait_ge(S["v_tr"], 1)
            then(act.activation(kv_new[:, 0:2, :], ps[:, 2, 0:256].rearrange("p (b n) -> p b n", b=2), ACT.Copy))
            then(act.activation(kv_new[0:NS, 2, :], ps[0:NS, 2, 256:384], ACT.Copy), "v_cp")
            act.wait_ge(S["ivqk"], 1)
            then(act.activation(sq[:, :, :], sq[:, :, :], ACT.Sqrt), "rsqk")
            for n in range(2 * NC):
                c, x = n // 2, n % 2
                act.wait_ge(S["gate"], n + 1)
                then(act.activation((uT if x else rT)[:, c, :], ps[:, n % 3, 0:T], ACT.Sigmoid,
                                    bias=vec[:, c, R_BX if x else R_BA:(R_BX if x else R_BA) + 1]), "gate_s")
            act.wait_ge(S["sp"], 1)
            for c in range(NC):
                then(act.activation(hs[:, c, :], rT[:, c, :], ACT.Tanh, scale=small[:, 24 + c:25 + c]))
                then(act.activation(rT[:, c, :], rT[:, c, :], ACT.Exp, scale=small[:, 28 + c:29 + c]), "av")
            act.wait_ge(S["u2"], 1)
            then(act.activation(tq[:, :, :], tq[:, :, :], ACT.Sqrt), "us")
            act.wait_ge(S["sc_t"], 1)
            then(act.activation(s_nT, ps[:, 6, 0:64], ACT.Copy), "sc_cp")
            act.wait_ge(S["neg_m"], 1)
            for n, pt in ((1, p1_sb), (0, p0_sb)):
                for h in range(8):
                    act.activation(pt[:, h, :], pt[:, h, :], ACT.Exp, scale=SCALE,
                                   bias=smx[:, 1, 8 * n + h:8 * n + h + 1],
                                   accum_out=smx[:, 2, 8 * n + h:8 * n + h + 1]).then_inc(s_act, 1)
                    up(s_act)
            then(act.activation(smx[:, 3, :], smx[:, 3, :], ACT.Exp), "exps")
            act.wait_ge(S["s_neg"], 1)
            then(act.activation(s_sb, s_sb, ACT.Exp, scale=SCALE, bias=small[0:64, 33:34],
                                accum_out=small[0:64, 34:35]))
            then(act.activation(small[0:64, 35:36], sink_s[:, :], ACT.Exp, bias=small[0:64, 33:34]), "s_exp")
            act.wait_ge(S["krow_tr"], 1)
            then(act.activation(k_rows[:, 0, :], ps[:, 7, 256:384], ACT.Copy))
            then(act.activation(k_rows[0:NS, 1, :], ps[0:NS, 7, 384:512], ACT.Copy), "krow_cp")
            for g in (0, 2, 4):
                act.wait_ge(S["p_tr"], g + 1)
                then(act.activation(pT[:, g, :], ps[:, g, :], ACT.Copy), "p_cp")
            act.wait_ge(S["s_ptr"], 1)
            then(act.activation(s_pT, ps[:, 6, 0:64], ACT.Copy))
            then(act.activation(s_dT, ps[0:NS, 6, 128:192], ACT.Copy), "s_pcp")
            act.wait_ge(S["rnn"], 1)
            then(act.activation(tq[:, :, :], yT[:, :, :], ACT.Square), "sqg")
            act.wait_ge(S["o_cp"], 3)
            then(act.activation(sq[:, 0:NC, :], oT[:, :, :], ACT.Square), "sqg")
            act.wait_ge(S["ivg"], 1)
            then(act.activation(rs_t[:, :, :], rs_t[:, :, :], ACT.Sqrt), "rsg")
            act.wait_ge(S["st_tr"], 1)
            st = scr[0:9, 6144:7680].rearrange("p (g n) -> p g n", g=3)
            then(act.activation(st[0:9, 0, :], ps[0:9, 0, :], ACT.Copy))
            then(act.activation(st[0:3, 1, :], ps[0:3, 1, :], ACT.Copy))
            then(act.activation(st[0:NS, 2, :], ps[0:NS, 2, :], ACT.Copy), "st_cp")
            act.dma_start(o["new_h_prompt"][0], st[0:1, 0, :]).then_inc(s_stout, 16)
            act.dma_start(o["new_h_sample"][0], st[1:9, 0, :]).then_inc(s_stout, 16)
            act.dma_start(o["new_conv_prompt"][0, 0], st[0:3, 1, :]).then_inc(s_stout, 16)
            act.dma_start(o["new_conv_sample"][0, :, 2], st[0:NS, 2, :]).then_inc(s_stout, 16)
            for i in range(NT):
                act.wait_ge(S["xmid"], 2 * i + 2)
                if i == 0:
                    act.wait_ge(S["mixed"], 2)
                then(act.activation(h_row[:, i, :], x_row[0:TT, i, :], ACT.Square,
                                    accum_out=small[0:TT, 36 + i:37 + i]), "ss_f")
            act.wait_ge(S["ms_f"], 1)
            then(act.activation(small[0:TT, 40:43], small[0:TT, 40:43], ACT.Sqrt), "rstd_f")
            for kt in range(1, KT, 2):
                act.wait_ge(S["xnt_tr"], kt + 1)
                then(act.activation(hT[:, kt, :], ps[:, kt % 4, 0:T], ACT.Copy), "xnt_cp")
            act.wait_ge(S["topd"], 1)
            then(act.activation(rt[:, 48:60], rt[:, 48:60], ACT.Exp), "tope")

            def copy_x(q):
                act.wait_ge(m_xtr, q + 1)
                act.activation(xT[:, :, :], ps[:, 0, :].rearrange("p (k t) -> p k t", k=KT),
                               ACT.Copy).then_inc(m_xT, 1)

            def item(q):
                act.wait_ge(m_g, q + 1)
                act.activation(sig_sb, g_sb, ACT.Sigmoid, scale=ALPHA).then_inc(m_sig, 1)
                copy_x(q + 1)
                act.wait_ge(m_atr, q + 1)
                act.activation(actT[:, :, :], ps[:, 3, :].rearrange("p (j t) -> p j t", j=4),
                               ACT.Copy).then_inc(m_aT, 1)

            def bias_gu(q, e):
                act.dma_start(b_gu[0:4, :], bgu_v[bass.ds(e * 4, 4), :]).then_inc(m_bgu, 16)

            def bias_dn(q, e):
                act.dma_start(b_dn[0:2, :], bdn_v[bass.ds(e * 2, 2), :]).then_inc(m_bdn, 16)

            act.wait_ge(s_zero, 6)
            bias_gu(0, 0)
            bias_dn(0, 0)
            copy_x(0)

            def step(q, e_next):
                item(q)
                bias_gu(q + 1, e_next)
                act.wait_ge(m_y, q + 1)
                bias_dn(q + 1, e_next)

            with act.Fori(0, E - 1) as q:
                step(q, q + 1)
            act.wait_ge(S["ovd"], 1)
            n_over = act.value_load(ovi[0:1, 0:1], min_val=0, max_val=N_OVER)
            item(E - 1)
            with act.If(n_over > 0):
                with act.Fori(0, n_over) as m:
                    e = act.value_load(ovi[0:1, bass.ds(m + 1, 1)], min_val=0, max_val=E - 1)
                    bias_gu(m + E, e)
                    act.wait_ge(m_y, m + E)
                    bias_dn(m + E, e)
                    item(m + E)

        @block.vector
        def _(dve):
            up = counter()

            def then(ins, name=None):
                s = S[name] if name else s_dve
                n = up(s)
                ins.then_inc(s, 1)
                dve.wait_ge(s, n)

            def inv(dst, src, scale):
                then(dve.tensor_scalar(dst, src, scale, EPS, ALU.mult, ALU.add))

            dve.wait_ge(S["ss_x"], NT)
            inv(small[0:TT, 4:7], small[0:TT, 0:3], 1.0 / D)
            then(dve.reciprocal(small[0:TT, 4:7], small[0:TT, 4:7]), "ms_x")
            dve.wait_ge(S["rstd_x"], 1)
            dve.wait_ge(s_gm, 16)
            for i in range(NT):
                then(dve.scalar_tensor_tensor(out=h_row[:, i, :], in0=x_row[0:TT, i, :], scalar=small[0:TT, 8 + i:9 + i],
                                              in1=g_bc, op0=ALU.mult, op1=ALU.mult), "hrow")
            for kt in range(0, KT, 2):
                dve.wait_ge(S["ht_tr"], kt + 1)
                then(dve.tensor_copy(hT[:, kt, :], ps[:, kt % 4, 0:T]), "ht_cp2")
            dve.wait_ge(S["vec_cp"], 1)
            lam = vec[:, :, R_LAM]
            then(dve.tensor_scalar(small[:, 12:16], lam, -1.0, None, ALU.mult))
            then(dve.tensor_tensor(small[:, 16:20], lam, small[:, 12:16], ALU.max), "lamabs")
            dve.wait_ge(S["lamexp"], 1)
            z, w, w2, acc = small[:, 20:24], small[:, 44:48], small[:, 48:52], small[:, 52:56]
            then(dve.tensor_scalar(w, z, 2.0, None, ALU.add))
            then(dve.reciprocal(w, w))
            then(dve.tensor_tensor(w, w, z, ALU.mult))
            then(dve.tensor_tensor(w2, w, w, ALU.mult))
            then(dve.tensor_scalar(acc, w2, 1.0 / 17, 1.0 / 15, ALU.mult, ALU.add))
            for k in (13, 11, 9, 7, 5, 3, 1):
                then(dve.tensor_tensor(acc, acc, w2, ALU.mult))
                then(dve.tensor_scalar(acc, acc, 1.0 / k, None, ALU.add))
            then(dve.tensor_tensor(acc, acc, w, ALU.mult))
            then(dve.tensor_scalar(small[:, 12:16], small[:, 12:16], 0.0, None, ALU.max))
            then(dve.scalar_tensor_tensor(out=acc, in0=acc, scalar=2.0, in1=small[:, 12:16],
                                          op0=ALU.mult, op1=ALU.add))
            then(dve.tensor_scalar(small[:, 24:28], acc, LRU_C, None, ALU.mult))
            then(dve.tensor_scalar(small[:, 28:32], acc, -LRU_C, None, ALU.mult), "sp")

            for c in range(NC):
                dve.wait_ge(S["proj_cp"], c + 1)
                for out, tap in ((xc[:, c, 0:NP_], lambda j: xe[:, c, j:j + NP_]),
                                 (xc[:, c, NP_:T], lambda j: vec[:, c, R_CONV + j:R_CONV + 24:3] if j < 3
                                  else xs[:, c, :])):
                    then(dve.tensor_scalar(out, tap(0), vec[:, c, R_CW:R_CW + 1], vec[:, c, R_CB:R_CB + 1],
                                           ALU.mult, ALU.add))
                    for j in range(1, 4):
                        then(dve.scalar_tensor_tensor(out=out, in0=tap(j), scalar=vec[:, c, R_CW + j:R_CW + j + 1],
                                                      in1=out, op0=ALU.mult, op1=ALU.add),
                             "conv" if j == 3 else None)

            dve.wait_ge(S["msqk"], 1)
            then(dve.tensor_scalar(sq[:, :, :], ps[:, 3:8, 0:T], EPS, None, ALU.add))
            then(dve.reciprocal(sq[:, :, :], sq[:, :, :]), "ivqk")
            dve.wait_ge(S["rsqk"], 1)
            then(dve.scalar_tensor_tensor(out=qk[:, 0:4, :], in0=qk[:, 0:4, :], scalar=vgq[:, 0:1], in1=sq[:, 0:4, :],
                                          op0=ALU.mult, op1=ALU.mult))
            then(dve.scalar_tensor_tensor(out=qk[:, 4, :], in0=qk[:, 4, :], scalar=vgq[:, 1:2], in1=sq[:, 4, :],
                                          op0=ALU.mult, op1=ALU.mult), "qn")
            dve.wait_ge(S["rotd"], 1)
            cosb = cc("cos")[:, None, :].to_broadcast([P, 5, T])
            sinb = cc("sin")[:, None, :].to_broadcast([P, 5, T])
            then(dve.tensor_tensor(sq[:, :, :], ps[:, 3:8, 0:T], sinb, ALU.mult))
            then(dve.tensor_tensor(qk[:, :, :], qk[:, :, :], cosb, ALU.mult))
            then(dve.tensor_tensor(qk[:, :, :], qk[:, :, :], sq[:, :, :], ALU.add), "roped")
            dve.wait_ge(s_zero, 3)
            for g in range(2):
                then(dve.tensor_copy(qbd[64 * g:64 * g + 64, :, 4 * g:4 * g + 4].rearrange("p b c -> p c b"),
                                     qk[64 * g:64 * g + 64, 0:4, NP_:T]), "qbd_r")

            dve.wait_ge(S["av"], NC)
            then(dve.tensor_tensor(tq[:, :, :], rT[:, :, :], rT[:, :, :], ALU.mult))
            then(dve.scalar_tensor_tensor(out=tq[:, :, :], in0=tq[:, :, :], scalar=1.0, in1=hs[:, :, :],
                                          op0=ALU.add, op1=ALU.mult), "u2")
            then(dve.tensor_tensor(uT[:, :, :], uT[:, :, :], xc[:, :, :], ALU.mult))
            dve.wait_ge(S["scores"], 1)
            maskb = cc("mask")[:, None, :].to_broadcast([P, 8, 256])
            then(dve.tensor_tensor(p1_sb[:, :, :], ps[:, 0:4, :].rearrange("p g (h k) -> p (g h) k", h=2),
                                   maskb, ALU.add))
            then(dve.tensor_tensor(p0_sb[:, :, :], ps[:, 4:6, :].rearrange("p g (h k) -> p (g h) k", h=4),
                                   maskb[:, :, 128:256], ALU.add), "masked")
            then(dve.tensor_reduce(smx[:, 0, 8:16], p1_sb[:, :, :], AX, ALU.max))
            then(dve.tensor_reduce(smx[:, 0, 0:8], p0_sb[:, :, :], AX, ALU.max))
            dve.wait_ge(s_misc, 16 * 12)
            sinkb = sink_p[:, None, :].to_broadcast([P, 2, 8])
            m3 = smx[:, 0, :].rearrange("p (n h) -> p n h", n=2)
            then(dve.scalar_tensor_tensor(out=m3, in0=m3, scalar=SCALE, in1=sinkb, op0=ALU.mult, op1=ALU.max))
            then(dve.tensor_tensor(smx[:, 3, :].rearrange("p (n h) -> p n h", n=2), sinkb, m3, ALU.subtract))
            then(dve.tensor_scalar(smx[:, 1, :], smx[:, 0, :], -1.0, None, ALU.mult), "neg_m")
            dve.wait_ge(S["sc_tr"], 1)
            dve.wait_ge(s_con, 16)
            then(dve.tensor_tensor(s_dg, ps[0:64, 7, 0:8], cc("diag", 0, 64), ALU.mult))
            then(dve.tensor_reduce(s_sb[:, 128:129], s_dg, AX, ALU.add))
            then(dve.tensor_copy(s_sb[:, 0:128], ps[0:64, 7, 128:256]))
            then(dve.tensor_reduce(small[0:64, 32:33], s_sb, AX, ALU.max))
            then(dve.scalar_tensor_tensor(out=small[0:64, 33:34], in0=small[0:64, 32:33], scalar=SCALE,
                                          in1=sink_s[:, :], op0=ALU.mult, op1=ALU.max))
            then(dve.tensor_scalar(small[0:64, 33:34], small[0:64, 33:34], -1.0, None, ALU.mult), "s_neg")
            dve.wait_ge(S["us"], 1)
            then(dve.tensor_tensor(uT[:, :, :], uT[:, :, :], tq[:, :, :], ALU.mult))
            for c in range(NC):
                then(dve.tensor_tensor_scan(hs[:, c, 0:NP_], rT[:, c, 0:NP_], uT[:, c, 0:NP_], 0.0,
                                            ALU.mult, ALU.add))
            then(dve.tensor_tensor(hs[:, :, NP_:T], rT[:, :, NP_:T], vec[:, :, R_H0:R_H0 + NS], ALU.mult))
            then(dve.tensor_tensor(hs[:, :, NP_:T], hs[:, :, NP_:T], uT[:, :, NP_:T], ALU.add), "h_last")
            then(dve.tensor_tensor(yT[:, :, :], yT[:, :, :], hs[:, :, :], ALU.mult), "rnn")
            dve.wait_ge(S["exps"], 1)
            then(dve.tensor_tensor(smx[:, 2, :], smx[:, 2, :], smx[:, 3, :], ALU.add))
            then(dve.reciprocal(smx[:, 2, :], smx[:, 2, :]))
            for n, pt, w_ in ((0, p0_sb, 128), (1, p1_sb, 256)):
                then(dve.tensor_tensor(pt[:, :, :], pt[:, :, :],
                                       smx[:, 2, 8 * n:8 * n + 8][:, :, None].to_broadcast([P, 8, w_]), ALU.mult),
                     "pn")
            dve.wait_ge(S["s_exp"], 1)
            then(dve.tensor_tensor(small[0:64, 34:35], small[0:64, 34:35], small[0:64, 35:36], ALU.add))
            then(dve.reciprocal(small[0:64, 34:35], small[0:64, 34:35]))
            then(dve.tensor_scalar(s_sb, s_sb, small[0:64, 34:35], None, ALU.mult))
            then(dve.tensor_scalar(s_dg, cc("diag", 0, 64), s_sb[:, 128:129], None, ALU.mult), "s_pn")
            for g in (1, 3, 5):
                dve.wait_ge(S["p_tr"], g + 1)
                then(dve.tensor_copy(pT[:, g, :], ps[:, g, :]), "p_cp2")
            for n in range(2):
                dve.wait_ge(S["pv"], n + 1)
                then(dve.tensor_copy(oT[:, :, P * n:P * n + P],
                                     ps[:, 6 + n, :].rearrange("p (c t) -> p c t", c=NC)), "o_cp")
            dve.wait_ge(S["s_pv"], 1)
            for g in range(2):
                src = ps[64 * g:64 * g + 64, 5, 0:64].rearrange("p (b g c) -> p g c b", g=2, c=4)
                ins = dve.tensor_copy(oT[64 * g:64 * g + 64, :, NP_:T], src[:, g])
                then(ins, "o_cp" if g else None)
            dve.wait_ge(S["msg"], 2)
            then(dve.tensor_scalar(rs_t[:, :, :], ps[:, 3:5, 0:T], EPS, None, ALU.add))
            then(dve.reciprocal(rs_t[:, :, :], rs_t[:, :, :]), "ivg")
            dve.wait_ge(S["rsg"], 1)
            for c in range(NC):
                then(dve.scalar_tensor_tensor(out=yT[:, c, :], in0=yT[:, c, :], scalar=vec[:, c, R_GR:R_GR + 1],
                                              in1=rs_t[:, 0, :], op0=ALU.mult, op1=ALU.mult),
                     "mixed" if c == 3 else None)
            for c in range(NC):
                then(dve.scalar_tensor_tensor(out=oT[:, c, :], in0=oT[:, c, :], scalar=vec[:, c, R_GA:R_GA + 1],
                                              in1=rs_t[:, 1, :], op0=ALU.mult, op1=ALU.mult),
                     "mixed" if c == 3 else None)
            for i in range(NT):
                for n in range(2):
                    dve.wait_ge(S["outp"], 2 * i + n + 1)
                    then(dve.tensor_tensor(x_row[0:TT, i, 512 * n:512 * n + 512],
                                           x_row[0:TT, i, 512 * n:512 * n + 512],
                                           ps[0:TT, 2 * i + n, :], ALU.add), "xmid")
            dve.wait_ge(S["ss_f"], NT)
            inv(small[0:TT, 40:43], small[0:TT, 36:39], 1.0 / D)
            then(dve.reciprocal(small[0:TT, 40:43], small[0:TT, 40:43]), "ms_f")
            dve.wait_ge(S["rstd_f"], 1)
            dve.wait_ge(s_gf, 16)
            for i in range(NT):
                then(dve.scalar_tensor_tensor(out=h_row[:, i, :], in0=x_row[0:TT, i, :],
                                              scalar=small[0:TT, 40 + i:41 + i], in1=gf_bc,
                                              op0=ALU.mult, op1=ALU.mult), "xn")
            for kt in range(0, KT, 2):
                dve.wait_ge(S["xnt_tr"], kt + 1)
                then(dve.tensor_copy(hT[:, kt, :], ps[:, kt % 4, 0:T]), "xnt_cp2")

            lg = rt[:, 64:160].rearrange("p (i e) -> p i e", i=NT)
            mx8 = rt[:, 0:24].rearrange("p (i k) -> p i k", i=NT)
            ix8 = rt[:, 24:48].bitcast(U32).rearrange("p (i k) -> p i k", i=NT)
            ex = rt[:, 48:60].rearrange("p (i k) -> p i k", i=NT)
            dve.wait_ge(S["logit"], 1)
            then(dve.tensor_tensor(lg, ps[0:TT, 7, 0:96].rearrange("p (i e) -> p i e", i=NT),
                                   brt[:, None, :].to_broadcast([TT, NT, E]), ALU.add))
            for i in range(NT):
                then(dve.max(mx8[:, i, :], lg[:, i, :]))
                then(dve.max_index(ix8[:, i, :], mx8[:, i, :], lg[:, i, :]))
            then(dve.tensor_tensor(ex, mx8[:, :, 0:4], mx8[:, :, 0:1].to_broadcast([TT, NT, TK]), ALU.subtract), "topd")
            n12 = NT * TK
            ixf, posk, cch, bk, row = (rt[:, 160 + n12 * j:160 + n12 * (j + 1)] for j in range(5))
            msk = oht[:, 0:96].rearrange("p (i e) -> p i e", i=NT)
            then(dve.tensor_copy(ixf.rearrange("p (i k) -> p i k", i=NT), ix8[:, :, 0:4]))
            ohv = oh.rearrange("p (s e) -> p s e", e=E)
            then(dve.tensor_tensor(ohv, cc("iota", 0, TT)[:, None, :].to_broadcast([TT, n12, E]),
                                   ixf[:, :, None].to_broadcast([TT, n12, E]), ALU.is_equal))
            then(dve.tensor_reduce(msk, oh.rearrange("p (i k e) -> p i e k", i=NT, k=TK), AX, ALU.add), "mask")
            dve.wait_ge(S["tope"], 1)
            sm = rt[:, 220:223]
            then(dve.tensor_reduce(sm, ex, AX, ALU.add))
            then(dve.reciprocal(sm, sm))
            then(dve.tensor_tensor(pay[:, :, 2].bitcast(F32).rearrange("p (i k) -> p i k", i=NT), ex,
                                   sm[:, :, None].to_broadcast([TT, NT, TK]), ALU.mult), "pay_g")
            dve.wait_ge(S["posd"], 1)
            ohp = oht.rearrange("p (i k e) -> p i k e", i=NT, k=TK)
            posb = ps[0:TT, 6, 0:96].rearrange("p (i e) -> p i e", i=NT)[:, :, None, :].to_broadcast([TT, NT, TK, E])
            then(dve.tensor_tensor(ohp, oh.rearrange("p (i k e) -> p i k e", i=NT, k=TK), posb, ALU.mult))
            then(dve.tensor_reduce(posk, oht.rearrange("p (s e) -> p s e", e=E), AX, ALU.add))
            cnt, ext, incl, bm = (rt[:, 64 + 24 * 0:96], rt[:, 96:128], rt[:, 128:160], oht[:, 0:E])
            then(dve.tensor_copy(cnt, ps[0:TT, 6, 96:128]))
            then(dve.tensor_scalar(ext, cnt, float(CAP), None, ALU.is_gt))
            then(dve.tensor_scalar(cch, posk, float(CAP), None, ALU.is_ge))
            for j in range(2, -(-T // CAP)):
                then(dve.scalar_tensor_tensor(out=ext, in0=cnt, scalar=float(CAP * j), in1=ext,
                                              op0=ALU.is_gt, op1=ALU.add))
                then(dve.scalar_tensor_tensor(out=cch, in0=posk, scalar=float(CAP * j), in1=cch,
                                              op0=ALU.is_ge, op1=ALU.add))
            then(dve.tensor_tensor_scan(incl, ext, ext, 0.0, ALU.add, ALU.bypass))
            then(dve.scalar_tensor_tensor(out=bm, in0=incl, scalar=float(E - 1), in1=ext,
                                          op0=ALU.add, op1=ALU.subtract))
            then(dve.tensor_tensor(bm, bm, cc("iota", 0, TT), ALU.subtract))
            then(dve.tensor_tensor(ohv, ohv, bm[:, None, :].to_broadcast([TT, n12, E]), ALU.mult))
            then(dve.tensor_reduce(bk, ohv, AX, ALU.add))
            then(dve.scalar_tensor_tensor(out=bk, in0=cch, scalar=1.0, in1=bk, op0=ALU.is_ge, op1=ALU.mult))
            then(dve.tensor_tensor(bk, bk, ixf, ALU.add))
            then(dve.tensor_tensor(bk, bk, cch, ALU.add))
            then(dve.scalar_tensor_tensor(out=row, in0=cch, scalar=-float(CAP), in1=posk, op0=ALU.mult, op1=ALU.add))
            then(dve.scalar_tensor_tensor(out=row, in0=row, scalar=float(ITEMS), in1=bk, op0=ALU.mult, op1=ALU.add))
            then(dve.tensor_copy(rowi[:, :], row), "rows")
            le = oh[0:1, 0:N_OVER * 16]
            ov = rt[0:1, 0:1 + N_OVER]
            for h in range(2):
                lev = oh[0:1, 0:8 * E].rearrange("p (m e) -> p m e", e=E)
                then(dve.tensor_tensor(lev, incl[0:1, None, :].to_broadcast([1, 8, E]),
                                       cc("iota", 0, 1)[:, 8 * h:8 * h + 8, None].to_broadcast([1, 8, E]), ALU.is_le))
                then(dve.tensor_reduce(ov[:, 1 + 8 * h:9 + 8 * h], lev, AX, ALU.add))
            then(dve.tensor_copy(ov[:, 0:1], incl[0:1, E - 1:E]))
            then(dve.tensor_scalar(ov[:, 1:], ov[:, 1:], float(E - 1), None, ALU.min))
            then(dve.tensor_copy(ovi[:, :], ov), "ovd")
            dve.wait_ge(s_meta, 32)
            then(dve.tensor_scalar(meta[64:128, :, 1], meta[64:128, :, 1], 1, None, ALU.add), "metaok")

            def item(q):
                gu = ps[:, 1:3, :].rearrange("p n c -> p (n c)")
                dve.wait_ge(m_gu, q + 1)
                dve.tensor_scalar(g_sb, gu[:, 0::2], LIMIT, None, ALU.min).then_inc(m_g, 1)
                dve.tensor_scalar(up_sb, gu[:, 1::2], LIMIT, -LIMIT, ALU.min, ALU.max).then_inc(s_dve, 1)
                dve.wait_ge(m_g, q + 1)
                dve.wait_ge(s_dve, 2 * q + (base + 1))
                dve.scalar_tensor_tensor(out=up_sb, in0=up_sb, scalar=1.0, in1=g_sb,
                                         op0=ALU.add, op1=ALU.mult).then_inc(s_dve, 1)
                dve.wait_ge(s_dve, 2 * q + (base + 2))
                dve.wait_ge(m_sig, q + 1)
                dve.tensor_tensor(act_sb, up_sb, sig_sb, ALU.mult).then_inc(m_act, 1)
                dve.wait_ge(m_y, q + 1)
                dve.wait_ge(m_six, q + 1)
                dve.tensor_scalar(y_sb, ps[:, 4, :], meta[:, bass.ds(q, 1), 2].bitcast(F32), None,
                                  ALU.mult).then_inc(m_ysb, 1)

            base = up(s_dve, 0)
            with dve.Fori(0, E) as q:
                item(q)
            n_over = dve.value_load(ovi[0:1, 0:1], min_val=0, max_val=N_OVER)
            with dve.If(n_over > 0):
                with dve.Fori(0, n_over) as m:
                    item(m + E)

        @block.tensor
        def _(pe):
            def transpose(out, in_, k):
                return pe.transpose(out, in_, ident[0:k, 0:k])

            pe.wait_ge(s_con, 16)
            pe.wait_ge(s_vrow, 16 * 14)
            for c in range(NC):
                transpose(ps[:, 6, c * N_VROWS:(c + 1) * N_VROWS], v1[:, P * c:P * c + P], N_VROWS)
            transpose(ps[:, 6, 200:202], v2, 2).then_inc(S["vec_tr"], 1)
            pe.wait_ge(S["hrow"], NT)
            for kt in range(KT):
                if kt >= 4:
                    pe.wait_ge(S["ht_cp"] if kt % 2 else S["ht_cp2"], (kt - 4) // 2 + 1)
                for i in range(NT):
                    mm = transpose(ps[:, kt % 4, TT * i:TT * i + TT], h_row[:, i, P * kt:P * kt + P], TT)
                mm.then_inc(S["ht_tr"], 1)
            pe.wait_ge(S["ht_cp"], 4)
            pe.wait_ge(S["ht_cp2"], 4)
            lhs = [w_in[:, :, 768 + P * c:768 + P * c + P] for c in range(NC)]
            lhs += [w_in[:, :, P * c:P * c + P] for c in range(NC + 2)]
            lhs += [w_in[:, :, 1280 + P * c:1280 + P * c + P] for c in range(NC)]
            loads = {0: [0], 2: [1], 4: [2], 6: [3], 8: [4], 10: [5], 12: [6]}
            for n in range(14):
                for j in loads.get(n, []):
                    pe.wait_ge(s_win[j], 16)
                if n >= 4:
                    pe.wait_ge(S["proj_cp"], n - 3)
                for kt in range(KT):
                    mm = pe.matmul(ps[:, n % 4, 0:T], lhs[n][:, kt], hT[:, kt, :], start=(kt == 0), stop=(kt == KT - 1))
                mm.then_inc(S["proj"], 1)
            pe.wait_ge(S["proj_cp"], 14)
            pe.wait_ge(s_kc, 16)
            for b in range(NS):
                mm = transpose(ps[:, b // 4, P * (b % 4):P * (b % 4) + P], kc[:, b, :], P)
            mm.then_inc(S["kc_tr"], 1)
            for n in range(2):
                transpose(ps[:, 2, P * n:P * n + P], vT[:, P * n:P * n + P], P)
            transpose(ps[0:NS, 2, 256:384], vT[:, NP_:T], P).then_inc(S["v_tr"], 1)
            pe.wait_ge(S["sqqk"], 1)
            for c in range(5):
                mm = pe.matmul(ps[:, 3 + c, 0:T], cc("blk64"), sq[:, c, :], start=True, stop=True)
            mm.then_inc(S["msqk"], 1)
            pe.wait_ge(S["kc_cp"], 1)
            pe.wait_ge(S["v_cp"], 1)
            pe.wait_ge(s_bd, 64)
            pe.wait_ge(S["conv"], 2 * NC)
            for n in range(2 * NC):
                if n >= 3:
                    pe.wait_ge(S["gate_s"], n - 2)
                pe.matmul(ps[:, n % 3, 0:T], bd[:, n % 2, n // 2, :], xc[:, n // 2, :],
                          start=True, stop=True).then_inc(S["gate"], 1)
            pe.wait_ge(S["ivqk"], 1)
            pe.wait_ge(S["qn"], 1)
            for c in range(5):
                mm = pe.matmul(ps[:, 3 + c, 0:T], cc("rot"), qk[:, c, :], start=True, stop=True)
            mm.then_inc(S["rotd"], 1)
            pe.wait_ge(S["roped"], 1)
            pe.wait_ge(S["gate_s"], 2 * NC)
            for n, w in ((1, 256), (0, 128)):
                for g in range(2):
                    for c in range(4):
                        h = 4 * g + c
                        out = ps[:, h // 2, 256 * (h % 2):256 * (h % 2) + 256] if n else ps[:, 4 + g, P * c:P * c + P]
                        mm = pe.matmul(out, qk[64 * g:64 * g + 64, c, P * n:P * n + P],
                                       qk[64 * g:64 * g + 64, 4, 0:w], start=True, stop=True)
            mm.then_inc(S["scores"], 1)
            pe.wait_ge(S["qbd_r"], 2)
            pe.matmul(ps[0:64, 7, 0:NS], qbd[:, :, :].rearrange("p b h -> p (b h)"), qk[:, 4, NP_:T],
                      start=True, stop=True)
            for b in range(NS):
                mm = pe.matmul(ps[:, 6, 8 * b:8 * b + 8], kcT[:, b, :], qbd[:, b, :], start=True, stop=True)
            mm.then_inc(S["sc_t"], 1)
            transpose(ps[:, 7, 256:384], qk[:, 4, P:NP_], P)
            transpose(ps[0:NS, 7, 384:512], qk[:, 4, NP_:T], P).then_inc(S["krow_tr"], 1)
            pe.wait_ge(S["sc_cp"], 1)
            transpose(ps[0:64, 7, 128:256], s_nT, P).then_inc(S["sc_tr"], 1)
            groups = [(0, 0, 0), (0, 0, 1), (1, 0, 0), (1, 0, 1), (1, 1, 0), (1, 1, 1)]
            pe.wait_ge(S["masked"], 1)
            for j, (n, kb, g) in enumerate(groups):
                pe.wait_ge(S["pn"], n + 1)
                for c in range(4):
                    src = p1_sb if n else p0_sb
                    mm = transpose(ps[:, j, P * c:P * c + P], src[:, 4 * g + c, P * kb:P * kb + P], P)
                mm.then_inc(S["p_tr"], 1)
            pe.wait_ge(S["s_pn"], 1)
            transpose(ps[:, 6, 0:64], s_sb[:, 0:128], 64)
            transpose(ps[0:NS, 6, 128:192], s_dg, 64).then_inc(S["s_ptr"], 1)
            pe.wait_ge(S["p_cp"], 3)
            pe.wait_ge(S["p_cp2"], 3)
            pe.wait_ge(S["s_pcp"], 1)
            pe.wait_ge(S["krow_cp"], 1)
            for n in range(2):
                for g in range(2):
                    for kb in range(n + 1):
                        j = groups.index((n, kb, g))
                        mm = pe.matmul(ps[64 * g:64 * g + 64, 6 + n, :], kv_new[:, kb, 64 * g:64 * g + 64],
                                       pT[:, j, :], start=(kb == 0), stop=(kb == n))
                mm.then_inc(S["pv"], 1)
            pe.wait_ge(s_vc, 16)
            for b in range(NS):
                r = slice(8 * b, 8 * b + 8)
                pe.matmul(ps[:, 5, r], kv_new[0:NS, 2, :], s_dT[:, r], start=True, stop=False)
                mm = pe.matmul(ps[:, 5, r], vc[:, b, :], s_pT[:, r], start=False, stop=True)
            mm.then_inc(S["s_pv"], 1)
            pe.wait_ge(S["h_last"], 1)
            for c in range(NC):
                transpose(ps[0:9, 0, P * c:P * c + P], hs[:, c, NP_ - 1:T], P)
                transpose(ps[0:3, 1, P * c:P * c + P], xe[:, c, NP_:NP_ + 3], P)
                mm = transpose(ps[0:NS, 2, P * c:P * c + P], xs[:, c, :], P)
            mm.then_inc(S["st_tr"], 1)
            for j, src in enumerate((tq, sq)):
                pe.wait_ge(S["sqg"], j + 1)
                for c in range(NC):
                    mm = pe.matmul(ps[:, 3 + j, 0:T], cc("mean512"), src[:, c, :], start=(c == 0), stop=(c == NC - 1))
                mm.then_inc(S["msg"], 1)
            pe.wait_ge(s_wout, 48)
            pe.wait_ge(S["mixed"], 2)
            pe.wait_ge(S["st_cp"], 1)
            for i in range(NT):
                for n in range(2):
                    for kt in range(KT):
                        src = oT[:, kt, :] if kt < NC else yT[:, kt - NC, :]
                        mm = pe.matmul(ps[0:TT, 2 * i + n, :], src[:, TT * i:TT * i + TT],
                                       w_out[:, kt, 512 * n:512 * n + 512], start=(kt == 0), stop=(kt == KT - 1))
                    mm.then_inc(S["outp"], 1)
            pe.wait_ge(S["xn"], NT)
            for kt in range(KT):
                if kt >= 4:
                    pe.wait_ge(S["xnt_cp"] if kt % 2 else S["xnt_cp2"], (kt - 4) // 2 + 1)
                for i in range(NT):
                    mm = transpose(ps[:, kt % 4, TT * i:TT * i + TT], h_row[:, i, P * kt:P * kt + P], TT)
                mm.then_inc(S["xnt_tr"], 1)
            pe.wait_ge(S["xnt_cp"], 4)
            pe.wait_ge(S["xnt_cp2"], 4)
            pe.wait_ge(s_misc, 16 * 12)
            for i in range(NT):
                for kt in range(KT):
                    mm = pe.matmul(ps[0:TT, 7, E * i:E * i + E], hT[:, kt, TT * i:TT * i + TT], wr[:, kt, :],
                                   start=(kt == 0), stop=(kt == KT - 1))
            mm.then_inc(S["logit"], 1)
            pe.wait_ge(S["mask"], 1)
            msk = oht[:, 0:96].rearrange("p (i e) -> p i e", i=NT)
            for i in range(NT + 1):
                for j in range(min(i + 1, NT)):
                    mm = pe.matmul(ps[0:TT, 6, E * i:E * i + E], cc("tri" if i == j else "ones", 0, TT), msk[:, j, :],
                                   start=(j == 0), stop=(j == min(i, NT - 1)))
            mm.then_inc(S["posd"], 1)

            def x_transposes(q):
                pe.wait_ge(m_xg, 16 * q + 16)
                pe.sem_inc(m_passed[0], 1)
                for kt in range(KT):
                    mm = transpose(ps[:, 0, CAP * kt:CAP * kt + CAP], xg[:, P * kt:P * kt + P], CAP)
                mm.then_inc(m_xtr, 1)

            sel = cc("sel").rearrange("p (j m) -> p j m", j=6)

            def item(q):
                pe.wait_ge(m_xT, q + 1)
                for kt in range(KT):
                    pe.wait_ge(s_slot[kt], 16 * q + 16)
                    for n in range(2):
                        for h in range(2):
                            mm = pe.matmul(ps[64 * h:64 * h + 64, 1 + n, :], xT[:, kt, :],
                                           ring[:, kt, 1024 * h + 512 * n:1024 * h + 512 * n + 512],
                                           start=(kt == 0), stop=False)
                    mm.then_inc(m_used, 1)
                pe.wait_ge(m_bgu, 16 * q + 16)
                for n in range(2):
                    for h in range(2):
                        mm = pe.matmul(ps[64 * h:64 * h + 64, 1 + n, :], sel[:, 2 * h + n, :], b_gu,
                                       start=False, stop=True)
                mm.then_inc(m_gu, 1)
                x_transposes(q + 1)
                pe.wait_ge(m_act, q + 1)
                for j in range(4):
                    mm = transpose(ps[:, 3, P * j:P * j + P], act_sb[:, P * j:P * j + P], P)
                mm.then_inc(m_atr, 1)
                pe.wait_ge(m_aT, q + 1)
                for s in range(4):
                    pe.wait_ge(s_slot[KT + s], 16 * q + 16)
                    for t in range(2):
                        h, j = divmod(2 * s + t, 4)
                        for n in range(2):
                            mm = pe.matmul(ps[64 * n:64 * n + 64, 4, :], actT[:, j, 64 * h:64 * h + 64],
                                           ring[:, KT + s, 1024 * t + 512 * n:1024 * t + 512 * n + 512],
                                           start=(s == 0 and t == 0), stop=False)
                    mm.then_inc(m_used, 1)
                pe.wait_ge(m_bdn, 16 * q + 16)
                for n in range(2):
                    mm = pe.matmul(ps[64 * n:64 * n + 64, 4, :], sel[:, n, :], b_dn, start=False, stop=True)
                mm.then_inc(m_y, 1)

            x_transposes(0)
            with pe.Fori(0, E) as q:
                item(q)
            pe.wait_ge(S["ovd"], 1)
            n_over = pe.value_load(ovi[0:1, 0:1], min_val=0, max_val=N_OVER)
            with pe.If(n_over > 0):
                with pe.Fori(0, n_over) as m:
                    item(m + E)


def constants(np):
    c = {n: np.zeros((P, w), np.float32) for n, w in CONST_SIZES}
    i = np.arange(P)
    c["ident"][i, i] = 1
    c["blk64"][:] = (i[:, None] // HD == i[None, :] // HD) / np.float32(HD)
    c["mean512"][:] = 1.0 / DG
    for g in (0, HD):
        for d in range(8):
            c["rot"][g + d + 8, g + d] = -1
            c["rot"][g + d, g + d + 8] = 1
    pos = np.concatenate([np.arange(NP_), np.full(NS, 1024)]).astype(np.float32)
    inv_f = np.float32(500000.0) ** (-np.arange(0, 16, 2, dtype=np.float32) / np.float32(16))
    ang = (pos[:, None] * inv_f[None, :]).astype(np.float32)
    c["cos"][:] = 1
    for g in (0, HD):
        for b in (0, 8):
            c["cos"][g + b:g + b + 8] = np.cos(ang).T
            c["sin"][g + b:g + b + 8] = np.sin(ang).T
    c["mask"][:, 0:P] = np.where(i[None, :] >= i[:, None], 0, -1e30)
    c["mask"][:, P:] = np.where(i[None, :] <= i[:, None], 0, -1e30)
    c["iota"][:] = np.arange(E)
    c["tri"][:] = i[:, None] < np.arange(TT)[None, :]
    c["ones"][:] = 1
    c["diag"][:] = (i[:, None] // 8) == np.arange(NS)[None, :]
    for j in range(6):
        c["sel"][j, 64 * j:64 * j + 64] = 1
    con = np.concatenate([c[n] for n, _ in CONST_SIZES], axis=1)
    tok = np.arange(NT)[None, :, None] * TT + np.arange(TT)[:, None, None] + np.zeros((1, 1, TK), int)
    slots = np.stack([tok, 2 * tok], axis=-1).reshape(TT, -1).astype(np.int32)
    empty = np.full((CAP * ITEMS, 3), BIG, np.int32)
    return {"const": con, "slots": slots, "empty": empty}


_INS = ["x_prompt", "x_sample", "cache_k", "cache_v", "state_conv", "state_h", "g_mix_norm", "w_in", "g_q_norm",
        "g_k_norm", "attn_sinks", "conv_w", "conv_b", "w_lru_a", "b_lru_a", "w_lru_x", "b_lru_x", "lru_lambda",
        "g_attn_out", "g_rnn_out", "w_out", "g_ffn_norm", "w_router", "b_router", "w_gate_up", "b_gate_up",
        "w_down", "b_down"]
_OUTS = [("y_prompt", (1, 256, 1024)), ("y_sample", (8, 1, 1024)),
         ("new_k_prompt", (1, 1, 128, 2, 64)), ("new_v_prompt", (1, 1, 128, 2, 64)),
         ("new_conv_prompt", (1, 1, 3, 512)), ("new_h_prompt", (1, 1, 512)),
         ("new_k_sample", (1, 8, 128, 2, 64)), ("new_v_sample", (1, 8, 128, 2, 64)),
         ("new_conv_sample", (1, 8, 3, 512)), ("new_h_sample", (1, 8, 512))]


def kernel(**inputs):
    import numpy as _np
    import concourse.bacc as _bacc
    from concourse import mybir as _mybir
    from concourse.bass_utils import run_bass_kernel_spmd as _run

    nc = _bacc.Bacc("TRN2", target_bir_lowering=False, num_devices=1)
    arrays, a, o = {}, {}, {}
    given = {n: _np.ascontiguousarray(inputs[n]) for n in _INS}
    given.update(constants(_np))
    for name, v in given.items():
        arrays[f"in_{name}_dram"] = v
        a[name] = nc.dram_tensor(f"in_{name}_dram", v.shape, _mybir.dt.from_np(v.dtype), kind="ExternalInput").ap()
    for name, shape in _OUTS:
        o[name] = nc.dram_tensor(f"out_{name}_dram", shape, _mybir.dt.float32, kind="ExternalOutput").ap()
    scratch = {"xn": nc.dram_tensor("xn_dram", (T, D), _mybir.dt.float32, kind="Internal").ap(),
               "acc": nc.dram_tensor("acc_dram", (T, D), _mybir.dt.float32, kind="Internal").ap(),
               "table": nc.dram_tensor("table_dram", (CAP * ITEMS, 3), _mybir.dt.int32, kind="Internal").ap()}
    hybrid_layer(nc, a, o, scratch)
    r = _run(nc, [arrays], core_ids=[0])
    return tuple(r.results[0][f"out_{name}_dram"] for name, _ in _OUTS)
```

```python
from contextlib import ExitStack

import concourse.bass as bass
from concourse import mybir

F32 = mybir.dt.float32
I32 = mybir.dt.int32
U32 = mybir.dt.uint32
ALU = mybir.AluOpType
ACT = mybir.ActivationFunctionType
AX = mybir.AxisListType.X

P = 128
D = 1024
KT = D // P
NP_ = 256
NS = 8
T = NP_ + NS
TT = 88
NT = T // TT
HD = 64
NC = 4
DG = 512
E = 32
TK = 4
FF = 1024
D_IN = 1792
CAP = 64
N_OVER = 16
ITEMS = E + N_OVER + 2
SLOTS = 12
BIG = 1 << 20
EPS = 1e-6
SCALE = HD ** -0.5
LRU_C = 8.0
LIMIT = 7.0
ALPHA = 1.702

CONST_SIZES = [("ident", 128), ("blk64", 128), ("mean512", 128), ("rot", 128), ("cos", T), ("sin", T),
               ("mask", 256), ("iota", E), ("tri", TT), ("ones", TT), ("diag", NS), ("sel", 6 * 64)]
COFF = {}
_at = 0
for _n, _w in CONST_SIZES:
    COFF[_n] = (_at, _at + _w)
    _at += _w
NCONST = _at

R_CONV, R_H0, R_CW, R_CB, R_BA, R_BX, R_LAM, R_GR, R_GA, N_VROWS = 0, 24, 32, 36, 37, 38, 39, 40, 41, 42


def hybrid_layer(nc, a, o, scratch):
    ctx = ExitStack()
    with ctx:
        def sb(name, shape, dt=F32):
            return ctx.enter_context(nc.sbuf_tensor(name, shape, dt))

        def sem(name):
            return ctx.enter_context(nc.semaphore(name))

        ring = sb("ring", [P, SLOTS, 2 * FF])
        regA = sb("regA", [P, KT * D_IN])
        con = sb("con", [P, NCONST])
        x_row = sb("x_row", [P, NT, D])
        hT_t = sb("hT_t", [P, KT * T])
        qk = sb("qk", [P, 5, T])
        vT = sb("vT", [P, T])
        xe = sb("xe", [P, NC, 3 + NP_])
        xs = sb("xs", [P, NC, NS])
        yT = sb("yT", [P, NC, T])
        xc = sb("xc", [P, NC, T])
        bd = sb("bd", [P, 2, NC, P])
        vec = sb("vec", [P, NC, N_VROWS])
        vgq = sb("vgq", [P, 2])
        small = sb("small", [P, 64])
        smx = sb("smx", [P, 4, 16])
        kv_new = sb("kv_new", [P, 3, P])
        meta = sb("meta", [P, ITEMS, 3], I32)
        pay = sb("pay", [TT, NT * TK, 3], I32)
        rowi = sb("rowi", [TT, NT * TK], I32)
        ovi = sb("ovi", [1, 1 + N_OVER], I32)
        brt = sb("brt", [TT, E])
        wr = sb("wr", [P, KT, E])
        sink_p = sb("sink_p", [P, 8])
        sink_s = sb("sink_s", [64, 1])
        qbd = sb("qbd", [P, NS, 8])

        ps = ctx.enter_context(nc.psum_tensor("ps", [P, 8, 512], F32))

        def cc(name, p0=0, p1=P):
            return con[p0:p1, COFF[name][0]:COFF[name][1]]

        ident = cc("ident")
        w_in = regA[:, :].rearrange("p (k n) -> p k n", k=KT)
        w_out = regA[:, 0:KT * D].rearrange("p (k n) -> p k n", k=KT)

        def whole(kt):
            return w_in[:, kt, 0:NC * T].rearrange("p (c t) -> p c t", c=NC)

        rT = whole(5)
        uT = whole(6)
        hs = whole(7)
        tq = w_in[:, 4:8, NC * T:NC * T + T]
        k_rows = w_in[:, 4:6, 5 * T:5 * T + P]
        xg = regA[0:CAP, 0:1024]
        xT = regA[:, 1024:1536].rearrange("p (k t) -> p k t", k=KT)
        b_gu = regA[:, 1536:2048]
        b_dn = regA[:, 2048:2560]
        g_sb = regA[:, 2560:3072]
        up_sb = regA[:, 3072:3584]
        sig_sb = regA[:, 3584:4096]
        act_sb = regA[:, 4096:4608]
        actT = regA[:, 4608:5120].rearrange("p (j t) -> p j t", j=4)
        y_sb = regA[:, 5120:5632]
        gix = regA[:, 5632:5633].bitcast(I32)
        six = regA[:, 5634:5635].bitcast(I32)
        scr = ring[:, 8:12, :].rearrange("p s n -> p (s n)")
        h_row = scr[0:TT, 0:3072].rearrange("p (i n) -> p i n", i=NT)
        g_bc = scr[0:TT, 3072:4096]
        v1 = scr[0:N_VROWS, 4096:4608]
        v2 = scr[0:2, 4608:4736]
        sqq = scr[:, 0:5 * T].rearrange("p (c t) -> p c t", c=5)
        rs_t = scr[:, 0:2 * T].rearrange("p (c t) -> p c t", c=2)
        sq = scr[:, 1024:1024 + NC * T].rearrange("p (c t) -> p c t", c=NC)
        p1_sb = scr[:, 0:2048].rearrange("p (h k) -> p h k", h=8)
        p0_sb = scr[:, 2048:3072].rearrange("p (h k) -> p h k", h=8)
        pT = scr[:, 3072:6144].rearrange("p (g n) -> p g n", g=6)
        kc = scr[:, 6144:7168].rearrange("p (b n) -> p b n", b=NS)
        vc = scr[:, 7168:8192].rearrange("p (b n) -> p b n", b=NS)
        gf_bc = scr[0:TT, 3072:4096]
        hT = hT_t[:, :].rearrange("p (k t) -> p k t", k=KT)
        kcT = kc
        oT = hT_t[:, 1024:2080].rearrange("p (c t) -> p c t", c=NC)
        s_sb = scr[0:64, 6144:6273]
        s_nT = scr[:, 6280:6344]
        s_pT = scr[:, 6344:6408]
        s_dT = scr[0:NS, 6408:6472]
        s_dg = scr[0:64, 6472:6480]
        bdf = bd[:, :, :, :].rearrange("p a c n -> p (a c n)")
        oh = bdf[0:TT, 0:384]
        oht = bdf[0:TT, 384:768]
        rt = bdf[0:TT, 768:1024]

        sinkT = small[:, 0:8]

        s_x, s_con, s_vrow, s_gm, s_kc, s_vc, s_bd, s_misc, s_wout, s_gf = map(
            sem, ("x_landed", "const_landed", "vrows_landed", "gmix_landed", "kcache_landed", "vcache_landed",
                  "gatew_landed", "misc_landed", "wout_landed", "gffn_landed"))
        s_win = [sem(f"win_landed{j}") for j in range(7)]
        s_slot = [sem(f"slot_landed{j}") for j in range(SLOTS)]
        s_empty = sem("table_emptied")
        s_zero = sem("zeroed")
        s_dve, s_act, s_pool = sem("dve_step"), sem("act_step"), sem("pool_step")
        names = ("ss_x", "ms_x", "rstd_x", "hrow", "ht_tr", "ht_cp", "ht_cp2", "vec_tr", "vec_cp", "proj", "proj_cp", "y_cp", "bhalf", "gelu",
                 "kc_tr", "kc_cp", "v_tr", "v_cp", "sqqk", "msqk", "ivqk", "rsqk", "qn", "rotd", "roped",
                 "conv", "lamabs", "lamexp", "sp", "gate", "gate_s", "av", "u2", "us", "rnn", "sqg", "msg", "ivg",
                 "rsg", "mixed", "scores", "masked", "neg_m", "exps", "pn", "p_tr", "p_cp", "p_cp2", "pv", "o_cp", "qbd_r",
                 "sc_t", "sc_cp", "sc_tr", "s_neg", "s_exp", "s_pn", "s_ptr", "s_pcp", "s_pv", "s_ocp",
                 "h_last", "krow_cp", "st_tr", "st_cp", "outp", "xmid", "ss_f", "ms_f", "rstd_f", "xn",
                 "xnt_tr", "xnt_cp", "xnt_cp2", "logit", "topd", "tope", "mask", "posd", "rows", "ovd", "metaok", "pay_g")
        S = {n: sem(n) for n in names}
        s_kout, s_xnd, s_tab, s_meta, s_base, s_stout = map(
            sem, ("kv_stored", "xn_stored", "table_scattered", "meta_landed", "base_stored", "states_stored"))
        m_used, m_gu, m_g, m_sig, m_act, m_atr, m_aT, m_y, m_ysb, m_xtr, m_xT = map(
            sem, ("slot_used", "gateup_done", "g_done", "sigmoid_done", "act_done", "act_transposed", "actT_copied",
                  "down_done", "y_scaled", "x_transposed", "xT_copied"))
        m_bgu, m_bdn, m_gix, m_six, m_xg, m_add, s_out = map(
            sem, ("gu_bias_landed", "dn_bias_landed", "gather_index_set", "scatter_index_set", "x_gathered",
                  "results_added", "outputs_stored"))

        m_passed = [sem("pe_waits_passed"), sem("pool_waits_passed")]

        w_gu = a["w_gate_up"].rearrange("l e k n -> (l e k) n")
        w_dn = a["w_down"].rearrange("l e k n -> (l e k) n")
        bgu_v = a["b_gate_up"].rearrange("l e (j n) -> (l e j) n", n=512)
        bdn_v = a["b_down"].rearrange("l e (j n) -> (l e j) n", n=512)
        xn_d, acc_d, tab_d = scratch["xn"], scratch["acc"], scratch["table"]

        PBANK = [n % 2 for n in range(11)] + [0, 6, 7]

        block = ctx.enter_context(nc.Block())

        def counter():
            n = {}

            def up(s, k=1):
                n[s.name] = n.get(s.name, 0) + k
                return n[s.name]
            return up

        @block.sync
        def _(sp):
            xp = a["x_prompt"].rearrange("b t d -> (b t) d")
            xsm = a["x_sample"].rearrange("b t d -> (b t) d")
            sp.dma_start(x_row[0:TT, 0:2, :], xp[0:2 * TT, :].rearrange("(i p) d -> p i d", p=TT)).then_inc(s_x, 16)
            sp.dma_start(x_row[0:NP_ - 2 * TT, 2, :], xp[2 * TT:NP_, :]).then_inc(s_x, 16)
            sp.dma_start(x_row[NP_ - 2 * TT:TT, 2, :], xsm).then_inc(s_x, 16)
            sp.dma_start(con[:, :], a["const"][:, :]).then_inc(s_con, 16)
            for j, c0 in enumerate((0, 256, 512, 768, 1024, 1280, 1536)):
                sp.dma_start(w_in[:, :, c0:c0 + 256],
                             a["w_in"][0, :, c0:c0 + 256].rearrange("(k p) n -> p k n", p=P)).then_inc(s_win[j], 16)

            def load_slot(s, e):
                if s < KT:
                    src = w_gu[bass.ds(e * D + s * P, P), :]
                    dst = ring[:, s, :]
                else:
                    src = w_dn[bass.ds(e * FF + (s - KT) * 2 * P, 2 * P), :].rearrange("(t p) n -> p t n", p=P)
                    dst = ring[:, s, :].rearrange("p (t n) -> p t n", t=2)
                sp.dma_start(dst, src).then_inc(s_slot[s], 16)

            sp.wait_ge(s_vrow, 16 * 14)
            for s in range(KT):
                load_slot(s, 0)
            sp.wait_ge(S["proj"], 14)
            for g in range(2):
                sp.dma_start(w_out[64 * g:64 * g + 64, 0:NC, :],
                             a["w_out"][0, 256 * g:256 * g + 256, :].rearrange("(c d) n -> d c n", d=HD)
                             ).then_inc(s_wout, 16)
            sp.dma_start(w_out[:, NC:KT, :],
                         a["w_out"][0, DG:D, :].rearrange("(c p) n -> p c n", p=P)).then_inc(s_wout, 16)
            sp.wait_ge(S["pv"], 2)
            sp.dma_start(gf_bc, a["g_ffn_norm"].to_broadcast([TT, D])).then_inc(s_gf, 16)
            sp.wait_ge(S["xmid"], 2 * NT)
            sp.dma_start(acc_d[:, :].rearrange("(i p) d -> p i d", p=TT), x_row[0:TT, :, :]).then_inc(s_base, 16)
            sp.wait_ge(S["xn"], NT)
            sp.dma_start(xn_d[:, :].rearrange("(i p) d -> p i d", p=TT), h_row[:, :, :]).then_inc(s_xnd, 16)
            sp.wait_ge(s_xnd, 16)
            sp.wait_ge(s_stout, 16 * 4)
            sp.wait_ge(S["xnt_tr"], KT)
            for s in range(KT, SLOTS):
                load_slot(s, 0)
            sp.wait_ge(s_tab, 16 * NT * TK)
            for g in range(2):
                sp.dma_start(meta[64 * g:64 * g + 64, :, :],
                             tab_d[:, :].rearrange("(p i) f -> p i f", p=CAP)).then_inc(s_meta, 16)

            def load_item(q, e):
                for s in range(SLOTS):
                    sp.wait_ge(m_used, q * SLOTS - (SLOTS - 1 - s))
                    load_slot(s, e)

            with sp.Fori(1, E) as q:
                load_item(q, q)
            sp.wait_ge(S["ovd"], 1)
            n_over = sp.value_load(ovi[0:1, 0:1], min_val=0, max_val=N_OVER)
            with sp.If(n_over > 0):
                with sp.Fori(0, n_over) as m:
                    e = sp.value_load(ovi[0:1, bass.ds(m + 1, 1)], min_val=0, max_val=E - 1)
                    load_item(m + E, e)
            sp.wait_ge(s_kout, 16 * 7)
            sp.wait_ge(s_stout, 16 * 4)

        @block.gpsimd
        def _(pool):
            for t in (xe[:, :, 0:3], bd[:, :, :, :], qbd[:, :, :]):
                pool.memset(t, 0).then_inc(s_zero, 1)
            pool.wait_ge(s_zero, 2)
            for n, w in enumerate((a["w_lru_a"], a["w_lru_x"])):
                for j in range(2):
                    pool.dma_start(bd[64 * j:64 * j + 64, n, :, 64 * j:64 * j + 64],
                                   w[0].rearrange("(c j) i o -> j i c o", j=2)[j]).then_inc(s_bd, 16)
            pool.dma_start(kc[:, :, :], a["cache_k"][0].rearrange("b w k d -> w b (k d)")).then_inc(s_kc, 16)
            pool.dma_start(vc[:, :, :], a["cache_v"][0].rearrange("b w k d -> w b (k d)")).then_inc(s_vc, 16)
            pool.dma_start(wr[:, :, :], a["w_router"][0].rearrange("(k p) n -> p k n", p=P)).then_inc(s_misc, 16)
            pool.dma_start(brt[:, :], a["b_router"].to_broadcast([TT, E])).then_inc(s_misc, 16)
            pool.dma_start(sink_p[:, :], a["attn_sinks"].to_broadcast([P, 8])).then_inc(s_misc, 16)
            for b in range(NS):
                pool.dma_start(sink_s[8 * b:8 * b + 8, :],
                               a["attn_sinks"].rearrange("l h -> h l")).then_inc(s_misc, 16)
            pool.dma_start(pay[:, :, 0:2], a["slots"][:, :].rearrange("p (s f) -> p s f", f=2)).then_inc(s_misc, 16)
            pool.dma_start(tab_d[:, :], a["empty"][:, :]).then_inc(s_empty, 16)
            for name in "kv":
                pool.dma_start(o[f"new_{name}_sample"][0, :, 0:127].rearrange("b w k d -> b (w k d)"),
                               a[f"cache_{name}"][0, :, 1:128].rearrange("b w k d -> b (w k d)")
                               ).then_inc(s_kout, 16)
            pool.dma_start(o["new_conv_sample"][0, :, 0:2, :].rearrange("b j c -> b (j c)"),
                           a["state_conv"][0, :, 1:3, :].rearrange("b j c -> b (j c)")).then_inc(s_kout, 16)
            pool.wait_ge(S["v_cp"], 1)
            pool.dma_start(o["new_v_prompt"][0, 0].rearrange("w k d -> w (k d)"), kv_new[:, 1, :]).then_inc(s_kout, 16)
            pool.dma_start(o["new_v_sample"][0, :, 127].rearrange("b k d -> b (k d)"),
                           kv_new[0:NS, 2, :]).then_inc(s_kout, 16)
            pool.wait_ge(S["krow_cp"], 1)
            pool.dma_start(o["new_k_prompt"][0, 0].rearrange("w k d -> w (k d)"), k_rows[:, 0, :]).then_inc(s_kout, 16)
            pool.dma_start(o["new_k_sample"][0, :, 127].rearrange("b k d -> b (k d)"),
                           k_rows[0:NS, 1, :]).then_inc(s_kout, 16)

            pool.wait_ge(S["outp"], 2 * NT)
            for n, t in enumerate((b_gu, b_dn, xg)):
                pool.memset(t, 0.0).then_inc(s_zero, 1)
            pool.wait_ge(S["rows"], 1)
            pool.wait_ge(S["pay_g"], 1)
            pool.wait_ge(s_empty, 16)
            for s in range(NT * TK):
                pool.indirect_dma_start(tab_d[:, :],
                                        bass.IndirectOffsetOnAxis(ap=rowi[:, s:s + 1].bitcast(U32), axis=0),
                                        pay[:, s, :], None, bounds_check=CAP * ITEMS - 1,
                                        oob_is_err=False).then_inc(s_tab, 16)

            def gather(q):
                pool.tensor_copy(gix[0:CAP, :], meta[0:CAP, bass.ds(q, 1), 0]).then_inc(m_gix, 1)
                pool.wait_ge(m_gix, q + 1)
                pool.sem_inc(m_passed[1], 1)
                pool.indirect_dma_start(xg, None, xn_d[:, :],
                                        bass.IndirectOffsetOnAxis(ap=gix[0:CAP, 0:1].bitcast(U32), axis=0),
                                        bounds_check=T - 1, oob_is_err=False).then_inc(m_xg, 16)

            pool.wait_ge(S["metaok"], 1)
            pool.wait_ge(s_zero, 6)
            pool.wait_ge(s_xnd, 16)
            gather(0)
            pool.wait_ge(m_xg, 16)
            pool.wait_ge(m_xtr, 1)
            gather(1)
            pool.wait_ge(s_base, 16)

            halves = acc_d[:, :].rearrange("t (h d) -> (t h) d", h=2)

            def item(q):
                pool.tensor_copy(six, meta[:, bass.ds(q, 1), 1]).then_inc(m_six, 1)
                pool.wait_ge(m_xg, 16 * q + 32)
                pool.wait_ge(m_xtr, q + 2)
                gather(q + 2)
                pool.wait_ge(m_six, q + 1)
                pool.wait_ge(m_ysb, q + 1)
                pool.sem_inc(m_passed[1], 1)
                pool.indirect_dma_start(halves, bass.IndirectOffsetOnAxis(ap=six.bitcast(U32), axis=0),
                                        y_sb, None, bounds_check=2 * T - 1, oob_is_err=False,
                                        compute_op=ALU.add).then_inc(m_add, 16)
                pool.wait_ge(m_add, 16 * q + 16)

            with pool.Fori(0, E) as q:
                item(q)
            n_over = pool.value_load(ovi[0:1, 0:1], min_val=0, max_val=N_OVER)
            with pool.If(n_over > 0):
                with pool.Fori(0, n_over) as m:
                    item(m + E)
            pool.wait_ge(m_xg, 16 * E + 32 + 16 * n_over)
            pool.sem_inc(m_passed[1], 1)
            pool.dma_start(o["y_prompt"][0], acc_d[0:NP_, :]).then_inc(s_out, 16)
            pool.dma_start(o["y_sample"].rearrange("b t d -> (b t) d"), acc_d[NP_:T, :]).then_inc(s_out, 16)
            pool.wait_ge(s_out, 32)

        @block.scalar
        def _(act):
            up = counter()

            def then(ins, name=None):
                s = S[name] if name else s_act
                n = up(s)
                ins.then_inc(s, 1)
                act.wait_ge(s, n)

            act.dma_start(g_bc, a["g_mix_norm"].to_broadcast([TT, D])).then_inc(s_gm, 16)
            r = v1
            act.dma_start(r[R_CONV:R_CONV + 24, :], a["state_conv"][0].rearrange("b j c -> (b j) c")
                          ).then_inc(s_vrow, 16)
            act.dma_start(r[R_H0:R_H0 + NS, :], a["state_h"][0]).then_inc(s_vrow, 16)
            act.dma_start(r[R_CW:R_CW + 4, :], a["conv_w"][0]).then_inc(s_vrow, 16)
            act.dma_start(r[R_CB:R_CB + 1, :], a["conv_b"]).then_inc(s_vrow, 16)
            act.dma_start(r[R_BA:R_BA + 1, :], a["b_lru_a"].rearrange("l n c -> l (n c)")).then_inc(s_vrow, 16)
            act.dma_start(r[R_BX:R_BX + 1, :], a["b_lru_x"].rearrange("l n c -> l (n c)")).then_inc(s_vrow, 16)
            act.dma_start(r[R_LAM:R_LAM + 1, :], a["lru_lambda"]).then_inc(s_vrow, 16)
            act.dma_start(r[R_GR:R_GR + 1, :], a["g_rnn_out"]).then_inc(s_vrow, 16)
            for g in range(2):
                act.dma_start(r[R_GA:R_GA + 1, :].rearrange("p (c g d) -> p g c d", g=2, d=HD)[:, g],
                              a["g_attn_out"].rearrange("l (g c d) -> l g c d", g=2, d=HD)[:, g]
                              ).then_inc(s_vrow, 16)
                for n, w in enumerate((a["g_q_norm"], a["g_k_norm"])):
                    act.dma_start(v2[n:n + 1, 64 * g:64 * g + 64], w).then_inc(s_vrow, 16)
            act.wait_ge(s_x, 48)
            for i in range(NT):
                then(act.activation(h_row[:, i, :], x_row[0:TT, i, :], ACT.Square,
                                    accum_out=small[0:TT, i:i + 1]), "ss_x")
            act.wait_ge(S["ms_x"], 1)
            then(act.activation(small[0:TT, 8:11], small[0:TT, 4:7], ACT.Sqrt), "rstd_x")
            for kt in range(1, KT, 2):
                act.wait_ge(S["ht_tr"], kt + 1)
                then(act.activation(hT[:, kt, :], ps[:, kt % 4, 0:T], ACT.Copy), "ht_cp")

            def evacuate(n):
                act.wait_ge(S["proj"], n + 1)
                src = ps[:, PBANK[n], 0:T]
                if n < 4:
                    for h in (2 * n, 2 * n + 1):
                        g, p0 = h // 4, 64 * (h % 2)
                        then(act.activation(qk[64 * g:64 * g + 64, h % 4, :], src[p0:p0 + 64], ACT.Copy),
                             "proj_cp" if h % 2 else None)
                elif n == 4:
                    then(act.activation(qk[:, 4, :], src, ACT.Copy), "proj_cp")
                elif n == 5:
                    then(act.activation(vT[:, :], src, ACT.Copy), "proj_cp")
                else:
                    if n == 6:
                        act.wait_ge(s_zero, 1)
                    then(act.activation(xs[:, n - 6, :], src[:, NP_:T], ACT.Copy))
                    then(act.activation(xe[:, n - 6, 3:3 + NP_], src[:, 0:NP_], ACT.Copy), "proj_cp")

            evacuate(0)
            evacuate(1)
            act.wait_ge(S["vec_tr"], 1)
            then(act.activation(vec[:, :, :], ps[:, 6, 0:NC * N_VROWS].rearrange("p (c r) -> p c r", c=NC), ACT.Copy))
            then(act.activation(vgq[:, :], ps[:, 6, 200:202], ACT.Copy), "vec_cp")
            for n in range(2, 5):
                evacuate(n)
            then(act.activation(sqq[:, :, :], qk[:, :, :], ACT.Square), "sqqk")
            evacuate(5)
            act.wait_ge(S["lamabs"], 1)
            then(act.activation(small[:, 20:24], small[:, 16:20], ACT.Exp, scale=-1.0), "lamexp")
            act.wait_ge(S["kc_tr"], 1)
            then(act.activation(kcT[:, 0:4, :], ps[:, 2, :].rearrange("p (b n) -> p b n", b=4), ACT.Copy), "kc_cp")
            evacuate(6)
            act.wait_ge(S["kc_tr"], 2)
            then(act.activation(kcT[:, 4:8, :], ps[:, 2, :].rearrange("p (b n) -> p b n", b=4), ACT.Copy), "kc_cp")
            evacuate(7)
            act.wait_ge(S["v_tr"], 1)
            then(act.activation(kv_new[:, 0:2, :], ps[:, 2, 0:256].rearrange("p (b n) -> p b n", b=2), ACT.Copy))
            then(act.activation(kv_new[0:NS, 2, :], ps[0:NS, 2, 256:384], ACT.Copy), "v_cp")
            evacuate(8)
            act.wait_ge(S["ivqk"], 1)
            then(act.activation(sqq[:, :, :], sqq[:, :, :], ACT.Sqrt), "rsqk")
            evacuate(9)
            act.wait_ge(S["sc_t"], 1)
            then(act.activation(s_nT[:, :], ps[:, 1, 0:64], ACT.Copy), "sc_cp")

            def gate(n):
                c, x = n // 2, n % 2
                act.wait_ge(S["gate"], n + 1)
                then(act.activation((uT if x else rT)[:, c, :], ps[:, 2 + n % 4, 0:T], ACT.Tanh, scale=0.5,
                                    bias=small[:, 56 + 4 * x + c:57 + 4 * x + c]), "gate_s")

            act.wait_ge(S["bhalf"], 1)
            for n in range(4):
                gate(n)
            act.wait_ge(S["neg_m"], 1)
            for n, pt in ((1, p1_sb), (0, p0_sb)):
                for h in range(8):
                    act.activation(pt[:, h, :], pt[:, h, :], ACT.Exp, scale=SCALE,
                                   bias=smx[:, 1, 8 * n + h:8 * n + h + 1],
                                   accum_out=smx[:, 2, 8 * n + h:8 * n + h + 1]).then_inc(s_act, 1)
                    up(s_act)
            then(act.activation(smx[:, 3, :], smx[:, 3, :], ACT.Exp), "exps")
            act.wait_ge(S["s_neg"], 1)
            then(act.activation(s_sb[:, :], s_sb[:, :], ACT.Exp, scale=SCALE, bias=small[0:64, 33:34],
                                accum_out=small[0:64, 34:35]))
            then(act.activation(small[0:64, 35:36], sink_s[:, :], ACT.Exp, bias=small[0:64, 33:34]), "s_exp")
            for n in range(4, 2 * NC):
                gate(n)
            act.wait_ge(S["sp"], 1)
            for c in range(NC):
                then(act.activation(hs[:, c, :], rT[:, c, :], ACT.Tanh, scale=small[:, 24 + c:25 + c],
                                    bias=small[:, 24 + c:25 + c]))
                then(act.activation(rT[:, c, :], rT[:, c, :], ACT.Exp, scale=small[:, 28 + c:29 + c],
                                    bias=small[:, 28 + c:29 + c]), "av")
            for g in (0, 2, 4):
                act.wait_ge(S["p_tr"], g + 1)
                then(act.activation(pT[:, g, :], ps[:, 2 + g, :], ACT.Copy), "p_cp")
            act.wait_ge(S["s_ptr"], 1)
            then(act.activation(s_pT[:, :], ps[:, 0, 0:64], ACT.Copy))
            then(act.activation(s_dT[:, :], ps[0:NS, 0, 128:192], ACT.Copy), "s_pcp")
            then(act.activation(k_rows[:, 0, :], ps[:, 1, 256:384], ACT.Copy))
            then(act.activation(k_rows[0:NS, 1, :], ps[0:NS, 1, 384:512], ACT.Copy), "krow_cp")
            act.wait_ge(S["u2"], 1)
            then(act.activation(tq[:, :, :], tq[:, :, :], ACT.Sqrt, scale=0.25), "us")
            act.wait_ge(S["o_cp"], 3)
            then(act.activation(sq[:, 0:NC, :], oT[:, :, :], ACT.Square), "sqg")
            act.wait_ge(S["ivg"], 1)
            then(act.activation(rs_t[:, 1, :], rs_t[:, 1, :], ACT.Sqrt), "rsg")
            st = scr[0:9, 6144:7680].rearrange("p (g n) -> p g n", g=3)
            act.wait_ge(S["st_tr"], 1)
            then(act.activation(st[0:3, 1, :], ps[0:3, 7, :], ACT.Copy), "st_cp")
            act.wait_ge(S["y_cp"], 4)
            then(act.activation(yT[:, :, :], yT[:, :, :], ACT.Gelu_apprx_tanh), "gelu")
            act.wait_ge(S["st_tr"], 2)
            then(act.activation(st[0:NS, 2, :], ps[0:NS, 7, :], ACT.Copy), "st_cp")
            act.wait_ge(S["rnn"], 1)
            then(act.activation(tq[:, :, :], yT[:, :, :], ACT.Square), "sqg")
            act.wait_ge(S["ivg"], 2)
            then(act.activation(rs_t[:, 0, :], rs_t[:, 0, :], ACT.Sqrt), "rsg")
            act.wait_ge(S["st_tr"], 3)
            then(act.activation(st[0:9, 0, :], ps[0:9, 7, :], ACT.Copy), "st_cp")
            act.dma_start(o["new_h_prompt"][0], st[0:1, 0, :]).then_inc(s_stout, 16)
            act.dma_start(o["new_h_sample"][0], st[1:9, 0, :]).then_inc(s_stout, 16)
            act.dma_start(o["new_conv_prompt"][0, 0], st[0:3, 1, :]).then_inc(s_stout, 16)
            act.dma_start(o["new_conv_sample"][0, :, 2], st[0:NS, 2, :]).then_inc(s_stout, 16)
            for i in range(NT):
                act.wait_ge(S["xmid"], 2 * i + 2)
                if i == 0:
                    act.wait_ge(S["mixed"], 2)
                then(act.activation(h_row[:, i, :], x_row[0:TT, i, :], ACT.Square,
                                    accum_out=small[0:TT, 36 + i:37 + i]), "ss_f")
            act.wait_ge(S["ms_f"], 1)
            then(act.activation(small[0:TT, 40:43], small[0:TT, 40:43], ACT.Sqrt), "rstd_f")
            for kt in range(1, KT, 2):
                act.wait_ge(S["xnt_tr"], kt + 1)
                then(act.activation(hT[:, kt, :], ps[:, kt % 4, 0:T], ACT.Copy), "xnt_cp")
            act.wait_ge(S["topd"], 1)
            then(act.activation(rt[:, 48:60], rt[:, 48:60], ACT.Exp), "tope")

            def copy_x(q):
                act.wait_ge(m_xtr, q + 1)
                act.activation(xT[:, :, :], ps[:, 0, :].rearrange("p (k t) -> p k t", k=KT),
                               ACT.Copy).then_inc(m_xT, 1)

            def item(q):
                act.wait_ge(m_g, q + 1)
                act.activation(sig_sb, g_sb, ACT.Sigmoid, scale=ALPHA).then_inc(m_sig, 1)
                copy_x(q + 1)
                act.wait_ge(m_atr, q + 1)
                act.activation(actT[:, :, :], ps[:, 3, :].rearrange("p (j t) -> p j t", j=4),
                               ACT.Copy).then_inc(m_aT, 1)

            def bias_gu(q, e):
                act.dma_start(b_gu[0:4, :], bgu_v[bass.ds(e * 4, 4), :]).then_inc(m_bgu, 16)

            def bias_dn(q, e):
                act.dma_start(b_dn[0:2, :], bdn_v[bass.ds(e * 2, 2), :]).then_inc(m_bdn, 16)

            act.wait_ge(s_zero, 6)
            bias_gu(0, 0)
            bias_dn(0, 0)
            copy_x(0)

            def step(q, e_next):
                item(q)
                bias_gu(q + 1, e_next)
                act.wait_ge(m_y, q + 1)
                bias_dn(q + 1, e_next)

            with act.Fori(0, E - 1) as q:
                step(q, q + 1)
            act.wait_ge(S["ovd"], 1)
            n_over = act.value_load(ovi[0:1, 0:1], min_val=0, max_val=N_OVER)
            item(E - 1)
            with act.If(n_over > 0):
                with act.Fori(0, n_over) as m:
                    e = act.value_load(ovi[0:1, bass.ds(m + 1, 1)], min_val=0, max_val=E - 1)
                    bias_gu(m + E, e)
                    act.wait_ge(m_y, m + E)
                    bias_dn(m + E, e)
                    item(m + E)

        @block.vector
        def _(dve):
            up = counter()

            def then(ins, name=None):
                s = S[name] if name else s_dve
                n = up(s)
                ins.then_inc(s, 1)
                dve.wait_ge(s, n)

            def inv(dst, src, scale):
                then(dve.tensor_scalar(dst, src, scale, EPS, ALU.mult, ALU.add))

            dve.wait_ge(S["ss_x"], NT)
            inv(small[0:TT, 4:7], small[0:TT, 0:3], 1.0 / D)
            then(dve.reciprocal(small[0:TT, 4:7], small[0:TT, 4:7]), "ms_x")
            dve.wait_ge(S["rstd_x"], 1)
            dve.wait_ge(s_gm, 16)
            for i in range(NT):
                then(dve.scalar_tensor_tensor(out=h_row[:, i, :], in0=x_row[0:TT, i, :], scalar=small[0:TT, 8 + i:9 + i],
                                              in1=g_bc, op0=ALU.mult, op1=ALU.mult), "hrow")
            for kt in range(0, KT, 2):
                dve.wait_ge(S["ht_tr"], kt + 1)
                then(dve.tensor_copy(hT[:, kt, :], ps[:, kt % 4, 0:T]), "ht_cp2")
            dve.wait_ge(S["vec_cp"], 1)
            lam = vec[:, :, R_LAM]
            then(dve.tensor_scalar(small[:, 12:16], lam, -1.0, None, ALU.mult))
            then(dve.tensor_tensor(small[:, 16:20], lam, small[:, 12:16], ALU.max), "lamabs")
            dve.wait_ge(S["lamexp"], 1)
            z, w, w2, acc = small[:, 20:24], small[:, 44:48], small[:, 48:52], small[:, 52:56]
            then(dve.tensor_scalar(w, z, 2.0, None, ALU.add))
            then(dve.reciprocal(w, w))
            then(dve.tensor_tensor(w, w, z, ALU.mult))
            then(dve.tensor_tensor(w2, w, w, ALU.mult))
            then(dve.tensor_scalar(acc, w2, 1.0 / 17, 1.0 / 15, ALU.mult, ALU.add))
            for k in (13, 11, 9, 7, 5, 3, 1):
                then(dve.tensor_tensor(acc, acc, w2, ALU.mult))
                then(dve.tensor_scalar(acc, acc, 1.0 / k, None, ALU.add))
            then(dve.tensor_tensor(acc, acc, w, ALU.mult))
            then(dve.tensor_scalar(small[:, 12:16], small[:, 12:16], 0.0, None, ALU.max))
            then(dve.scalar_tensor_tensor(out=acc, in0=acc, scalar=2.0, in1=small[:, 12:16],
                                          op0=ALU.mult, op1=ALU.add))
            then(dve.tensor_scalar(small[:, 24:28], acc, LRU_C / 2, None, ALU.mult))
            then(dve.tensor_scalar(small[:, 28:32], acc, -LRU_C / 2, None, ALU.mult), "sp")
            then(dve.tensor_scalar(small[:, 56:60], vec[:, :, R_BA], 0.5, None, ALU.mult))
            then(dve.tensor_scalar(small[:, 60:64], vec[:, :, R_BX], 0.5, None, ALU.mult), "bhalf")

            def convolve(c):
                dve.wait_ge(S["proj_cp"], c + 7)
                for out, tap in ((xc[:, c, 0:NP_], lambda j: xe[:, c, j:j + NP_]),
                                 (xc[:, c, NP_:T], lambda j: vec[:, c, R_CONV + j:R_CONV + 24:3] if j < 3
                                  else xs[:, c, :])):
                    then(dve.tensor_scalar(out, tap(0), vec[:, c, R_CW:R_CW + 1], vec[:, c, R_CB:R_CB + 1],
                                           ALU.mult, ALU.add))
                    for j in range(1, 4):
                        then(dve.scalar_tensor_tensor(out=out, in0=tap(j), scalar=vec[:, c, R_CW + j:R_CW + j + 1],
                                                      in1=out, op0=ALU.mult, op1=ALU.add),
                             "conv" if j == 3 else None)

            def y_copy(c):
                dve.wait_ge(S["proj"], c + 11)
                then(dve.tensor_copy(yT[:, c, :], ps[:, PBANK[10 + c], 0:T]), "y_cp")

            dve.wait_ge(S["msqk"], 1)
            then(dve.tensor_scalar(sqq[:, :, :], ps[:, 3:8, 0:T], EPS, None, ALU.add))
            then(dve.reciprocal(sqq[:, :, :], sqq[:, :, :]), "ivqk")
            convolve(0)
            dve.wait_ge(S["rsqk"], 1)
            then(dve.scalar_tensor_tensor(out=qk[:, 0:4, :], in0=qk[:, 0:4, :], scalar=vgq[:, 0:1], in1=sqq[:, 0:4, :],
                                          op0=ALU.mult, op1=ALU.mult))
            then(dve.scalar_tensor_tensor(out=qk[:, 4, :], in0=qk[:, 4, :], scalar=vgq[:, 1:2], in1=sqq[:, 4, :],
                                          op0=ALU.mult, op1=ALU.mult), "qn")
            convolve(1)
            dve.wait_ge(S["rotd"], 1)
            cosb = cc("cos")[:, None, :].to_broadcast([P, 5, T])
            sinb = cc("sin")[:, None, :].to_broadcast([P, 5, T])
            then(dve.tensor_tensor(sqq[:, :, :], ps[:, 3:8, 0:T], sinb, ALU.mult))
            then(dve.tensor_tensor(qk[:, :, :], qk[:, :, :], cosb, ALU.mult))
            then(dve.tensor_tensor(qk[:, :, :], qk[:, :, :], sqq[:, :, :], ALU.add), "roped")
            y_copy(0)
            dve.wait_ge(s_zero, 3)
            for g in range(2):
                then(dve.tensor_copy(qbd[64 * g:64 * g + 64, :, 4 * g:4 * g + 4].rearrange("p b c -> p c b"),
                                     qk[64 * g:64 * g + 64, 0:4, NP_:T]), "qbd_r")
            convolve(2)
            convolve(3)

            dve.wait_ge(S["scores"], 1)
            maskb = cc("mask")[:, None, :].to_broadcast([P, 8, 256])
            then(dve.tensor_tensor(p1_sb[:, :, :], ps[:, 2:6, :].rearrange("p g (h k) -> p (g h) k", h=2),
                                   maskb, ALU.add), "masked")
            dve.wait_ge(S["scores"], 2)
            then(dve.tensor_tensor(p0_sb[:, :, :], ps[:, 6:8, :].rearrange("p g (h k) -> p (g h) k", h=4),
                                   maskb[:, :, 128:256], ALU.add), "masked")
            then(dve.tensor_reduce(smx[:, 0, 8:16], p1_sb[:, :, :], AX, ALU.max))
            then(dve.tensor_reduce(smx[:, 0, 0:8], p0_sb[:, :, :], AX, ALU.max))
            dve.wait_ge(s_misc, 16 * 12)
            sinkb = sink_p[:, None, :].to_broadcast([P, 2, 8])
            m3 = smx[:, 0, :].rearrange("p (n h) -> p n h", n=2)
            then(dve.scalar_tensor_tensor(out=m3, in0=m3, scalar=SCALE, in1=sinkb, op0=ALU.mult, op1=ALU.max))
            then(dve.tensor_tensor(smx[:, 3, :].rearrange("p (n h) -> p n h", n=2), sinkb, m3, ALU.subtract))
            then(dve.tensor_scalar(smx[:, 1, :], smx[:, 0, :], -1.0, None, ALU.mult), "neg_m")
            dve.wait_ge(S["sc_tr"], 1)
            then(dve.tensor_tensor(s_dg[:, :], ps[0:64, 1, 64:72], cc("diag", 0, 64), ALU.mult))
            then(dve.tensor_reduce(s_sb[:, 128:129], s_dg[:, :], AX, ALU.add))
            then(dve.tensor_copy(s_sb[:, 0:128], ps[0:64, 1, 128:256]))
            then(dve.tensor_reduce(small[0:64, 32:33], s_sb[:, :], AX, ALU.max))
            then(dve.scalar_tensor_tensor(out=small[0:64, 33:34], in0=small[0:64, 32:33], scalar=SCALE,
                                          in1=sink_s[:, :], op0=ALU.mult, op1=ALU.max))
            then(dve.tensor_scalar(small[0:64, 33:34], small[0:64, 33:34], -1.0, None, ALU.mult), "s_neg")
            y_copy(1)
            dve.wait_ge(S["exps"], 1)
            then(dve.tensor_tensor(smx[:, 2, :], smx[:, 2, :], smx[:, 3, :], ALU.add))
            then(dve.reciprocal(smx[:, 2, :], smx[:, 2, :]))
            for n, pt, w_ in ((0, p0_sb, 128), (1, p1_sb, 256)):
                then(dve.tensor_tensor(pt[:, :, :], pt[:, :, :],
                                       smx[:, 2, 8 * n:8 * n + 8][:, :, None].to_broadcast([P, 8, w_]), ALU.mult),
                     "pn")
            dve.wait_ge(S["s_exp"], 1)
            then(dve.tensor_tensor(small[0:64, 34:35], small[0:64, 34:35], small[0:64, 35:36], ALU.add))
            then(dve.reciprocal(small[0:64, 34:35], small[0:64, 34:35]))
            then(dve.tensor_scalar(s_sb[:, :], s_sb[:, :], small[0:64, 34:35], None, ALU.mult))
            then(dve.tensor_scalar(s_dg[:, :], cc("diag", 0, 64), s_sb[:, 128:129], None, ALU.mult), "s_pn")
            y_copy(2)
            y_copy(3)
            dve.wait_ge(S["gate_s"], 2 * NC)
            then(dve.scalar_tensor_tensor(out=uT[:, :, :], in0=uT[:, :, :], scalar=1.0, in1=xc[:, :, :],
                                          op0=ALU.add, op1=ALU.mult))
            dve.wait_ge(S["av"], NC)
            then(dve.tensor_tensor(tq[:, :, :], rT[:, :, :], rT[:, :, :], ALU.mult))
            then(dve.scalar_tensor_tensor(out=tq[:, :, :], in0=tq[:, :, :], scalar=1.0, in1=hs[:, :, :],
                                          op0=ALU.add, op1=ALU.mult), "u2")
            for g in (1, 3, 5):
                dve.wait_ge(S["p_tr"], g + 1)
                then(dve.tensor_copy(pT[:, g, :], ps[:, 2 + g, :]), "p_cp2")
            for n in range(2):
                dve.wait_ge(S["pv"], n + 1)
                then(dve.tensor_copy(oT[:, :, P * n:P * n + P],
                                     ps[:, n, :].rearrange("p (c t) -> p c t", c=NC)), "o_cp")
            dve.wait_ge(S["s_pv"], 1)
            for g in range(2):
                src = ps[64 * g:64 * g + 64, 7, 0:64].rearrange("p (b g c) -> p g c b", g=2, c=4)
                ins = dve.tensor_copy(oT[64 * g:64 * g + 64, :, NP_:T], src[:, g])
                then(ins, "o_cp" if g else None)
            dve.wait_ge(S["us"], 1)
            then(dve.tensor_tensor(uT[:, :, :], uT[:, :, :], tq[:, :, :], ALU.mult))
            for c in range(NC):
                then(dve.tensor_tensor_scan(hs[:, c, 0:NP_], rT[:, c, 0:NP_], uT[:, c, 0:NP_], 0.0,
                                            ALU.mult, ALU.add))
            dve.wait_ge(S["msg"], 1)
            then(dve.tensor_scalar(rs_t[:, 1, :], ps[:, 6, 0:T], EPS, None, ALU.add))
            then(dve.reciprocal(rs_t[:, 1, :], rs_t[:, 1, :]), "ivg")
            then(dve.tensor_tensor(hs[:, :, NP_:T], rT[:, :, NP_:T], vec[:, :, R_H0:R_H0 + NS], ALU.mult))
            then(dve.tensor_tensor(hs[:, :, NP_:T], hs[:, :, NP_:T], uT[:, :, NP_:T], ALU.add), "h_last")
            dve.wait_ge(S["rsg"], 1)
            for c in range(NC):
                then(dve.scalar_tensor_tensor(out=oT[:, c, :], in0=oT[:, c, :], scalar=vec[:, c, R_GA:R_GA + 1],
                                              in1=rs_t[:, 1, :], op0=ALU.mult, op1=ALU.mult),
                     "mixed" if c == 3 else None)
            dve.wait_ge(S["gelu"], 1)
            then(dve.tensor_tensor(yT[:, :, :], yT[:, :, :], hs[:, :, :], ALU.mult), "rnn")
            dve.wait_ge(S["msg"], 2)
            then(dve.tensor_scalar(rs_t[:, 0, :], ps[:, 6, 0:T], EPS, None, ALU.add))
            then(dve.reciprocal(rs_t[:, 0, :], rs_t[:, 0, :]), "ivg")
            dve.wait_ge(S["rsg"], 2)
            for c in range(NC):
                then(dve.scalar_tensor_tensor(out=yT[:, c, :], in0=yT[:, c, :], scalar=vec[:, c, R_GR:R_GR + 1],
                                              in1=rs_t[:, 0, :], op0=ALU.mult, op1=ALU.mult),
                     "mixed" if c == 3 else None)
            for i in range(NT):
                for n in range(2):
                    dve.wait_ge(S["outp"], 2 * i + n + 1)
                    then(dve.tensor_tensor(x_row[0:TT, i, 512 * n:512 * n + 512],
                                           x_row[0:TT, i, 512 * n:512 * n + 512],
                                           ps[0:TT, 2 * i + n, :], ALU.add), "xmid")
            dve.wait_ge(S["ss_f"], NT)
            inv(small[0:TT, 40:43], small[0:TT, 36:39], 1.0 / D)
            then(dve.reciprocal(small[0:TT, 40:43], small[0:TT, 40:43]), "ms_f")
            dve.wait_ge(S["rstd_f"], 1)
            dve.wait_ge(s_gf, 16)
            for i in range(NT):
                then(dve.scalar_tensor_tensor(out=h_row[:, i, :], in0=x_row[0:TT, i, :],
                                              scalar=small[0:TT, 40 + i:41 + i], in1=gf_bc,
                                              op0=ALU.mult, op1=ALU.mult), "xn")
            for kt in range(0, KT, 2):
                dve.wait_ge(S["xnt_tr"], kt + 1)
                then(dve.tensor_copy(hT[:, kt, :], ps[:, kt % 4, 0:T]), "xnt_cp2")

            lg = rt[:, 64:160].rearrange("p (i e) -> p i e", i=NT)
            mx8 = rt[:, 0:24].rearrange("p (i k) -> p i k", i=NT)
            ix8 = rt[:, 24:48].bitcast(U32).rearrange("p (i k) -> p i k", i=NT)
            ex = rt[:, 48:60].rearrange("p (i k) -> p i k", i=NT)
            dve.wait_ge(S["logit"], 1)
            then(dve.tensor_tensor(lg, ps[0:TT, 7, 0:96].rearrange("p (i e) -> p i e", i=NT),
                                   brt[:, None, :].to_broadcast([TT, NT, E]), ALU.add))
            for i in range(NT):
                then(dve.max(mx8[:, i, :], lg[:, i, :]))
                then(dve.max_index(ix8[:, i, :], mx8[:, i, :], lg[:, i, :]))
            then(dve.tensor_tensor(ex, mx8[:, :, 0:4], mx8[:, :, 0:1].to_broadcast([TT, NT, TK]), ALU.subtract), "topd")
            n12 = NT * TK
            ixf, posk, cch, bk, row = (rt[:, 160 + n12 * j:160 + n12 * (j + 1)] for j in range(5))
            msk = oht[:, 0:96].rearrange("p (i e) -> p i e", i=NT)
            then(dve.tensor_copy(ixf.rearrange("p (i k) -> p i k", i=NT), ix8[:, :, 0:4]))
            ohv = oh.rearrange("p (s e) -> p s e", e=E)
            then(dve.tensor_tensor(ohv, cc("iota", 0, TT)[:, None, :].to_broadcast([TT, n12, E]),
                                   ixf[:, :, None].to_broadcast([TT, n12, E]), ALU.is_equal))
            then(dve.tensor_reduce(msk, oh.rearrange("p (i k e) -> p i e k", i=NT, k=TK), AX, ALU.add), "mask")
            dve.wait_ge(S["tope"], 1)
            sm = rt[:, 220:223]
            then(dve.tensor_reduce(sm, ex, AX, ALU.add))
            then(dve.reciprocal(sm, sm))
            then(dve.tensor_tensor(pay[:, :, 2].bitcast(F32).rearrange("p (i k) -> p i k", i=NT), ex,
                                   sm[:, :, None].to_broadcast([TT, NT, TK]), ALU.mult), "pay_g")
            dve.wait_ge(S["posd"], 1)
            ohp = oht.rearrange("p (i k e) -> p i k e", i=NT, k=TK)
            posb = ps[0:TT, 6, 0:96].rearrange("p (i e) -> p i e", i=NT)[:, :, None, :].to_broadcast([TT, NT, TK, E])
            then(dve.tensor_tensor(ohp, oh.rearrange("p (i k e) -> p i k e", i=NT, k=TK), posb, ALU.mult))
            then(dve.tensor_reduce(posk, oht.rearrange("p (s e) -> p s e", e=E), AX, ALU.add))
            cnt, ext, incl, bm = (rt[:, 64 + 24 * 0:96], rt[:, 96:128], rt[:, 128:160], oht[:, 0:E])
            then(dve.tensor_copy(cnt, ps[0:TT, 6, 96:128]))
            then(dve.tensor_scalar(ext, cnt, float(CAP), None, ALU.is_gt))
            then(dve.tensor_scalar(cch, posk, float(CAP), None, ALU.is_ge))
            for j in range(2, -(-T // CAP)):
                then(dve.scalar_tensor_tensor(out=ext, in0=cnt, scalar=float(CAP * j), in1=ext,
                                              op0=ALU.is_gt, op1=ALU.add))
                then(dve.scalar_tensor_tensor(out=cch, in0=posk, scalar=float(CAP * j), in1=cch,
                                              op0=ALU.is_ge, op1=ALU.add))
            then(dve.tensor_tensor_scan(incl, ext, ext, 0.0, ALU.add, ALU.bypass))
            then(dve.scalar_tensor_tensor(out=bm, in0=incl, scalar=float(E - 1), in1=ext,
                                          op0=ALU.add, op1=ALU.subtract))
            then(dve.tensor_tensor(bm, bm, cc("iota", 0, TT), ALU.subtract))
            then(dve.tensor_tensor(ohv, ohv, bm[:, None, :].to_broadcast([TT, n12, E]), ALU.mult))
            then(dve.tensor_reduce(bk, ohv, AX, ALU.add))
            then(dve.scalar_tensor_tensor(out=bk, in0=cch, scalar=1.0, in1=bk, op0=ALU.is_ge, op1=ALU.mult))
            then(dve.tensor_tensor(bk, bk, ixf, ALU.add))
            then(dve.tensor_tensor(bk, bk, cch, ALU.add))
            then(dve.scalar_tensor_tensor(out=row, in0=cch, scalar=-float(CAP), in1=posk, op0=ALU.mult, op1=ALU.add))
            then(dve.scalar_tensor_tensor(out=row, in0=row, scalar=float(ITEMS), in1=bk, op0=ALU.mult, op1=ALU.add))
            then(dve.tensor_copy(rowi[:, :], row), "rows")
            le = oh[0:1, 0:N_OVER * 16]
            ov = rt[0:1, 0:1 + N_OVER]
            for h in range(2):
                lev = oh[0:1, 0:8 * E].rearrange("p (m e) -> p m e", e=E)
                then(dve.tensor_tensor(lev, incl[0:1, None, :].to_broadcast([1, 8, E]),
                                       cc("iota", 0, 1)[:, 8 * h:8 * h + 8, None].to_broadcast([1, 8, E]), ALU.is_le))
                then(dve.tensor_reduce(ov[:, 1 + 8 * h:9 + 8 * h], lev, AX, ALU.add))
            then(dve.tensor_copy(ov[:, 0:1], incl[0:1, E - 1:E]))
            then(dve.tensor_scalar(ov[:, 1:], ov[:, 1:], float(E - 1), None, ALU.min))
            then(dve.tensor_copy(ovi[:, :], ov), "ovd")
            dve.wait_ge(s_meta, 32)
            then(dve.tensor_scalar(meta[64:128, :, 1], meta[64:128, :, 1], 1, None, ALU.add), "metaok")

            def item(q):
                gu = ps[:, 1:3, :].rearrange("p n c -> p (n c)")
                dve.wait_ge(m_gu, q + 1)
                dve.tensor_scalar(g_sb, gu[:, 0::2], LIMIT, None, ALU.min).then_inc(m_g, 1)
                dve.tensor_scalar(up_sb, gu[:, 1::2], LIMIT, -LIMIT, ALU.min, ALU.max).then_inc(s_dve, 1)
                dve.wait_ge(m_g, q + 1)
                dve.wait_ge(s_dve, 2 * q + (base + 1))
                dve.scalar_tensor_tensor(out=up_sb, in0=up_sb, scalar=1.0, in1=g_sb,
                                         op0=ALU.add, op1=ALU.mult).then_inc(s_dve, 1)
                dve.wait_ge(s_dve, 2 * q + (base + 2))
                dve.wait_ge(m_sig, q + 1)
                dve.tensor_tensor(act_sb, up_sb, sig_sb, ALU.mult).then_inc(m_act, 1)
                dve.wait_ge(m_y, q + 1)
                dve.wait_ge(m_six, q + 1)
                dve.tensor_scalar(y_sb, ps[:, 4, :], meta[:, bass.ds(q, 1), 2].bitcast(F32), None,
                                  ALU.mult).then_inc(m_ysb, 1)

            base = up(s_dve, 0)
            with dve.Fori(0, E) as q:
                item(q)
            n_over = dve.value_load(ovi[0:1, 0:1], min_val=0, max_val=N_OVER)
            with dve.If(n_over > 0):
                with dve.Fori(0, n_over) as m:
                    item(m + E)

        @block.tensor
        def _(pe):
            def transpose(out, in_, k):
                return pe.transpose(out, in_, ident[0:k, 0:k])

            pe.wait_ge(s_con, 16)
            pe.wait_ge(S["hrow"], NT)
            for kt in range(KT):
                if kt >= 4:
                    pe.wait_ge(S["ht_cp"] if kt % 2 else S["ht_cp2"], (kt - 4) // 2 + 1)
                for i in range(NT):
                    mm = transpose(ps[:, kt % 4, TT * i:TT * i + TT], h_row[:, i, P * kt:P * kt + P], TT)
                mm.then_inc(S["ht_tr"], 1)
            pe.wait_ge(S["ht_cp"], 4)
            pe.wait_ge(S["ht_cp2"], 4)

            def project(n):
                if n % 2 == 0:
                    pe.wait_ge(s_win[n // 2], 16)
                if 2 <= n <= 10:
                    pe.wait_ge(S["proj_cp"], n - 1)
                elif n == 11:
                    pe.wait_ge(S["y_cp"], 1)
                elif n == 12:
                    pe.wait_ge(S["masked"], 2)
                for kt in range(KT):
                    mm = pe.matmul(ps[:, PBANK[n], 0:T], w_in[:, kt, P * n:P * n + P], hT[:, kt, :],
                                   start=(kt == 0), stop=(kt == KT - 1))
                mm.then_inc(S["proj"], 1)

            project(0)
            project(1)
            pe.wait_ge(s_vrow, 16 * 14)
            for c in range(NC):
                transpose(ps[:, 6, c * N_VROWS:(c + 1) * N_VROWS], v1[:, P * c:P * c + P], N_VROWS)
            transpose(ps[:, 6, 200:202], v2, 2).then_inc(S["vec_tr"], 1)
            for n in range(2, 6):
                project(n)
            pe.wait_ge(S["vec_cp"], 1)
            pe.wait_ge(S["sqqk"], 1)
            for c in range(5):
                mm = pe.matmul(ps[:, 3 + c, 0:T], cc("blk64"), sqq[:, c, :], start=True, stop=True)
            mm.then_inc(S["msqk"], 1)
            pe.wait_ge(s_kc, 16)
            for half in range(2):
                if half:
                    pe.wait_ge(S["kc_cp"], 1)
                for b in range(4):
                    mm = transpose(ps[:, 2, P * b:P * b + P], kc[:, 4 * half + b, :], P)
                mm.then_inc(S["kc_tr"], 1)
                project(6 + half)
            pe.wait_ge(S["kc_cp"], 2)
            for n in range(2):
                transpose(ps[:, 2, P * n:P * n + P], vT[:, P * n:P * n + P], P)
            transpose(ps[0:NS, 2, 256:384], vT[:, NP_:T], P).then_inc(S["v_tr"], 1)
            project(8)
            project(9)
            pe.wait_ge(S["ivqk"], 1)
            pe.wait_ge(S["qn"], 1)
            for c in range(5):
                mm = pe.matmul(ps[:, 3 + c, 0:T], cc("rot"), qk[:, c, :], start=True, stop=True)
            mm.then_inc(S["rotd"], 1)
            project(10)
            pe.wait_ge(S["roped"], 1)
            pe.wait_ge(S["v_cp"], 1)
            for n, w in ((1, 256), (0, 128)):
                for g in range(2):
                    for c in range(4):
                        h = 4 * g + c
                        out = ps[:, 2 + h // 2, 256 * (h % 2):256 * (h % 2) + 256] if n else ps[:, 6 + g, P * c:P * c + P]
                        mm = pe.matmul(out, qk[64 * g:64 * g + 64, c, P * n:P * n + P],
                                       qk[64 * g:64 * g + 64, 4, 0:w], start=True, stop=True)
                mm.then_inc(S["scores"], 1)
            pe.wait_ge(S["qbd_r"], 2)
            pe.wait_ge(S["proj_cp"], 10)
            pe.matmul(ps[0:64, 1, 64:64 + NS], qbd[:, :, :].rearrange("p b h -> p (b h)"), qk[:, 4, NP_:T],
                      start=True, stop=True)
            for b in range(NS):
                pe.matmul(ps[:, 1, 8 * b:8 * b + 8], kcT[:, b, :], qbd[:, b, :], start=True, stop=True)
            transpose(ps[:, 1, 256:384], qk[:, 4, P:NP_], P)
            transpose(ps[0:NS, 1, 384:512], qk[:, 4, NP_:T], P).then_inc(S["sc_t"], 1)

            def gate(n):
                if n >= 4:
                    pe.wait_ge(S["gate_s"], n - 3)
                pe.matmul(ps[:, 2 + n % 4, 0:T], bd[:, n % 2, n // 2, :], xc[:, n // 2, :],
                          start=True, stop=True).then_inc(S["gate"], 1)

            pe.wait_ge(s_bd, 64)
            pe.wait_ge(S["conv"], 2 * NC)
            pe.wait_ge(S["masked"], 1)
            for n in range(4):
                gate(n)
            for n in range(4, 2 * NC):
                gate(n)
            pe.wait_ge(S["sc_cp"], 1)
            transpose(ps[0:64, 1, 128:256], s_nT[:, :], P).then_inc(S["sc_tr"], 1)
            for n in range(11, 14):
                project(n)
            groups = [(0, 0, 0), (0, 0, 1), (1, 0, 0), (1, 0, 1), (1, 1, 0), (1, 1, 1)]
            pe.wait_ge(S["gate_s"], 2 * NC)
            for j, (n, kb, g) in enumerate(groups):
                pe.wait_ge(S["pn"], n + 1)
                if j == 4:
                    pe.wait_ge(S["y_cp"], 4)
                for c in range(4):
                    src = p1_sb if n else p0_sb
                    mm = transpose(ps[:, 2 + j, P * c:P * c + P], src[:, 4 * g + c, P * kb:P * kb + P], P)
                mm.then_inc(S["p_tr"], 1)
            pe.wait_ge(S["s_pn"], 1)
            transpose(ps[:, 0, 0:64], s_sb[:, 0:128], 64)
            transpose(ps[0:NS, 0, 128:192], s_dg[:, :], 64).then_inc(S["s_ptr"], 1)
            pe.wait_ge(S["p_cp"], 3)
            pe.wait_ge(S["p_cp2"], 3)
            pe.wait_ge(S["s_pcp"], 1)
            pe.wait_ge(S["krow_cp"], 1)
            for n in range(2):
                for g in range(2):
                    for kb in range(n + 1):
                        j = groups.index((n, kb, g))
                        mm = pe.matmul(ps[64 * g:64 * g + 64, n, :], kv_new[:, kb, 64 * g:64 * g + 64],
                                       pT[:, j, :], start=(kb == 0), stop=(kb == n))
                mm.then_inc(S["pv"], 1)
            pe.wait_ge(s_vc, 16)
            for b in range(NS):
                r = slice(8 * b, 8 * b + 8)
                pe.matmul(ps[:, 7, r], kv_new[0:NS, 2, :], s_dT[:, r], start=True, stop=False)
                mm = pe.matmul(ps[:, 7, r], vc[:, b, :], s_pT[:, r], start=False, stop=True)
            mm.then_inc(S["s_pv"], 1)

            def mean_square(j, src):
                pe.wait_ge(S["sqg"], j)
                for c in range(NC):
                    mm = pe.matmul(ps[:, 6, 0:T], cc("mean512"), src[:, c, :], start=(c == 0), stop=(c == NC - 1))
                mm.then_inc(S["msg"], 1)

            def out_half(i, n, half):
                for c in range(NC):
                    src = (yT if half else oT)[:, c, :]
                    mm = pe.matmul(ps[0:TT, 2 * i + n, :], src[:, TT * i:TT * i + TT],
                                   w_out[:, NC * half + c, 512 * n:512 * n + 512],
                                   start=(half == 0 and c == 0), stop=(half == 1 and c == NC - 1))
                return mm

            def states(j, rows, src):
                for c in range(NC):
                    mm = transpose(ps[0:rows, 7, P * c:P * c + P], src(c), P)
                mm.then_inc(S["st_tr"], 1)

            mean_square(1, sq)
            states(0, 3, lambda c: xe[:, c, NP_:NP_ + 3])
            pe.wait_ge(s_wout, 48)
            pe.wait_ge(S["mixed"], 1)
            for i in range(NT):
                for n in range(2):
                    out_half(i, n, 0)
                if i == 0:
                    pe.wait_ge(S["st_cp"], 1)
                    states(1, NS, lambda c: xs[:, c, :])
            mean_square(2, tq)
            pe.wait_ge(S["h_last"], 1)
            pe.wait_ge(S["st_cp"], 2)
            states(2, 9, lambda c: hs[:, c, NP_ - 1:T])
            pe.wait_ge(S["mixed"], 2)
            for i in range(NT):
                for n in range(2):
                    out_half(i, n, 1).then_inc(S["outp"], 1)
            pe.wait_ge(S["xn"], NT)
            for kt in range(KT):
                if kt >= 4:
                    pe.wait_ge(S["xnt_cp"] if kt % 2 else S["xnt_cp2"], (kt - 4) // 2 + 1)
                for i in range(NT):
                    mm = transpose(ps[:, kt % 4, TT * i:TT * i + TT], h_row[:, i, P * kt:P * kt + P], TT)
                mm.then_inc(S["xnt_tr"], 1)
            pe.wait_ge(S["xnt_cp"], 4)
            pe.wait_ge(S["xnt_cp2"], 4)
            pe.wait_ge(s_misc, 16 * 12)
            pe.wait_ge(S["st_cp"], 3)
            for i in range(NT):
                for kt in range(KT):
                    mm = pe.matmul(ps[0:TT, 7, E * i:E * i + E], hT[:, kt, TT * i:TT * i + TT], wr[:, kt, :],
                                   start=(kt == 0), stop=(kt == KT - 1))
            mm.then_inc(S["logit"], 1)
            pe.wait_ge(S["mask"], 1)
            msk = oht[:, 0:96].rearrange("p (i e) -> p i e", i=NT)
            for i in range(NT + 1):
                for j in range(min(i + 1, NT)):
                    mm = pe.matmul(ps[0:TT, 6, E * i:E * i + E], cc("tri" if i == j else "ones", 0, TT), msk[:, j, :],
                                   start=(j == 0), stop=(j == min(i, NT - 1)))
            mm.then_inc(S["posd"], 1)

            def x_transposes(q):
                pe.wait_ge(m_xg, 16 * q + 16)
                pe.sem_inc(m_passed[0], 1)
                for kt in range(KT):
                    mm = transpose(ps[:, 0, CAP * kt:CAP * kt + CAP], xg[:, P * kt:P * kt + P], CAP)
                mm.then_inc(m_xtr, 1)

            sel = cc("sel").rearrange("p (j m) -> p j m", j=6)

            def item(q):
                pe.wait_ge(m_xT, q + 1)
                for kt in range(KT):
                    pe.wait_ge(s_slot[kt], 16 * q + 16)
                    for n in range(2):
                        for h in range(2):
                            mm = pe.matmul(ps[64 * h:64 * h + 64, 1 + n, :], xT[:, kt, :],
                                           ring[:, kt, 1024 * h + 512 * n:1024 * h + 512 * n + 512],
                                           start=(kt == 0), stop=False)
                    mm.then_inc(m_used, 1)
                pe.wait_ge(m_bgu, 16 * q + 16)
                for n in range(2):
                    for h in range(2):
                        mm = pe.matmul(ps[64 * h:64 * h + 64, 1 + n, :], sel[:, 2 * h + n, :], b_gu,
                                       start=False, stop=True)
                mm.then_inc(m_gu, 1)
                x_transposes(q + 1)
                pe.wait_ge(m_act, q + 1)
                for j in range(4):
                    mm = transpose(ps[:, 3, P * j:P * j + P], act_sb[:, P * j:P * j + P], P)
                mm.then_inc(m_atr, 1)
                pe.wait_ge(m_aT, q + 1)
                for s in range(4):
                    pe.wait_ge(s_slot[KT + s], 16 * q + 16)
                    for t in range(2):
                        h, j = divmod(2 * s + t, 4)
                        for n in range(2):
                            mm = pe.matmul(ps[64 * n:64 * n + 64, 4, :], actT[:, j, 64 * h:64 * h + 64],
                                           ring[:, KT + s, 1024 * t + 512 * n:1024 * t + 512 * n + 512],
                                           start=(s == 0 and t == 0), stop=False)
                    mm.then_inc(m_used, 1)
                pe.wait_ge(m_bdn, 16 * q + 16)
                for n in range(2):
                    mm = pe.matmul(ps[64 * n:64 * n + 64, 4, :], sel[:, n, :], b_dn, start=False, stop=True)
                mm.then_inc(m_y, 1)

            x_transposes(0)
            with pe.Fori(0, E) as q:
                item(q)
            pe.wait_ge(S["ovd"], 1)
            n_over = pe.value_load(ovi[0:1, 0:1], min_val=0, max_val=N_OVER)
            with pe.If(n_over > 0):
                with pe.Fori(0, n_over) as m:
                    item(m + E)


def constants(np):
    c = {n: np.zeros((P, w), np.float32) for n, w in CONST_SIZES}
    i = np.arange(P)
    c["ident"][i, i] = 1
    c["blk64"][:] = (i[:, None] // HD == i[None, :] // HD) / np.float32(HD)
    c["mean512"][:] = 1.0 / DG
    for g in (0, HD):
        for d in range(8):
            c["rot"][g + d + 8, g + d] = -1
            c["rot"][g + d, g + d + 8] = 1
    pos = np.concatenate([np.arange(NP_), np.full(NS, 1024)]).astype(np.float32)
    inv_f = np.float32(500000.0) ** (-np.arange(0, 16, 2, dtype=np.float32) / np.float32(16))
    ang = (pos[:, None] * inv_f[None, :]).astype(np.float32)
    c["cos"][:] = 1
    for g in (0, HD):
        for b in (0, 8):
            c["cos"][g + b:g + b + 8] = np.cos(ang).T
            c["sin"][g + b:g + b + 8] = np.sin(ang).T
    c["mask"][:, 0:P] = np.where(i[None, :] >= i[:, None], 0, -1e30)
    c["mask"][:, P:] = np.where(i[None, :] <= i[:, None], 0, -1e30)
    c["iota"][:] = np.arange(E)
    c["tri"][:] = i[:, None] < np.arange(TT)[None, :]
    c["ones"][:] = 1
    c["diag"][:] = (i[:, None] // 8) == np.arange(NS)[None, :]
    for j in range(6):
        c["sel"][j, 64 * j:64 * j + 64] = 1
    con = np.concatenate([c[n] for n, _ in CONST_SIZES], axis=1)
    tok = np.arange(NT)[None, :, None] * TT + np.arange(TT)[:, None, None] + np.zeros((1, 1, TK), int)
    slots = np.stack([tok, 2 * tok], axis=-1).reshape(TT, -1).astype(np.int32)
    empty = np.full((CAP * ITEMS, 3), BIG, np.int32)
    return {"const": con, "slots": slots, "empty": empty}


_INS = ["x_prompt", "x_sample", "cache_k", "cache_v", "state_conv", "state_h", "g_mix_norm", "w_in", "g_q_norm",
        "g_k_norm", "attn_sinks", "conv_w", "conv_b", "w_lru_a", "b_lru_a", "w_lru_x", "b_lru_x", "lru_lambda",
        "g_attn_out", "g_rnn_out", "w_out", "g_ffn_norm", "w_router", "b_router", "w_gate_up", "b_gate_up",
        "w_down", "b_down"]
_OUTS = [("y_prompt", (1, 256, 1024)), ("y_sample", (8, 1, 1024)),
         ("new_k_prompt", (1, 1, 128, 2, 64)), ("new_v_prompt", (1, 1, 128, 2, 64)),
         ("new_conv_prompt", (1, 1, 3, 512)), ("new_h_prompt", (1, 1, 512)),
         ("new_k_sample", (1, 8, 128, 2, 64)), ("new_v_sample", (1, 8, 128, 2, 64)),
         ("new_conv_sample", (1, 8, 3, 512)), ("new_h_sample", (1, 8, 512))]


def kernel(**inputs):
    import numpy as _np
    import concourse.bacc as _bacc
    from concourse import mybir as _mybir
    from concourse.bass_utils import run_bass_kernel_spmd as _run

    nc = _bacc.Bacc("TRN2", target_bir_lowering=False, num_devices=1)
    arrays, a, o = {}, {}, {}
    given = {n: _np.ascontiguousarray(inputs[n]) for n in _INS}
    given.update(constants(_np))
    for name, v in given.items():
        arrays[f"in_{name}_dram"] = v
        a[name] = nc.dram_tensor(f"in_{name}_dram", v.shape, _mybir.dt.from_np(v.dtype), kind="ExternalInput").ap()
    for name, shape in _OUTS:
        o[name] = nc.dram_tensor(f"out_{name}_dram", shape, _mybir.dt.float32, kind="ExternalOutput").ap()
    scratch = {"xn": nc.dram_tensor("xn_dram", (T, D), _mybir.dt.float32, kind="Internal").ap(),
               "acc": nc.dram_tensor("acc_dram", (T, D), _mybir.dt.float32, kind="Internal").ap(),
               "table": nc.dram_tensor("table_dram", (CAP * ITEMS, 3), _mybir.dt.int32, kind="Internal").ap()}
    hybrid_layer(nc, a, o, scratch)
    r = _run(nc, [arrays], core_ids=[0])
    return tuple(r.results[0][f"out_{name}_dram"] for name, _ in _OUTS)
```

```python
from contextlib import ExitStack

import concourse.bass as bass
from concourse import mybir

F32 = mybir.dt.float32
I32 = mybir.dt.int32
U32 = mybir.dt.uint32
ALU = mybir.AluOpType
ACT = mybir.ActivationFunctionType
AX = mybir.AxisListType.X

P = 128
D = 1024
KT = D // P
NP_ = 256
NS = 8
T = NP_ + NS
TT = 88
NT = T // TT
HD = 64
NC = 4
DG = 512
E = 32
TK = 4
FF = 1024
D_IN = 1792
CAP = 64
N_OVER = 16
ITEMS = E + N_OVER
SLOTS = 12
POS0 = 4096
EPS = 1e-6
SCALE = HD ** -0.5
LRU_C = 8.0
LIMIT = 7.0
ALPHA = 1.702

E_BIAS = 8

CONST_SIZES = [("ident", 128), ("blk64", 128), ("mean512", 128), ("rot", 128), ("cos", T), ("sin", T),
               ("mask", 256), ("iota", E), ("tri", TT), ("ones", TT), ("diag", NS), ("sel", 4 * 64),
               ("slot", P), ("tok", NT)]
COFF = {}
_at = 0
for _n, _w in CONST_SIZES:
    COFF[_n] = (_at, _at + _w)
    _at += _w
NCONST = _at

R_CONV, R_H0, R_CW, R_CB, R_BA, R_BX, R_LAM, R_GR, R_GA, N_VROWS = 0, 24, 32, 36, 37, 38, 39, 40, 41, 42


def hybrid_layer(nc, a, o):
    ctx = ExitStack()
    with ctx:
        def sb(name, shape, dt=F32):
            return ctx.enter_context(nc.sbuf_tensor(name, shape, dt))

        def sem(name):
            return ctx.enter_context(nc.semaphore(name))

        ring = sb("ring", [P, SLOTS, 2 * FF])
        regA = sb("regA", [P, KT * D_IN])
        con = sb("con", [P, NCONST])
        x_row = sb("x_row", [P, NT, D])
        hT_t = sb("hT_t", [P, KT * T])
        qk = sb("qk", [P, 5, T])
        vT = sb("vT", [P, T])
        xe = sb("xe", [P, NC, 3 + NP_])
        xs = sb("xs", [P, NC, NS])
        yT = sb("yT", [P, NC, T])
        xc = sb("xc", [P, NC, T])
        bd = sb("bd", [P, 2, NC, P])
        vec = sb("vec", [P, NC, N_VROWS])
        vgq = sb("vgq", [P, 2])
        small = sb("small", [P, 64])
        smx = sb("smx", [P, 4, 16])
        kv_new = sb("kv_new", [P, 3, P])
        ovi = sb("ovi", [1, 1 + N_OVER], I32)
        brt = sb("brt", [TT, E])
        wr = sb("wr", [P, KT, E])
        sink_p = sb("sink_p", [P, 8])
        sink_s = sb("sink_s", [64, 1])
        qbd = sb("qbd", [P, NS, 8])

        ps = ctx.enter_context(nc.psum_tensor("ps", [P, 8, 512], F32))

        def cc(name, p0=0, p1=P):
            return con[p0:p1, COFF[name][0]:COFF[name][1]]

        ident = cc("ident")
        w_in = regA[:, :].rearrange("p (k n) -> p k n", k=KT)
        w_out = regA[:, 0:KT * D].rearrange("p (k n) -> p k n", k=KT)

        def whole(kt):
            return w_in[:, kt, 0:NC * T].rearrange("p (c t) -> p c t", c=NC)

        rT = whole(5)
        uT = whole(6)
        hs = whole(7)
        tq = w_in[:, 4:8, NC * T:NC * T + T]
        k_rows = w_in[:, 4:6, 5 * T:5 * T + P]
        xg_sb = regA[:, 0:512]
        xT = regA[:, 1024:1536].rearrange("p (j t) -> p j t", j=4)
        b_gu = regA[:, 1536:2048]
        g_sb = regA[:, 2560:3072]
        up_sb = regA[:, 3072:3584]
        sig_sb = regA[:, 3584:4096]
        act_sb = regA[:, 4096:4608]
        actT = regA[:, 4608:5120].rearrange("p (j t) -> p j t", j=4)
        y_sb = regA[:, 5120:5632]
        xn_row = regA[0:TT, 10416:10416 + NT * D].rearrange("p (i n) -> p i n", i=NT)

        def chosen(n0, n, rows=TT):
            return regA[0:rows, 13488 + n0:13488 + n0 + n]

        place_cols = chosen(0, NT * ITEMS).rearrange("p (i m) -> p i m", i=NT)
        gate_cols = chosen(150, NT * ITEMS).rearrange("p (i m) -> p i m", i=NT)
        oneh = chosen(300, NT * P).rearrange("p (i s) -> p i s", i=NT)
        tokg = chosen(684, NT * 2).rearrange("p (i f) -> p i f", i=NT)
        idxg = chosen(692, 2, P)
        tokens = regA[:, 8904:8904 + T]
        bias_dn = regA[0:E, 9168:9168 + D]
        gateT = regA[0:E, 8192:8192 + T]
        gated = regA[:, 8636:8636 + T]
        scr = ring[:, 8:12, :].rearrange("p s n -> p (s n)")
        h_row = scr[0:TT, 0:3072].rearrange("p (i n) -> p i n", i=NT)
        g_bc = scr[0:TT, 3072:4096]
        v1 = scr[0:N_VROWS, 4096:4608]
        v2 = scr[0:2, 4608:4736]
        sqq = scr[:, 0:5 * T].rearrange("p (c t) -> p c t", c=5)
        rs_t = scr[:, 0:2 * T].rearrange("p (c t) -> p c t", c=2)
        sq = scr[:, 1024:1024 + NC * T].rearrange("p (c t) -> p c t", c=NC)
        p1_sb = scr[:, 0:2048].rearrange("p (h k) -> p h k", h=8)
        p0_sb = scr[:, 2048:3072].rearrange("p (h k) -> p h k", h=8)
        pT = scr[:, 3072:6144].rearrange("p (g n) -> p g n", g=6)
        kc = scr[:, 6144:7168].rearrange("p (b n) -> p b n", b=NS)
        vc = scr[:, 7168:8192].rearrange("p (b n) -> p b n", b=NS)
        gf_bc = scr[0:TT, 3072:4096]
        hT = hT_t[:, :].rearrange("p (k t) -> p k t", k=KT)
        kcT = kc
        oT = hT_t[:, 1024:2080].rearrange("p (c t) -> p c t", c=NC)
        s_sb = scr[0:64, 6144:6273]
        s_nT = scr[:, 6280:6344]
        s_pT = scr[:, 6344:6408]
        s_dT = scr[0:NS, 6408:6472]
        s_dg = scr[0:64, 6472:6480]
        bdf = bd[:, :, :, :].rearrange("p a c n -> p (a c n)")
        oh = bdf[0:TT, 0:384]
        oht = bdf[0:TT, 384:768]
        rt = bdf[0:TT, 768:1024]

        sinkT = small[:, 0:8]

        s_con, s_vrow, s_gm, s_kc, s_vc, s_bd, s_misc, s_wout, s_gf = map(
            sem, ("const_landed", "vrows_landed", "gmix_landed", "kcache_landed", "vcache_landed",
                  "gatew_landed", "misc_landed", "wout_landed", "gffn_landed"))
        s_x = [sem(f"x_landed{i}") for i in range(NT)]
        s_win = [sem(f"win_landed{j}") for j in range(7)]
        s_slot = [sem(f"slot_landed{j}") for j in range(SLOTS)]
        s_zero = sem("zeroed")
        s_dve, s_act, s_pool = sem("dve_step"), sem("act_step"), sem("pool_step")
        names = ("ss_x", "ms_x", "rstd_x", "hrow", "ht_tr", "ht_cp", "ht_cp2", "vec_tr", "vec_cp", "proj", "proj_cp", "y_cp", "bhalf", "gelu",
                 "kc_tr", "kc_cp", "v_tr", "v_cp", "sqqk", "msqk", "ivqk", "rsqk", "qn", "rotd", "roped",
                 "conv", "lamabs", "lamexp", "sp", "gate", "gate_s", "av", "u2", "us", "rnn", "sqg", "msg", "ivg",
                 "rsg", "mixed", "scores", "masked", "neg_m", "exps", "pn", "p_tr", "p_cp", "p_cp2", "pv", "o_cp", "qbd_r",
                 "sc_t", "sc_cp", "sc_tr", "s_neg", "s_exp", "s_pn", "s_ptr", "s_pcp", "s_pv", "s_ocp",
                 "h_last", "krow_cp", "st_tr", "st_cp", "outp", "xmid", "ss_f", "ms_f", "rstd_f", "xn",
                 "xnt_tr", "xnt_cp", "xnt_cp2", "logit", "topd", "tope", "mask", "posd", "ovd", "gt_tr", "gt_cp")
        S = {n: sem(n) for n in names}
        s_kout, s_tok, s_stout = map(sem, ("kv_stored", "tokens_and_bias_landed", "states_stored"))
        m_used, m_gu, m_g, m_sig, m_act, m_atr, m_aT, m_ysb, m_xg, m_xgs, m_xtr, m_xT = map(
            sem, ("slot_used", "gateup_done", "g_done", "sigmoid_done", "act_done", "act_transposed", "actT_copied",
                  "y_copied", "x_gathered", "x_rows_copied", "x_transposed", "xT_copied"))
        m_bgu, m_idx, m_gated, m_oh, m_pl, m_add, s_out = map(
            sem, ("gu_bias_landed", "slots_known", "gates_placed", "item_chosen",
                  "results_placed", "results_added", "outputs_stored"))

        beside_ahead, beside_last = ((6, 7), (1, 2), (3, 0)), ((6, 7), (0, 5), (1, 2))
        m_passed, sp_passed = sem("pe_waits_passed"), sem("sp_waits_passed")

        w_gu = a["w_gate_up"].rearrange("l e k n -> (l e k) n")
        w_dn = a["w_down"].rearrange("l e k n -> (l e k) n")
        bgu_v = a["b_gate_up"].rearrange("l e (j n) -> (l e j) n", n=512)

        PBANK = [n % 2 for n in range(11)] + [0, 6, 7]

        block = ctx.enter_context(nc.Block())

        def counter():
            n = {}

            def up(s, k=1):
                n[s.name] = n.get(s.name, 0) + k
                return n[s.name]
            return up

        @block.sync
        def _(sp):
            xp = a["x_prompt"].rearrange("b t d -> (b t) d")
            xsm = a["x_sample"].rearrange("b t d -> (b t) d")
            for i in range(NT - 1):
                sp.dma_start(x_row[0:TT, i, :], xp[i * TT:(i + 1) * TT, :]).then_inc(s_x[i], 16)
            sp.dma_start(x_row[0:NP_ - 2 * TT, 2, :], xp[2 * TT:NP_, :]).then_inc(s_x[2], 16)
            sp.dma_start(x_row[NP_ - 2 * TT:TT, 2, :], xsm).then_inc(s_x[2], 16)
            sp.dma_start(con[:, :], a["const"][:, :]).then_inc(s_con, 16)
            for j, c0 in enumerate((0, 256, 512, 768, 1024, 1280, 1536)):
                if j == 2:
                    r = v1
                    for r0, n, src in ((R_CONV, 24, a["state_conv"][0].rearrange("b j c -> (b j) c")),
                                       (R_H0, NS, a["state_h"][0]), (R_CW, 4, a["conv_w"][0]), (R_CB, 1, a["conv_b"]),
                                       (R_BA, 1, a["b_lru_a"].rearrange("l n c -> l (n c)")),
                                       (R_BX, 1, a["b_lru_x"].rearrange("l n c -> l (n c)")),
                                       (R_LAM, 1, a["lru_lambda"]), (R_GR, 1, a["g_rnn_out"])):
                        sp.dma_start(r[r0:r0 + n, :], src).then_inc(s_vrow, 16)
                    for g in range(2):
                        sp.dma_start(r[R_GA:R_GA + 1, :].rearrange("p (c g d) -> p g c d", g=2, d=HD)[:, g],
                                     a["g_attn_out"].rearrange("l (g c d) -> l g c d", g=2, d=HD)[:, g]
                                     ).then_inc(s_vrow, 16)
                        for n, w in enumerate((a["g_q_norm"], a["g_k_norm"])):
                            sp.dma_start(v2[n:n + 1, 64 * g:64 * g + 64], w).then_inc(s_vrow, 16)
                sp.dma_start(w_in[:, :, c0:c0 + 256],
                             a["w_in"][0, :, c0:c0 + 256].rearrange("(k p) n -> p k n", p=P)).then_inc(s_win[j], 16)

            def load_slot(s, e):
                if s < KT:
                    src = w_gu[bass.ds(e * D + s * P, P), :]
                    dst = ring[:, s, :]
                else:
                    src = w_dn[bass.ds(e * FF + (s - KT) * 2 * P, 2 * P), :].rearrange("(t p) n -> p t n", p=P)
                    dst = ring[:, s, :].rearrange("p (t n) -> p t n", t=2)
                sp.dma_start(dst, src).then_inc(s_slot[s], 16)

            for s in range(KT):
                load_slot(s, 0)
            sp.wait_ge(S["proj"], 14)
            for g in range(2):
                sp.dma_start(w_out[64 * g:64 * g + 64, 0:NC, :],
                             a["w_out"][0, 256 * g:256 * g + 256, :].rearrange("(c d) n -> d c n", d=HD)
                             ).then_inc(s_wout, 16)
            sp.dma_start(w_out[:, NC:KT, :],
                         a["w_out"][0, DG:D, :].rearrange("(c p) n -> p c n", p=P)).then_inc(s_wout, 16)
            sp.wait_ge(S["pv"], 2)
            sp.dma_start(gf_bc, a["g_ffn_norm"].to_broadcast([TT, D])).then_inc(s_gf, 16)
            sp.wait_ge(S["xn"], NT)
            sp.dma_start(tokens, a["tokens"][:, :]).then_inc(s_tok, 16)
            sp.dma_start(bias_dn, a["b_down"][0]).then_inc(s_tok, 16)
            sp.wait_ge(s_stout, 16 * 4)
            for s in range(KT, SLOTS):
                load_slot(s, 0)

            def load_item(q, e):
                for s in range(SLOTS):
                    sp.wait_ge(m_used, q * SLOTS - (SLOTS - 1 - s))
                    load_slot(s, e)

            with sp.Fori(1, E) as q:
                load_item(q, q)
            sp.wait_ge(S["ovd"], 1)
            n_over = sp.value_load(ovi[0:1, 0:1], min_val=0, max_val=N_OVER)
            with sp.If(n_over > 0):
                with sp.Fori(0, n_over) as m:
                    e = sp.value_load(ovi[0:1, bass.ds(m + 1, 1)], min_val=0, max_val=E - 1)
                    load_item(m + E, e)
            yp = o["y_prompt"][0]
            for i in range(NT):
                sp.wait_ge(m_add, 6 * E + 2 * (i + 1) + 6 * n_over)
                sp.sem_inc(sp_passed, 1)
                rows = min(TT, NP_ - TT * i)
                sp.dma_start(yp[TT * i:TT * i + rows, :], x_row[0:rows, i, :]).then_inc(s_out, 16)
            sp.dma_start(o["y_sample"].rearrange("b t d -> (b t) d"), x_row[NP_ - 2 * TT:TT, 2, :]).then_inc(s_out, 16)
            sp.wait_ge(s_out, 16 * (NT + 1))
            sp.wait_ge(s_kout, 16 * 7)
            sp.wait_ge(s_stout, 16 * 4)

        @block.gpsimd
        def _(pool):
            for t in (xe[:, :, 0:3], bd[:, :, :, :], qbd[:, :, :]):
                pool.memset(t, 0).then_inc(s_zero, 1)
            pool.wait_ge(s_zero, 2)
            for n, w in enumerate((a["w_lru_a"], a["w_lru_x"])):
                for j in range(2):
                    pool.dma_start(bd[64 * j:64 * j + 64, n, :, 64 * j:64 * j + 64],
                                   w[0].rearrange("(c j) i o -> j i c o", j=2)[j]).then_inc(s_bd, 16)
            pool.dma_start(kc[:, :, :], a["cache_k"][0].rearrange("b w k d -> w b (k d)")).then_inc(s_kc, 16)
            pool.dma_start(vc[:, :, :], a["cache_v"][0].rearrange("b w k d -> w b (k d)")).then_inc(s_vc, 16)
            pool.dma_start(wr[:, :, :], a["w_router"][0].rearrange("(k p) n -> p k n", p=P)).then_inc(s_misc, 16)
            pool.dma_start(brt[:, :], a["b_router"].to_broadcast([TT, E])).then_inc(s_misc, 16)
            pool.dma_start(sink_p[:, :], a["attn_sinks"].to_broadcast([P, 8])).then_inc(s_misc, 16)
            for b in range(NS):
                pool.dma_start(sink_s[8 * b:8 * b + 8, :],
                               a["attn_sinks"].rearrange("l h -> h l")).then_inc(s_misc, 16)
            for name in "kv":
                pool.dma_start(o[f"new_{name}_sample"][0, :, 0:127].rearrange("b w k d -> b (w k d)"),
                               a[f"cache_{name}"][0, :, 1:128].rearrange("b w k d -> b (w k d)")
                               ).then_inc(s_kout, 16)
            pool.dma_start(o["new_conv_sample"][0, :, 0:2, :].rearrange("b j c -> b (j c)"),
                           a["state_conv"][0, :, 1:3, :].rearrange("b j c -> b (j c)")).then_inc(s_kout, 16)
            pool.wait_ge(S["v_cp"], 1)
            pool.dma_start(o["new_v_prompt"][0, 0].rearrange("w k d -> w (k d)"), kv_new[:, 1, :]).then_inc(s_kout, 16)
            pool.dma_start(o["new_v_sample"][0, :, 127].rearrange("b k d -> b (k d)"),
                           kv_new[0:NS, 2, :]).then_inc(s_kout, 16)
            pool.wait_ge(S["krow_cp"], 1)
            pool.dma_start(o["new_k_prompt"][0, 0].rearrange("w k d -> w (k d)"), k_rows[:, 0, :]).then_inc(s_kout, 16)
            pool.dma_start(o["new_k_sample"][0, :, 127].rearrange("b k d -> b (k d)"),
                           k_rows[0:NS, 1, :]).then_inc(s_kout, 16)

            pool.wait_ge(S["outp"], 2 * NT)
            pool.memset(b_gu, 0.0).then_inc(s_zero, 1)

        @block.scalar
        def _(act):
            up = counter()

            def then(ins, name=None):
                s = S[name] if name else s_act
                n = up(s)
                ins.then_inc(s, 1)
                act.wait_ge(s, n)

            act.dma_start(g_bc, a["g_mix_norm"].to_broadcast([TT, D])).then_inc(s_gm, 16)
            def square_x(i):
                act.wait_ge(s_x[i], 32 if i == 2 else 16)
                then(act.activation(h_row[:, i, :], x_row[0:TT, i, :], ACT.Square,
                                    accum_out=small[0:TT, i:i + 1]), "ss_x")

            def root_x(i):
                act.wait_ge(S["ms_x"], i + 1)
                then(act.activation(small[0:TT, 8 + i:9 + i], small[0:TT, 4 + i:5 + i], ACT.Sqrt), "rstd_x")

            square_x(0)
            square_x(1)
            root_x(0)
            square_x(2)
            root_x(1)
            root_x(2)
            for kt in range(1, KT, 2):
                act.wait_ge(S["ht_tr"], kt + 1)
                then(act.activation(hT[:, kt, :], ps[:, kt % 4, 0:T], ACT.Copy), "ht_cp")

            def evacuate(n):
                act.wait_ge(S["proj"], n + 1)
                src = ps[:, PBANK[n], 0:T]
                if n < 4:
                    for h in (2 * n, 2 * n + 1):
                        g, p0 = h // 4, 64 * (h % 2)
                        then(act.activation(qk[64 * g:64 * g + 64, h % 4, :], src[p0:p0 + 64], ACT.Copy),
                             "proj_cp" if h % 2 else None)
                elif n == 4:
                    then(act.activation(qk[:, 4, :], src, ACT.Copy), "proj_cp")
                elif n == 5:
                    then(act.activation(vT[:, :], src, ACT.Copy), "proj_cp")
                else:
                    if n == 6:
                        act.wait_ge(s_zero, 1)
                    then(act.activation(xs[:, n - 6, :], src[:, NP_:T], ACT.Copy))
                    then(act.activation(xe[:, n - 6, 3:3 + NP_], src[:, 0:NP_], ACT.Copy), "proj_cp")

            evacuate(0)
            evacuate(1)
            act.wait_ge(S["vec_tr"], 1)
            then(act.activation(vec[:, :, :], ps[:, 6, 0:NC * N_VROWS].rearrange("p (c r) -> p c r", c=NC), ACT.Copy))
            then(act.activation(vgq[:, :], ps[:, 6, 200:202], ACT.Copy), "vec_cp")
            evacuate(2)
            act.wait_ge(S["lamabs"], 1)
            then(act.activation(small[:, 20:24], small[:, 16:20], ACT.Exp, scale=-1.0), "lamexp")
            evacuate(3)
            evacuate(4)
            then(act.activation(sqq[:, :, :], qk[:, :, :], ACT.Square), "sqqk")
            evacuate(5)
            act.wait_ge(S["kc_tr"], 1)
            then(act.activation(kcT[:, 0:4, :], ps[:, 2, :].rearrange("p (b n) -> p b n", b=4), ACT.Copy), "kc_cp")
            evacuate(6)
            act.wait_ge(S["kc_tr"], 2)
            then(act.activation(kcT[:, 4:8, :], ps[:, 2, :].rearrange("p (b n) -> p b n", b=4), ACT.Copy), "kc_cp")
            evacuate(7)
            act.wait_ge(S["v_tr"], 1)
            then(act.activation(kv_new[:, 0:2, :], ps[:, 2, 0:256].rearrange("p (b n) -> p b n", b=2), ACT.Copy))
            then(act.activation(kv_new[0:NS, 2, :], ps[0:NS, 2, 256:384], ACT.Copy), "v_cp")
            evacuate(8)
            act.wait_ge(S["ivqk"], 1)
            then(act.activation(sqq[:, :, :], sqq[:, :, :], ACT.Sqrt), "rsqk")
            evacuate(9)
            act.wait_ge(S["sc_t"], 1)
            then(act.activation(s_nT[:, :], ps[:, 1, 0:64], ACT.Copy), "sc_cp")

            def gate(n):
                c, x = n // 2, n % 2
                act.wait_ge(S["gate"], n + 1)
                then(act.activation((uT if x else rT)[:, c, :], ps[:, 2 + n % 4, 0:T], ACT.Tanh, scale=0.5,
                                    bias=small[:, 56 + 4 * x + c:57 + 4 * x + c]), "gate_s")

            act.wait_ge(S["bhalf"], 1)
            for n in range(4):
                gate(n)
            act.wait_ge(S["neg_m"], 1)
            for n, pt in ((1, p1_sb), (0, p0_sb)):
                for h in range(8):
                    act.activation(pt[:, h, :], pt[:, h, :], ACT.Exp, scale=SCALE,
                                   bias=smx[:, 1, 8 * n + h:8 * n + h + 1],
                                   accum_out=smx[:, 2, 8 * n + h:8 * n + h + 1]).then_inc(s_act, 1)
                    up(s_act)
            then(act.activation(smx[:, 3, :], smx[:, 3, :], ACT.Exp), "exps")
            act.wait_ge(S["s_neg"], 1)
            then(act.activation(s_sb[:, :], s_sb[:, :], ACT.Exp, scale=SCALE, bias=small[0:64, 33:34],
                                accum_out=small[0:64, 34:35]))
            then(act.activation(small[0:64, 35:36], sink_s[:, :], ACT.Exp, bias=small[0:64, 33:34]), "s_exp")
            for n in range(4, 2 * NC):
                gate(n)
            act.wait_ge(S["sp"], 1)
            for c in range(NC):
                then(act.activation(hs[:, c, :], rT[:, c, :], ACT.Tanh, scale=small[:, 24 + c:25 + c],
                                    bias=small[:, 24 + c:25 + c]))
                then(act.activation(rT[:, c, :], rT[:, c, :], ACT.Exp, scale=small[:, 28 + c:29 + c],
                                    bias=small[:, 28 + c:29 + c]), "av")
            for g in (0, 2, 4):
                act.wait_ge(S["p_tr"], g + 1)
                then(act.activation(pT[:, g, :], ps[:, 2 + g, :], ACT.Copy), "p_cp")
                if g == 0:
                    act.wait_ge(S["s_ptr"], 1)
                    then(act.activation(s_pT[:, :], ps[:, 0, 0:64], ACT.Copy))
                    then(act.activation(s_dT[:, :], ps[0:NS, 0, 128:192], ACT.Copy), "s_pcp")
            then(act.activation(k_rows[:, 0, :], ps[:, 1, 256:384], ACT.Copy))
            then(act.activation(k_rows[0:NS, 1, :], ps[0:NS, 1, 384:512], ACT.Copy), "krow_cp")
            act.wait_ge(S["o_cp"], 3)
            then(act.activation(sq[:, 0:NC, :], oT[:, :, :], ACT.Square), "sqg")
            act.wait_ge(S["u2"], 1)
            then(act.activation(tq[:, :, :], tq[:, :, :], ACT.Sqrt, scale=0.25), "us")
            act.wait_ge(S["ivg"], 1)
            then(act.activation(rs_t[:, 1, :], rs_t[:, 1, :], ACT.Sqrt), "rsg")
            st = scr[0:9, 6144:7680].rearrange("p (g n) -> p g n", g=3)
            act.wait_ge(S["st_tr"], 1)
            then(act.activation(st[0:3, 1, :], ps[0:3, 7, :], ACT.Copy), "st_cp")
            act.wait_ge(S["y_cp"], 4)
            then(act.activation(yT[:, :, :], yT[:, :, :], ACT.Gelu_apprx_tanh), "gelu")
            act.wait_ge(S["rnn"], 1)
            then(act.activation(tq[:, :, :], yT[:, :, :], ACT.Square), "sqg")
            act.wait_ge(S["st_tr"], 2)
            then(act.activation(st[0:NS, 2, :], ps[0:NS, 7, :], ACT.Copy), "st_cp")
            act.wait_ge(S["ivg"], 2)
            then(act.activation(rs_t[:, 0, :], rs_t[:, 0, :], ACT.Sqrt), "rsg")
            act.wait_ge(S["st_tr"], 3)
            then(act.activation(st[0:9, 0, :], ps[0:9, 7, :], ACT.Copy), "st_cp")
            act.dma_start(o["new_h_prompt"][0], st[0:1, 0, :]).then_inc(s_stout, 16)
            act.dma_start(o["new_h_sample"][0], st[1:9, 0, :]).then_inc(s_stout, 16)
            act.dma_start(o["new_conv_prompt"][0, 0], st[0:3, 1, :]).then_inc(s_stout, 16)
            act.dma_start(o["new_conv_sample"][0, :, 2], st[0:NS, 2, :]).then_inc(s_stout, 16)
            def square_f(i):
                act.wait_ge(S["xmid"], 2 * i + 2)
                then(act.activation(xn_row[:, i, :], x_row[0:TT, i, :], ACT.Square,
                                    accum_out=small[0:TT, 36 + i:37 + i]), "ss_f")
                act.wait_ge(S["ms_f"], i + 1)
                then(act.activation(small[0:TT, 40 + i:41 + i], small[0:TT, 40 + i:41 + i], ACT.Sqrt), "rstd_f")

            def copy_f(i):
                act.wait_ge(S["xnt_tr"], 2 * i + 1)
                then(act.activation(hT[:, 0:4, TT * i:TT * i + TT],
                                    ps[:, 6, 0:4 * TT].rearrange("p (k t) -> p k t", k=4), ACT.Copy), "xnt_cp")

            def exp_top(i):
                act.wait_ge(S["topd"], i + 1)
                then(act.activation(rt[:, 48 + 4 * i:52 + 4 * i], rt[:, 48 + 4 * i:52 + 4 * i], ACT.Exp), "tope")

            square_f(0)
            square_f(1)
            copy_f(0)
            square_f(2)
            copy_f(1)
            exp_top(0)
            copy_f(2)
            exp_top(1)
            exp_top(2)

            def copy_rows(q):
                act.wait_ge(m_xg, q + 1)
                act.activation(xg_sb, ps[:, 6, :], ACT.Copy).then_inc(m_xgs, 1)

            def copy_x(q):
                act.wait_ge(m_xtr, q + 1)
                act.activation(xT[:, :, :], ps[:, 0, :].rearrange("p (j t) -> p j t", j=4),
                               ACT.Copy).then_inc(m_xT, 1)

            def item(q, ahead):
                act.wait_ge(m_g, q + 1)
                act.activation(sig_sb, g_sb, ACT.Sigmoid, scale=ALPHA).then_inc(m_sig, 1)
                if ahead:
                    copy_rows(q + 1)
                act.wait_ge(m_atr, q + 1)
                act.activation(actT[:, :, :], ps[:, 3, :].rearrange("p (j t) -> p j t", j=4),
                               ACT.Copy).then_inc(m_aT, 1)
                if ahead:
                    copy_x(q + 1)

            def bias_gu(q, e):
                act.dma_start(b_gu[0:4, :], bgu_v[bass.ds(e * 4, 4), :]).then_inc(m_bgu, 16)

            act.wait_ge(s_zero, 4)
            bias_gu(0, 0)
            copy_rows(0)
            copy_x(0)
            act.wait_ge(S["gt_tr"], 1)
            act.activation(gateT, ps[0:E, 7, 0:T], ACT.Copy).then_inc(S["gt_cp"], 1)

            def step(q, e_next):
                item(q, True)
                bias_gu(q + 1, e_next)

            with act.Fori(0, E - 1) as q:
                step(q, q + 1)
            act.wait_ge(S["ovd"], 1)
            n_over = act.value_load(ovi[0:1, 0:1], min_val=0, max_val=N_OVER)
            item(E - 1, False)
            with act.If(n_over > 0):
                with act.Fori(0, n_over) as m:
                    e = act.value_load(ovi[0:1, bass.ds(m + 1, 1)], min_val=0, max_val=E - 1)
                    bias_gu(m + E, e)
                    copy_rows(m + E)
                    copy_x(m + E)
                    item(m + E, False)

        @block.vector
        def _(dve):
            up = counter()

            def then(ins, name=None):
                s = S[name] if name else s_dve
                n = up(s)
                ins.then_inc(s, 1)
                dve.wait_ge(s, n)

            def inv(dst, src, scale):
                then(dve.tensor_scalar(dst, src, scale, EPS, ALU.mult, ALU.add))

            def mean_x(i):
                dve.wait_ge(S["ss_x"], i + 1)
                inv(small[0:TT, 4 + i:5 + i], small[0:TT, i:i + 1], 1.0 / D)
                then(dve.reciprocal(small[0:TT, 4 + i:5 + i], small[0:TT, 4 + i:5 + i]), "ms_x")

            def norm_x(i):
                dve.wait_ge(S["rstd_x"], i + 1)
                then(dve.scalar_tensor_tensor(out=h_row[:, i, :], in0=x_row[0:TT, i, :], scalar=small[0:TT, 8 + i:9 + i],
                                              in1=g_bc, op0=ALU.mult, op1=ALU.mult), "hrow")

            mean_x(0)
            mean_x(1)
            dve.wait_ge(s_gm, 16)
            norm_x(0)
            mean_x(2)
            norm_x(1)
            norm_x(2)
            for kt in range(0, KT, 2):
                dve.wait_ge(S["ht_tr"], kt + 1)
                then(dve.tensor_copy(hT[:, kt, :], ps[:, kt % 4, 0:T]), "ht_cp2")
            dve.wait_ge(S["vec_cp"], 1)
            lam = vec[:, :, R_LAM]
            then(dve.tensor_scalar(small[:, 12:16], lam, -1.0, None, ALU.mult))
            then(dve.tensor_tensor(small[:, 16:20], lam, small[:, 12:16], ALU.max), "lamabs")
            dve.wait_ge(S["lamexp"], 1)
            z, w, w2, acc = small[:, 20:24], small[:, 44:48], small[:, 48:52], small[:, 52:56]
            then(dve.tensor_scalar(w, z, 2.0, None, ALU.add))
            then(dve.reciprocal(w, w))
            then(dve.tensor_tensor(w, w, z, ALU.mult))
            then(dve.tensor_tensor(w2, w, w, ALU.mult))
            then(dve.tensor_scalar(acc, w2, 1.0 / 17, 1.0 / 15, ALU.mult, ALU.add))
            for k in (13, 11, 9, 7, 5, 3, 1):
                then(dve.tensor_tensor(acc, acc, w2, ALU.mult))
                then(dve.tensor_scalar(acc, acc, 1.0 / k, None, ALU.add))
            then(dve.tensor_tensor(acc, acc, w, ALU.mult))
            then(dve.tensor_scalar(small[:, 12:16], small[:, 12:16], 0.0, None, ALU.max))
            then(dve.scalar_tensor_tensor(out=acc, in0=acc, scalar=2.0, in1=small[:, 12:16],
                                          op0=ALU.mult, op1=ALU.add))
            then(dve.tensor_scalar(small[:, 24:28], acc, LRU_C / 2, None, ALU.mult))
            then(dve.tensor_scalar(small[:, 28:32], acc, -LRU_C / 2, None, ALU.mult), "sp")
            then(dve.tensor_scalar(small[:, 56:60], vec[:, :, R_BA], 0.5, None, ALU.mult))
            then(dve.tensor_scalar(small[:, 60:64], vec[:, :, R_BX], 0.5, None, ALU.mult), "bhalf")

            def convolve(c):
                dve.wait_ge(S["proj_cp"], c + 7)
                for out, tap in ((xc[:, c, 0:NP_], lambda j: xe[:, c, j:j + NP_]),
                                 (xc[:, c, NP_:T], lambda j: vec[:, c, R_CONV + j:R_CONV + 24:3] if j < 3
                                  else xs[:, c, :])):
                    then(dve.tensor_scalar(out, tap(0), vec[:, c, R_CW:R_CW + 1], vec[:, c, R_CB:R_CB + 1],
                                           ALU.mult, ALU.add))
                    for j in range(1, 4):
                        then(dve.scalar_tensor_tensor(out=out, in0=tap(j), scalar=vec[:, c, R_CW + j:R_CW + j + 1],
                                                      in1=out, op0=ALU.mult, op1=ALU.add),
                             "conv" if j == 3 else None)

            def y_copy(c):
                dve.wait_ge(S["proj"], c + 11)
                then(dve.tensor_copy(yT[:, c, :], ps[:, PBANK[10 + c], 0:T]), "y_cp")

            dve.wait_ge(S["msqk"], 1)
            then(dve.tensor_scalar(sqq[:, :, :], ps[:, 3:8, 0:T], EPS, None, ALU.add))
            then(dve.reciprocal(sqq[:, :, :], sqq[:, :, :]), "ivqk")
            convolve(0)
            dve.wait_ge(S["rsqk"], 1)
            then(dve.scalar_tensor_tensor(out=qk[:, 0:4, :], in0=qk[:, 0:4, :], scalar=vgq[:, 0:1], in1=sqq[:, 0:4, :],
                                          op0=ALU.mult, op1=ALU.mult))
            then(dve.scalar_tensor_tensor(out=qk[:, 4, :], in0=qk[:, 4, :], scalar=vgq[:, 1:2], in1=sqq[:, 4, :],
                                          op0=ALU.mult, op1=ALU.mult), "qn")
            convolve(1)
            dve.wait_ge(S["rotd"], 1)
            cosb = cc("cos")[:, None, :].to_broadcast([P, 5, T])
            sinb = cc("sin")[:, None, :].to_broadcast([P, 5, T])
            then(dve.tensor_tensor(sqq[:, :, :], ps[:, 3:8, 0:T], sinb, ALU.mult))
            then(dve.tensor_tensor(qk[:, :, :], qk[:, :, :], cosb, ALU.mult))
            then(dve.tensor_tensor(qk[:, :, :], qk[:, :, :], sqq[:, :, :], ALU.add), "roped")
            y_copy(0)
            dve.wait_ge(s_zero, 3)
            for g in range(2):
                then(dve.tensor_copy(qbd[64 * g:64 * g + 64, :, 4 * g:4 * g + 4].rearrange("p b c -> p c b"),
                                     qk[64 * g:64 * g + 64, 0:4, NP_:T]), "qbd_r")
            convolve(2)
            convolve(3)

            dve.wait_ge(S["scores"], 1)
            maskb = cc("mask")[:, None, :].to_broadcast([P, 8, 256])
            then(dve.tensor_tensor(p1_sb[:, :, :], ps[:, 2:6, :].rearrange("p g (h k) -> p (g h) k", h=2),
                                   maskb, ALU.add), "masked")
            dve.wait_ge(S["scores"], 2)
            then(dve.tensor_tensor(p0_sb[:, :, :], ps[:, 6:8, :].rearrange("p g (h k) -> p (g h) k", h=4),
                                   maskb[:, :, 128:256], ALU.add), "masked")
            then(dve.tensor_reduce(smx[:, 0, 8:16], p1_sb[:, :, :], AX, ALU.max))
            then(dve.tensor_reduce(smx[:, 0, 0:8], p0_sb[:, :, :], AX, ALU.max))
            dve.wait_ge(s_misc, 16 * 11)
            sinkb = sink_p[:, None, :].to_broadcast([P, 2, 8])
            m3 = smx[:, 0, :].rearrange("p (n h) -> p n h", n=2)
            then(dve.scalar_tensor_tensor(out=m3, in0=m3, scalar=SCALE, in1=sinkb, op0=ALU.mult, op1=ALU.max))
            then(dve.tensor_tensor(smx[:, 3, :].rearrange("p (n h) -> p n h", n=2), sinkb, m3, ALU.subtract))
            then(dve.tensor_scalar(smx[:, 1, :], smx[:, 0, :], -1.0, None, ALU.mult), "neg_m")
            dve.wait_ge(S["sc_tr"], 1)
            then(dve.tensor_tensor(s_dg[:, :], ps[0:64, 1, 64:72], cc("diag", 0, 64), ALU.mult))
            then(dve.tensor_reduce(s_sb[:, 128:129], s_dg[:, :], AX, ALU.add))
            then(dve.tensor_copy(s_sb[:, 0:128], ps[0:64, 1, 128:256]))
            then(dve.tensor_reduce(small[0:64, 32:33], s_sb[:, :], AX, ALU.max))
            then(dve.scalar_tensor_tensor(out=small[0:64, 33:34], in0=small[0:64, 32:33], scalar=SCALE,
                                          in1=sink_s[:, :], op0=ALU.mult, op1=ALU.max))
            then(dve.tensor_scalar(small[0:64, 33:34], small[0:64, 33:34], -1.0, None, ALU.mult), "s_neg")
            y_copy(1)
            dve.wait_ge(S["exps"], 1)
            then(dve.tensor_tensor(smx[:, 2, :], smx[:, 2, :], smx[:, 3, :], ALU.add))
            then(dve.reciprocal(smx[:, 2, :], smx[:, 2, :]))
            def over_sums(n, pt, w_):
                then(dve.tensor_tensor(pt[:, :, :], pt[:, :, :],
                                       smx[:, 2, 8 * n:8 * n + 8][:, :, None].to_broadcast([P, 8, w_]), ALU.mult),
                     "pn")

            over_sums(0, p0_sb, 128)
            dve.wait_ge(S["s_exp"], 1)
            then(dve.tensor_tensor(small[0:64, 34:35], small[0:64, 34:35], small[0:64, 35:36], ALU.add))
            then(dve.reciprocal(small[0:64, 34:35], small[0:64, 34:35]))
            then(dve.tensor_scalar(s_sb[:, :], s_sb[:, :], small[0:64, 34:35], None, ALU.mult))
            then(dve.tensor_scalar(s_dg[:, :], cc("diag", 0, 64), s_sb[:, 128:129], None, ALU.mult), "s_pn")
            over_sums(1, p1_sb, 256)
            y_copy(2)
            y_copy(3)
            for g in (1, 3, 5):
                dve.wait_ge(S["p_tr"], g + 1)
                then(dve.tensor_copy(pT[:, g, :], ps[:, 2 + g, :]), "p_cp2")
            dve.wait_ge(S["gate_s"], 2 * NC)
            then(dve.scalar_tensor_tensor(out=uT[:, :, :], in0=uT[:, :, :], scalar=1.0, in1=xc[:, :, :],
                                          op0=ALU.add, op1=ALU.mult))
            def out_copy(n):
                dve.wait_ge(S["pv"], n + 1)
                then(dve.tensor_copy(oT[:, :, P * n:P * n + P],
                                     ps[:, n, :].rearrange("p (c t) -> p c t", c=NC)), "o_cp")

            out_copy(0)
            dve.wait_ge(S["s_pv"], 1)
            for g in range(2):
                cached, own = (ps[64 * g:64 * g + 64, 2 + j, 0:64].rearrange("p (b g c) -> p g c b", g=2, c=4)[:, g]
                               for j in range(2))
                ins = dve.tensor_copy(oT[64 * g:64 * g + 64, :, NP_:T], own)
                then(ins)
                ins = dve.tensor_tensor(oT[64 * g:64 * g + 64, :, NP_:T], oT[64 * g:64 * g + 64, :, NP_:T], cached,
                                        ALU.add)
                then(ins, "o_cp" if g else None)
            out_copy(1)
            dve.wait_ge(S["av"], NC)
            then(dve.tensor_tensor(tq[:, :, :], rT[:, :, :], rT[:, :, :], ALU.mult))
            then(dve.scalar_tensor_tensor(out=tq[:, :, :], in0=tq[:, :, :], scalar=1.0, in1=hs[:, :, :],
                                          op0=ALU.add, op1=ALU.mult), "u2")
            dve.wait_ge(S["msg"], 1)
            then(dve.tensor_scalar(rs_t[:, 1, :], ps[:, 6, 0:T], EPS, None, ALU.add))
            then(dve.reciprocal(rs_t[:, 1, :], rs_t[:, 1, :]), "ivg")
            dve.wait_ge(S["rsg"], 1)
            for c in range(NC):
                then(dve.scalar_tensor_tensor(out=oT[:, c, :], in0=oT[:, c, :], scalar=vec[:, c, R_GA:R_GA + 1],
                                              in1=rs_t[:, 1, :], op0=ALU.mult, op1=ALU.mult),
                     "mixed" if c == 3 else None)
            dve.wait_ge(S["us"], 1)
            then(dve.tensor_tensor(uT[:, :, :], uT[:, :, :], tq[:, :, :], ALU.mult))
            for c in range(NC):
                then(dve.tensor_tensor_scan(hs[:, c, 0:NP_], rT[:, c, 0:NP_], uT[:, c, 0:NP_], 0.0,
                                            ALU.mult, ALU.add))
            then(dve.tensor_tensor(hs[:, :, NP_:T], rT[:, :, NP_:T], vec[:, :, R_H0:R_H0 + NS], ALU.mult))
            then(dve.tensor_tensor(hs[:, :, NP_:T], hs[:, :, NP_:T], uT[:, :, NP_:T], ALU.add), "h_last")
            dve.wait_ge(S["gelu"], 1)
            then(dve.tensor_tensor(yT[:, :, :], yT[:, :, :], hs[:, :, :], ALU.mult), "rnn")
            dve.wait_ge(S["msg"], 2)
            then(dve.tensor_scalar(rs_t[:, 0, :], ps[:, 6, 0:T], EPS, None, ALU.add))
            then(dve.reciprocal(rs_t[:, 0, :], rs_t[:, 0, :]), "ivg")
            dve.wait_ge(S["rsg"], 2)
            for c in range(NC):
                then(dve.scalar_tensor_tensor(out=yT[:, c, :], in0=yT[:, c, :], scalar=vec[:, c, R_GR:R_GR + 1],
                                              in1=rs_t[:, 0, :], op0=ALU.mult, op1=ALU.mult),
                     "mixed" if c == 3 else None)
            def ffn_norm(i):
                for n in range(2):
                    dve.wait_ge(S["outp"], 2 * i + n + 1)
                    then(dve.tensor_tensor(x_row[0:TT, i, 512 * n:512 * n + 512],
                                           x_row[0:TT, i, 512 * n:512 * n + 512],
                                           ps[0:TT, 2 * i + n, :], ALU.add), "xmid")
                dve.wait_ge(S["ss_f"], i + 1)
                inv(small[0:TT, 40 + i:41 + i], small[0:TT, 36 + i:37 + i], 1.0 / D)
                then(dve.reciprocal(small[0:TT, 40 + i:41 + i], small[0:TT, 40 + i:41 + i]), "ms_f")
                dve.wait_ge(S["rstd_f"], i + 1)
                dve.wait_ge(s_gf, 16)
                then(dve.scalar_tensor_tensor(out=xn_row[:, i, :], in0=x_row[0:TT, i, :],
                                              scalar=small[0:TT, 40 + i:41 + i], in1=gf_bc,
                                              op0=ALU.mult, op1=ALU.mult), "xn")

            def copy_f(i):
                dve.wait_ge(S["xnt_tr"], 2 * i + 2)
                then(dve.tensor_copy(hT[:, 4:8, TT * i:TT * i + TT],
                                     ps[:, 7, 0:4 * TT].rearrange("p (k t) -> p k t", k=4)), "xnt_cp2")

            lg = rt[:, 64:160].rearrange("p (i e) -> p i e", i=NT)
            mx8 = rt[:, 0:24].rearrange("p (i k) -> p i k", i=NT)
            ix8 = rt[:, 24:48].bitcast(U32).rearrange("p (i k) -> p i k", i=NT)
            ex = rt[:, 48:60].rearrange("p (i k) -> p i k", i=NT)
            ixf, gt = (rt[:, 160 + 12 * j:172 + 12 * j].rearrange("p (i k) -> p i k", i=NT) for j in range(2))
            sm = rt[:, 220:223]
            msk = oht[:, 0:96].rearrange("p (i e) -> p i e", i=NT)
            ohv = oh.rearrange("p (i k e) -> p i k e", i=NT, k=TK)

            def top4(i):
                dve.wait_ge(S["logit"], i + 1)
                then(dve.tensor_tensor(lg[:, i, :], ps[0:TT, 2 * i, 0:E], brt[:, :], ALU.add))
                then(dve.max(mx8[:, i, :], lg[:, i, :]))
                then(dve.tensor_tensor(ex[:, i, :], mx8[:, i, 0:4], mx8[:, i, 0:1].to_broadcast([TT, TK]),
                                       ALU.subtract), "topd")
                then(dve.max_index(ix8[:, i, :], mx8[:, i, :], lg[:, i, :]))
                then(dve.tensor_copy(ixf[:, i, :], ix8[:, i, 0:4]))
                then(dve.tensor_tensor(ohv[:, i], cc("iota", 0, TT)[:, None, :].to_broadcast([TT, TK, E]),
                                       ixf[:, i, :, None].to_broadcast([TT, TK, E]), ALU.is_equal))
                then(dve.tensor_reduce(msk[:, i, :], ohv[:, i].rearrange("p k e -> p e k"), AX, ALU.add), "mask")

            def gates(i):
                dve.wait_ge(S["tope"], i + 1)
                then(dve.tensor_reduce(sm[:, i:i + 1], ex[:, i, :], AX, ALU.add))
                then(dve.reciprocal(sm[:, i:i + 1], sm[:, i:i + 1]))
                then(dve.tensor_scalar(gt[:, i, :], ex[:, i, :], sm[:, i:i + 1], None, ALU.mult))
                then(dve.tensor_tensor(ohv[:, i], ohv[:, i], gt[:, i, :, None].to_broadcast([TT, TK, E]), ALU.mult))
                then(dve.tensor_reduce(gate_cols[:, i, 0:E], ohv[:, i].rearrange("p k e -> p e k"), AX, ALU.add))

            def places(i):
                dve.wait_ge(S["posd"], i + 1)
                then(dve.scalar_tensor_tensor(out=place_cols[:, i, 0:E], in0=ps[0:TT, 2 * i + 1, 0:E],
                                              scalar=float(POS0), in1=msk[:, i, :], op0=ALU.add, op1=ALU.mult))

            ffn_norm(0)
            ffn_norm(1)
            copy_f(0)
            top4(0)
            ffn_norm(2)
            copy_f(1)
            top4(1)
            copy_f(2)
            then(dve.tensor_copy(tokg[:, :, 0], cc("tok", 0, TT)))
            gates(0)
            places(0)
            top4(2)
            gates(1)
            places(1)
            gates(2)
            places(2)

            def choose(q):
                for i in range(NT):
                    dve.tensor_scalar(oneh[:, i, :], cc("slot", 0, TT), place_cols[:, i, bass.ds(q, 1)], None,
                                      ALU.is_equal).then_inc(m_oh, 1)
                dve.tensor_copy(tokg[:, :, 1:2], gate_cols[:, :, bass.ds(q, 1)]).then_inc(m_oh, 1)

            choose(0)
            cnt, ext, incl, excl = rt[:, 64:96], rt[:, 96:128], rt[:, 128:160], oh[:, 0:E]
            dve.wait_ge(S["posd"], NT + 1)
            then(dve.tensor_copy(cnt, ps[0:TT, 4, E:2 * E]))
            then(dve.tensor_scalar(ext, cnt, float(CAP), None, ALU.is_gt))
            for j in range(2, -(-T // CAP)):
                then(dve.scalar_tensor_tensor(out=ext, in0=cnt, scalar=float(CAP * j), in1=ext,
                                              op0=ALU.is_gt, op1=ALU.add))
            then(dve.tensor_tensor_scan(incl, ext, ext, 0.0, ALU.add, ALU.bypass))
            then(dve.tensor_tensor(excl, incl, ext, ALU.subtract))
            exps, nth = rt[:, 160:160 + N_OVER], rt[:, 176:176 + N_OVER]
            m8 = oh[:, 128:128 + 8 * E].rearrange("p (m e) -> p m e", e=E)
            sel8 = oht[:, 0:8 * E].rearrange("p (m e) -> p m e", e=E)

            def over_e(row):
                return row[:, None, :].to_broadcast([TT, 8, E])

            for h in range(2):
                r8 = slice(8 * h, 8 * h + 8)
                m_b = cc("iota", 0, TT)[:, r8, None].to_broadcast([TT, 8, E])
                then(dve.tensor_tensor(m8, over_e(incl), m_b, ALU.is_le))
                then(dve.tensor_reduce(exps[:, r8], m8, AX, ALU.add))
                then(dve.tensor_tensor(sel8, over_e(cc("iota", 0, TT)), exps[:, r8, None].to_broadcast([TT, 8, E]),
                                       ALU.is_equal))
                then(dve.tensor_tensor(m8, sel8, over_e(excl), ALU.mult))
                then(dve.tensor_reduce(nth[:, r8], m8, AX, ALU.add))
                then(dve.tensor_tensor(nth[:, r8], nth[:, r8], cc("iota", 0, TT)[:, r8], ALU.subtract))
                then(dve.tensor_scalar(nth[:, r8], nth[:, r8], float(CAP), -float(CAP), ALU.mult, ALU.add))
                for i in range(NT):
                    for t in (place_cols, gate_cols):
                        then(dve.tensor_tensor(m8, sel8, over_e(t[:, i, 0:E]), ALU.mult))
                        then(dve.tensor_reduce(t[:, i, E + 8 * h:E + 8 * h + 8], m8, AX, ALU.add))
                    then(dve.tensor_tensor(place_cols[:, i, E + 8 * h:E + 8 * h + 8], place_cols[:, i, E + 8 * h:E + 8 * h + 8],
                                           nth[:, r8], ALU.add))
            ov = rt[0:1, 192:193 + N_OVER]
            then(dve.tensor_copy(ov[:, 0:1], incl[0:1, E - 1:E]))
            then(dve.tensor_scalar(ov[:, 1:], exps[0:1, :], float(E - 1), None, ALU.min))
            then(dve.tensor_copy(ovi[:, :], ov), "ovd")

            def slots_of(q):
                dve.wait_ge(m_xg, q + 1)
                dve.tensor_copy(idxg, ps[:, 5, 0:2]).then_inc(m_idx, 1)

            def place_gates(q):
                dve.wait_ge(m_idx, q + 1)
                dve.tensor_scalar(gated, tokens, idxg[:, 0:1], idxg[:, 1:2], ALU.is_equal,
                                  ALU.mult).then_inc(m_gated, 1)

            def add(n_placed, banks):
                for i in range(NT):
                    dve.wait_ge(m_pl, 3 * n_placed + i + 1)
                    for n in range(2):
                        half = x_row[0:TT, i, 512 * n:512 * n + 512]
                        dve.tensor_tensor(half, half, ps[0:TT, banks[i][n], :], ALU.add).then_inc(m_add, 1)

            def item(q, ahead, placed):
                gu = ps[:, 1:3, :].rearrange("p n c -> p (n c)")
                if ahead:
                    dve.wait_ge(m_xg, q + 1)
                    choose(q + 1)
                dve.wait_ge(m_gu, q + 1)
                dve.tensor_scalar(g_sb, gu[:, 0::2], LIMIT, None, ALU.min).then_inc(m_g, 1)
                dve.tensor_scalar(up_sb, gu[:, 1::2], LIMIT, -LIMIT, ALU.min, ALU.max).then_inc(s_dve, 1)
                dve.wait_ge(m_g, q + 1)
                dve.wait_ge(s_dve, 2 * q + (base + 1))
                dve.scalar_tensor_tensor(out=up_sb, in0=up_sb, scalar=1.0, in1=g_sb,
                                         op0=ALU.add, op1=ALU.mult).then_inc(s_dve, 1)
                dve.wait_ge(s_dve, 2 * q + (base + 2))
                dve.wait_ge(m_sig, q + 1)
                dve.tensor_tensor(act_sb, up_sb, sig_sb, ALU.mult).then_inc(m_act, 1)
                if placed is not None:
                    add(q + placed, beside_ahead if ahead else beside_last)
                place_gates(q)
                dve.wait_ge(m_used, SLOTS * q + SLOTS)
                dve.tensor_copy(y_sb, ps[:, 4, :]).then_inc(m_ysb, 1)
                dve.wait_ge(m_gated, q + 1)
                if ahead:
                    slots_of(q + 1)
                if placed is not None:
                    dve.wait_ge(m_add, 6 * q + (6 * placed + 6))

            slots_of(0)
            dve.wait_ge(s_tok, 32)
            base = up(s_dve, 0)
            item(0, True, None)
            with dve.Fori(1, E_BIAS) as q:
                item(q, True, -1)
            add(E_BIAS - 1, beside_ahead)
            dve.wait_ge(m_add, 6 * E_BIAS)
            with dve.Fori(E_BIAS, E - 1) as q:
                item(q, True, 0)
            item(E - 1, False, 0)
            n_over = dve.value_load(ovi[0:1, 0:1], min_val=0, max_val=N_OVER)
            with dve.If(n_over > 0):
                with dve.Fori(0, n_over) as m:
                    dve.wait_ge(m_xg, m + E)
                    choose(m + E)
                    slots_of(m + E)
                    item(m + E, False, 0)
            add(n_over + E, beside_last)

        @block.tensor
        def _(pe):
            def transpose(out, in_, k):
                return pe.transpose(out, in_, ident[0:k, 0:k])

            pe.wait_ge(s_con, 16)
            pe.wait_ge(S["hrow"], NT)
            for kt in range(KT):
                if kt >= 4:
                    pe.wait_ge(S["ht_cp"] if kt % 2 else S["ht_cp2"], (kt - 4) // 2 + 1)
                for i in range(NT):
                    mm = transpose(ps[:, kt % 4, TT * i:TT * i + TT], h_row[:, i, P * kt:P * kt + P], TT)
                mm.then_inc(S["ht_tr"], 1)
            pe.wait_ge(S["ht_cp"], 4)
            pe.wait_ge(S["ht_cp2"], 4)

            def project(n):
                if n % 2 == 0:
                    pe.wait_ge(s_win[n // 2], 16)
                if 2 <= n <= 10:
                    pe.wait_ge(S["proj_cp"], n - 1)
                elif n == 11:
                    pe.wait_ge(S["y_cp"], 1)
                elif n == 12:
                    pe.wait_ge(S["masked"], 2)
                for kt in range(KT):
                    mm = pe.matmul(ps[:, PBANK[n], 0:T], w_in[:, kt, P * n:P * n + P], hT[:, kt, :],
                                   start=(kt == 0), stop=(kt == KT - 1))
                mm.then_inc(S["proj"], 1)

            project(0)
            project(1)
            pe.wait_ge(s_vrow, 16 * 14)
            for c in range(NC):
                transpose(ps[:, 6, c * N_VROWS:(c + 1) * N_VROWS], v1[:, P * c:P * c + P], N_VROWS)
            transpose(ps[:, 6, 200:202], v2, 2).then_inc(S["vec_tr"], 1)
            for n in range(2, 6):
                project(n)
            pe.wait_ge(S["vec_cp"], 1)
            pe.wait_ge(S["sqqk"], 1)
            for c in range(5):
                mm = pe.matmul(ps[:, 3 + c, 0:T], cc("blk64"), sqq[:, c, :], start=True, stop=True)
            mm.then_inc(S["msqk"], 1)
            pe.wait_ge(s_kc, 16)
            for half in range(2):
                if half:
                    pe.wait_ge(S["kc_cp"], 1)
                for b in range(4):
                    mm = transpose(ps[:, 2, P * b:P * b + P], kc[:, 4 * half + b, :], P)
                mm.then_inc(S["kc_tr"], 1)
                project(6 + half)
            pe.wait_ge(S["kc_cp"], 2)
            for n in range(2):
                transpose(ps[:, 2, P * n:P * n + P], vT[:, P * n:P * n + P], P)
            transpose(ps[0:NS, 2, 256:384], vT[:, NP_:T], P).then_inc(S["v_tr"], 1)
            project(8)
            project(9)
            pe.wait_ge(S["ivqk"], 1)
            pe.wait_ge(S["qn"], 1)
            for c in range(5):
                mm = pe.matmul(ps[:, 3 + c, 0:T], cc("rot"), qk[:, c, :], start=True, stop=True)
            mm.then_inc(S["rotd"], 1)
            project(10)
            pe.wait_ge(S["roped"], 1)
            pe.wait_ge(S["v_cp"], 1)
            for n, w in ((1, 256), (0, 128)):
                for c in range(4):
                    for g in range(2):
                        h = 4 * g + c
                        out = ps[:, 2 + h // 2, 256 * (h % 2):256 * (h % 2) + 256] if n else ps[:, 6 + g, P * c:P * c + P]
                        mm = pe.matmul(out, qk[64 * g:64 * g + 64, c, P * n:P * n + P],
                                       qk[64 * g:64 * g + 64, 4, 0:w], start=True, stop=True)
                mm.then_inc(S["scores"], 1)
            pe.wait_ge(S["qbd_r"], 2)
            pe.wait_ge(S["proj_cp"], 10)
            pe.matmul(ps[0:64, 1, 64:64 + NS], qbd[:, :, :].rearrange("p b h -> p (b h)"), qk[:, 4, NP_:T],
                      start=True, stop=True)
            for b in range(NS):
                pe.matmul(ps[:, 1, 8 * b:8 * b + 8], kcT[:, b, :], qbd[:, b, :], start=True, stop=True)
            transpose(ps[:, 1, 256:384], qk[:, 4, P:NP_], P)
            transpose(ps[0:NS, 1, 384:512], qk[:, 4, NP_:T], P).then_inc(S["sc_t"], 1)

            def gate(n):
                if n >= 4:
                    pe.wait_ge(S["gate_s"], n - 3)
                pe.matmul(ps[:, 2 + n % 4, 0:T], bd[:, n % 2, n // 2, :], xc[:, n // 2, :],
                          start=True, stop=True).then_inc(S["gate"], 1)

            pe.wait_ge(s_bd, 64)
            pe.wait_ge(S["conv"], 2 * NC)
            pe.wait_ge(S["masked"], 1)
            for n in range(4):
                gate(n)
            for n in range(4, 2 * NC):
                gate(n)
            pe.wait_ge(S["sc_cp"], 1)
            transpose(ps[0:64, 1, 128:256], s_nT[:, :], P).then_inc(S["sc_tr"], 1)
            for n in range(11, 14):
                project(n)
            groups = [(0, 0, 0), (0, 0, 1), (1, 0, 0), (1, 0, 1), (1, 1, 0), (1, 1, 1)]
            pe.wait_ge(S["gate_s"], 2 * NC)
            for j, (n, kb, g) in enumerate(groups):
                pe.wait_ge(S["pn"], n + 1)
                if j == 4:
                    pe.wait_ge(S["y_cp"], 4)
                for c in range(4):
                    src = p1_sb if n else p0_sb
                    mm = transpose(ps[:, 2 + j, P * c:P * c + P], src[:, 4 * g + c, P * kb:P * kb + P], P)
                mm.then_inc(S["p_tr"], 1)
                if j == 1:
                    pe.wait_ge(S["s_pn"], 1)
                    transpose(ps[:, 0, 0:64], s_sb[:, 0:128], 64)
                    transpose(ps[0:NS, 0, 128:192], s_dg[:, :], 64).then_inc(S["s_ptr"], 1)

            def attend(n):
                for kb in range(n + 1):
                    for g in range(2):
                        j = groups.index((n, kb, g))
                        mm = pe.matmul(ps[64 * g:64 * g + 64, n, :], kv_new[:, kb, 64 * g:64 * g + 64],
                                       pT[:, j, :], start=(kb == 0), stop=(kb == n))
                mm.then_inc(S["pv"], 1)

            pe.wait_ge(S["p_cp"], 1)
            pe.wait_ge(S["p_cp2"], 1)
            pe.wait_ge(S["s_pcp"], 1)
            attend(0)
            pe.wait_ge(s_vc, 16)
            pe.matmul(ps[:, 3, 0:64], kv_new[0:NS, 2, :], s_dT, start=True, stop=True)
            for b in range(NS):
                r = slice(8 * b, 8 * b + 8)
                mm = pe.matmul(ps[:, 2, r], vc[:, b, :], s_pT[:, r], start=True, stop=True)
            mm.then_inc(S["s_pv"], 1)
            pe.wait_ge(S["p_cp"], 3)
            pe.wait_ge(S["p_cp2"], 3)
            pe.wait_ge(S["krow_cp"], 1)
            attend(1)

            def mean_square(j, src):
                pe.wait_ge(S["sqg"], j)
                for c in range(NC):
                    mm = pe.matmul(ps[:, 6, 0:T], cc("mean512"), src[:, c, :], start=(c == 0), stop=(c == NC - 1))
                mm.then_inc(S["msg"], 1)

            def out_half(i, n, half):
                for c in range(NC):
                    src = (yT if half else oT)[:, c, :]
                    mm = pe.matmul(ps[0:TT, 2 * i + n, :], src[:, TT * i:TT * i + TT],
                                   w_out[:, NC * half + c, 512 * n:512 * n + 512],
                                   start=(half == 0 and c == 0), stop=(half == 1 and c == NC - 1))
                return mm

            def states(j, rows, src):
                for c in range(NC):
                    mm = transpose(ps[0:rows, 7, P * c:P * c + P], src(c), P)
                mm.then_inc(S["st_tr"], 1)

            mean_square(1, sq)
            states(0, 3, lambda c: xe[:, c, NP_:NP_ + 3])
            pe.wait_ge(s_wout, 48)
            pe.wait_ge(S["mixed"], 1)
            for i in range(NT):
                for n in range(2):
                    out_half(i, n, 0)
                if i == 1:
                    mean_square(2, tq)
                    pe.wait_ge(S["st_cp"], 1)
                    states(1, NS, lambda c: xs[:, c, :])
            pe.wait_ge(S["h_last"], 1)
            pe.wait_ge(S["st_cp"], 2)
            states(2, 9, lambda c: hs[:, c, NP_ - 1:T])
            pe.wait_ge(S["mixed"], 2)

            def out_tile(i):
                for n in range(2):
                    out_half(i, n, 1).then_inc(S["outp"], 1)

            def logits(i):
                pe.wait_ge(S["xn"], i + 1)
                for half, copied in enumerate((S["xnt_cp"], S["xnt_cp2"])):
                    if i:
                        pe.wait_ge(copied, i)
                    for j in range(4):
                        kt = 4 * half + j
                        mm = transpose(ps[:, 6 + half, TT * j:TT * j + TT], xn_row[:, i, P * kt:P * kt + P], TT)
                    mm.then_inc(S["xnt_tr"], 1)
                for half, copied in enumerate((S["xnt_cp"], S["xnt_cp2"])):
                    pe.wait_ge(copied, i + 1)
                    for kt in range(4 * half, 4 * half + 4):
                        mm = pe.matmul(ps[0:TT, 2 * i, 0:E], hT[:, kt, TT * i:TT * i + TT], wr[:, kt, :],
                                       start=(kt == 0), stop=(kt == KT - 1))
                mm.then_inc(S["logit"], 1)

            msk = oht[:, 0:96].rearrange("p (i e) -> p i e", i=NT)

            def count_before(i):
                pe.wait_ge(S["mask"], i + 1)
                for j in range(i + 1):
                    mm = pe.matmul(ps[0:TT, 2 * i + 1, 0:E], cc("tri" if i == j else "ones", 0, TT), msk[:, j, :],
                                   start=(j == 0), stop=(j == i))
                mm.then_inc(S["posd"], 1)

            out_tile(0)
            out_tile(1)
            pe.wait_ge(s_misc, 16 * 11)
            pe.wait_ge(S["st_cp"], 3)
            logits(0)
            out_tile(2)
            logits(1)
            count_before(0)
            logits(2)
            count_before(1)
            count_before(2)
            for j in range(NT):
                mm = pe.matmul(ps[0:TT, 4, E:2 * E], cc("ones", 0, TT), msk[:, j, :], start=(j == 0), stop=(j == NT - 1))
            mm.then_inc(S["posd"], 1)

            def gather(q):
                pe.wait_ge(m_oh, 4 * q + 4)
                pe.sem_inc(m_passed, 1)
                for i in range(NT):
                    for n in range(2):
                        pe.matmul(ps[64 * n:64 * n + 64, 6, :], oneh[:, i, 0:CAP], xn_row[:, i, 512 * n:512 * n + 512],
                                  start=(i == 0), stop=(i == NT - 1))
                for i in range(NT):
                    mm = pe.matmul(ps[:, 5, 0:2], oneh[:, i, :], tokg[:, i, :], start=(i == 0), stop=(i == NT - 1))
                mm.then_inc(m_xg, 1)

            def x_transposes(q):
                pe.wait_ge(m_xgs, q + 1)
                pe.sem_inc(m_passed, 1)
                for j in range(4):
                    mm = transpose(ps[:, 0, P * j:P * j + P], xg_sb[:, P * j:P * j + P], P)
                mm.then_inc(m_xtr, 1)

            sel = cc("sel").rearrange("p (j m) -> p j m", j=4)

            def place(q, banks, free=None):
                pe.wait_ge(m_ysb, q + 1)
                pe.wait_ge(m_gated, q + 1)
                pe.sem_inc(m_passed, 1)
                for i in range(NT):
                    if i == NT - 1 and free:
                        free()
                    for n in range(2):
                        mm = pe.matmul(ps[0:TT, banks[i][n], :], gated[64 * n:64 * n + 64, TT * i:TT * i + TT],
                                       y_sb[64 * n:64 * n + 64, :], start=True, stop=True)
                    mm.then_inc(m_pl, 1)

            def place_biases(banks):
                pe.wait_ge(s_tok, 32)
                pe.wait_ge(S["gt_cp"], 1)
                pe.wait_ge(m_xT, E_BIAS + 1)
                for i in range(NT):
                    for n in range(2):
                        mm = pe.matmul(ps[0:TT, banks[i][n], :], gateT[:, TT * i:TT * i + TT],
                                       bias_dn[:, 512 * n:512 * n + 512], start=True, stop=True)
                    mm.then_inc(m_pl, 1)

            def item(q, ahead, placed):
                pe.wait_ge(m_xT, q + 1)
                for kt in range(KT):
                    pe.wait_ge(s_slot[kt], 16 * q + 16)
                    for n in range(2):
                        for h in range(2):
                            mm = pe.matmul(ps[64 * h:64 * h + 64, 1 + n, :],
                                           xT[:, kt % 4, 64 * (kt // 4):64 * (kt // 4) + 64],
                                           ring[:, kt, 1024 * h + 512 * n:1024 * h + 512 * n + 512],
                                           start=(kt == 0), stop=False)
                    mm.then_inc(m_used, 1)
                pe.wait_ge(m_bgu, 16 * q + 16)
                for n in range(2):
                    for h in range(2):
                        mm = pe.matmul(ps[64 * h:64 * h + 64, 1 + n, :], sel[:, 2 * h + n, :], b_gu,
                                       start=False, stop=True)
                mm.then_inc(m_gu, 1)
                if ahead:
                    pe.wait_ge(m_idx, q + 1)
                    gather(q + 1)
                else:
                    pe.wait_ge(m_idx, q + 1)
                    place(q - 1, beside_last, lambda: pe.wait_ge(m_act, q + 1))
                pe.wait_ge(m_act, q + 1)
                for j in range(4):
                    mm = transpose(ps[:, 3, P * j:P * j + P], act_sb[:, P * j:P * j + P], P)
                mm.then_inc(m_atr, 1)

                def transposes_copied():
                    pe.wait_ge(m_aT, q + 1)
                    pe.wait_ge(m_xT, q + 2)

                if ahead:
                    x_transposes(q + 1)
                    if placed is not None:
                        place(q - 1, beside_ahead, transposes_copied)
                pe.wait_ge(m_aT, q + 1)
                for s in range(4):
                    pe.wait_ge(s_slot[KT + s], 16 * q + 16)
                    for t in range(2):
                        h, j = divmod(2 * s + t, 4)
                        for n in range(2):
                            mm = pe.matmul(ps[64 * n:64 * n + 64, 4, :], actT[:, j, 64 * h:64 * h + 64],
                                           ring[:, KT + s, 1024 * t + 512 * n:1024 * t + 512 * n + 512],
                                           start=(s == 0 and t == 0), stop=(s == 3 and t == 1))
                    mm.then_inc(m_used, 1)
                if placed is not None:
                    pe.wait_ge(m_add, 6 * q + (6 * placed + 6))

            gather(0)
            for i in range(NT):
                mm = transpose(ps[0:E, 7, TT * i:TT * i + TT], gate_cols[:, i, 0:E], TT)
            mm.then_inc(S["gt_tr"], 1)
            x_transposes(0)
            item(0, True, None)
            with pe.Fori(1, E_BIAS) as q:
                item(q, True, -1)
            place_biases(beside_ahead)
            pe.wait_ge(m_add, 6 * E_BIAS)
            with pe.Fori(E_BIAS, E - 1) as q:
                item(q, True, 0)
            item(E - 1, False, 0)
            pe.wait_ge(S["ovd"], 1)
            n_over = pe.value_load(ovi[0:1, 0:1], min_val=0, max_val=N_OVER)
            with pe.If(n_over > 0):
                with pe.Fori(0, n_over) as m:
                    pe.wait_ge(m_idx, m + E)
                    gather(m + E)
                    x_transposes(m + E)
                    item(m + E, False, 0)
            place(n_over + (E - 1), beside_last)


def constants(np):
    c = {n: np.zeros((P, w), np.float32) for n, w in CONST_SIZES}
    i = np.arange(P)
    c["ident"][i, i] = 1
    c["blk64"][:] = (i[:, None] // HD == i[None, :] // HD) / np.float32(HD)
    c["mean512"][:] = 1.0 / DG
    for g in (0, HD):
        for d in range(8):
            c["rot"][g + d + 8, g + d] = -1
            c["rot"][g + d, g + d + 8] = 1
    pos = np.concatenate([np.arange(NP_), np.full(NS, 1024)]).astype(np.float32)
    inv_f = np.float32(500000.0) ** (-np.arange(0, 16, 2, dtype=np.float32) / np.float32(16))
    ang = (pos[:, None] * inv_f[None, :]).astype(np.float32)
    c["cos"][:] = 1
    for g in (0, HD):
        for b in (0, 8):
            c["cos"][g + b:g + b + 8] = np.cos(ang).T
            c["sin"][g + b:g + b + 8] = np.sin(ang).T
    c["mask"][:, 0:P] = np.where(i[None, :] >= i[:, None], 0, -1e30)
    c["mask"][:, P:] = np.where(i[None, :] <= i[:, None], 0, -1e30)
    c["iota"][:] = np.arange(E)
    c["tri"][:] = i[:, None] < np.arange(TT)[None, :]
    c["ones"][:] = 1
    c["diag"][:] = (i[:, None] // 8) == np.arange(NS)[None, :]
    for j in range(4):
        c["sel"][j, 64 * j:64 * j + 64] = 1
    con = np.concatenate([c[n] for n, _ in CONST_SIZES], axis=1)
    c["slot"][:] = POS0 + np.arange(P)[None, :] % CAP
    c["tok"][0:TT] = np.arange(NT)[None, :] * TT + np.arange(TT)[:, None]
    con = np.concatenate([c[n] for n, _ in CONST_SIZES], axis=1)
    tokens = np.zeros((P, T), np.float32) + np.arange(T, dtype=np.float32)
    return {"const": con, "tokens": tokens}


_INS = ["x_prompt", "x_sample", "cache_k", "cache_v", "state_conv", "state_h", "g_mix_norm", "w_in", "g_q_norm",
        "g_k_norm", "attn_sinks", "conv_w", "conv_b", "w_lru_a", "b_lru_a", "w_lru_x", "b_lru_x", "lru_lambda",
        "g_attn_out", "g_rnn_out", "w_out", "g_ffn_norm", "w_router", "b_router", "w_gate_up", "b_gate_up",
        "w_down", "b_down"]
_OUTS = [("y_prompt", (1, 256, 1024)), ("y_sample", (8, 1, 1024)),
         ("new_k_prompt", (1, 1, 128, 2, 64)), ("new_v_prompt", (1, 1, 128, 2, 64)),
         ("new_conv_prompt", (1, 1, 3, 512)), ("new_h_prompt", (1, 1, 512)),
         ("new_k_sample", (1, 8, 128, 2, 64)), ("new_v_sample", (1, 8, 128, 2, 64)),
         ("new_conv_sample", (1, 8, 3, 512)), ("new_h_sample", (1, 8, 512))]


def kernel(**inputs):
    import numpy as _np
    import concourse.bacc as _bacc
    from concourse import mybir as _mybir
    from concourse.bass_utils import run_bass_kernel_spmd as _run

    nc = _bacc.Bacc("TRN2", target_bir_lowering=False, num_devices=1)
    arrays, a, o = {}, {}, {}
    given = {n: _np.ascontiguousarray(inputs[n]) for n in _INS}
    given.update(constants(_np))
    for name, v in given.items():
        arrays[f"in_{name}_dram"] = v
        a[name] = nc.dram_tensor(f"in_{name}_dram", v.shape, _mybir.dt.from_np(v.dtype), kind="ExternalInput").ap()
    for name, shape in _OUTS:
        o[name] = nc.dram_tensor(f"out_{name}_dram", shape, _mybir.dt.float32, kind="ExternalOutput").ap()
    hybrid_layer(nc, a, o)
    r = _run(nc, [arrays], core_ids=[0])
    return tuple(r.results[0][f"out_{name}_dram"] for name, _ in _OUTS)
```
